# Optimizing a Trainium2 kernel written in Bass

```python
import jax, jax.numpy as jnp
from jax import lax
import numpy as np

D_MODEL = 1024
BATCH = 1
SEQ = 2048
DEPTH = 2
DEC_BATCH = 8
DEC_SEQ = 1
PAST_LEN = 2048
PAGE_SIZE = 128

N_A = DEPTH // 2
N_B = DEPTH - N_A
CONV_W = 3
HEAD_DIM = 128
N_GROUPS = 3
WINDOWS = (128, 512, 2048)
DILATIONS = (1, 4, 16)
HEADS = 8
KV_HEADS = 2
Q_PER_KV = HEADS // KV_HEADS
ATTN_WIDTH = HEADS * HEAD_DIM
Q_WIDTH = N_GROUPS * HEADS * HEAD_DIM
KV_WIDTH = 2 * N_GROUPS * KV_HEADS * HEAD_DIM
ROPE_THETA = 10000.0
EPS = 1e-6
SCALE = HEAD_DIM ** -0.5

kernel_name = "yoco_shortconv_dilated_window_decoder"

def rms_norm(x, g):
    x32 = x.astype(jnp.float32)
    y = x32 * lax.rsqrt(jnp.mean(x32 * x32, axis=-1, keepdims=True) + EPS)
    return (y * g.astype(jnp.float32)).astype(x.dtype)

def rope(x, pos):
    half = HEAD_DIM // 2
    inv_freq = ROPE_THETA ** (-jnp.arange(half, dtype=jnp.float32) * 2.0 / HEAD_DIM)
    ang = pos.astype(jnp.float32)[:, None] * inv_freq[None, :]
    cos = jnp.cos(ang)[:, None, :]
    sin = jnp.sin(ang)[:, None, :]
    x32 = x.astype(jnp.float32)
    x1, x2 = x32[..., :half], x32[..., half:]
    return jnp.concatenate([x1 * cos - x2 * sin, x2 * cos + x1 * sin], axis=-1).astype(x.dtype)

def causal_short_conv(up, w, T):
    return sum(up[:, k:k + T] * w[k] for k in range(CONV_W))

def conv_layer(x, past, g_pre, w_in, w_conv, w_out, g_post):
    T = x.shape[1]
    h = rms_norm(x, g_pre)
    b_gate, c_gate, u_in, z = jnp.split(h @ w_in, 4, axis=-1)
    u = c_gate * u_in
    up = jnp.concatenate([past.astype(u.dtype), u], axis=1)
    y = b_gate * causal_short_conv(up, w_conv, T)
    out = (y * jax.nn.silu(z)) @ w_out
    return x + rms_norm(out, g_post), up[:, -(CONV_W - 1):]

def shared_kv(x, g, w_kv, pos):
    Bx, T = x.shape[:2]
    kv = (rms_norm(x, g) @ w_kv).reshape(Bx, T, 2, N_GROUPS * KV_HEADS, HEAD_DIM)
    k = rope(kv[:, :, 0], pos).reshape(Bx, T, N_GROUPS, KV_HEADS, HEAD_DIM)
    v = kv[:, :, 1].reshape(Bx, T, N_GROUPS, KV_HEADS, HEAD_DIM)
    return k, v

def b_queries(h, w_in, pos):
    Bx, T = h.shape[:2]
    proj = h @ w_in
    q = rope(proj[..., :Q_WIDTH].reshape(Bx, T, N_GROUPS * HEADS, HEAD_DIM), pos)
    return q.reshape(Bx, T, N_GROUPS, HEADS, HEAD_DIM), proj[..., Q_WIDTH:]

def band_attn_prompt(q, k, v, window, dilation):
    Bx, S = q.shape[:2]
    n = S // dilation
    w = window // dilation
    blk = w
    n_pad = -(-n // blk) * blk
    nb = n_pad // blk

    def strided(a):
        a = a.reshape(Bx, n, dilation, a.shape[2], HEAD_DIM).transpose(0, 2, 1, 3, 4)
        return jnp.pad(a, ((0, 0), (0, 0), (0, n_pad - n), (0, 0), (0, 0)))

    def band(a):
        a = jnp.pad(a, ((0, 0), (0, 0), (blk, 0), (0, 0), (0, 0)))
        a = a.reshape(Bx, dilation, nb + 1, blk, KV_HEADS, HEAD_DIM)
        return jnp.concatenate([a[:, :, :-1], a[:, :, 1:]], axis=3)

    qs = strided(q).reshape(Bx, dilation, nb, blk, KV_HEADS, Q_PER_KV, HEAD_DIM).astype(jnp.float32)
    ks = band(strided(k)).astype(jnp.float32)
    vs = band(strided(v)).astype(jnp.float32)
    s = jnp.einsum('brnqkgd,brnjkd->brnkgqj', qs, ks) * SCALE
    i_idx = jnp.arange(nb)[:, None, None] * blk + jnp.arange(blk)[None, :, None]
    j_idx = jnp.arange(nb)[:, None, None] * blk - blk + jnp.arange(2 * blk)[None, None, :]
    dist = i_idx - j_idx
    mask = (j_idx >= 0) & (dist >= 0) & (dist <= w)
    s = jnp.where(mask[:, None, None], s, -jnp.inf)
    lse = jax.nn.logsumexp(s, axis=-1)
    p = jnp.exp(s - lse[..., None])
    o = jnp.einsum('brnkgqj,brnjkd->brnqkgd', p, vs)
    o = o.reshape(Bx, dilation, n_pad, HEADS, HEAD_DIM)[:, :, :n]
    o = o.transpose(0, 2, 1, 3, 4).reshape(Bx, S, HEADS, HEAD_DIM)
    lse = lse.transpose(0, 1, 2, 5, 3, 4).reshape(Bx, dilation, n_pad, HEADS)[:, :, :n]
    lse = lse.transpose(0, 2, 1, 3).reshape(Bx, S, HEADS)
    return o, lse

def window_attn_sample(q, kc, vc, n_past, window, dilation):
    Bd, T = q.shape[:2]
    nk = window // dilation + 1
    idx = (n_past + jnp.arange(T))[:, None] - dilation * jnp.arange(nk)[None, :]
    valid = idx >= 0
    idx = jnp.maximum(idx, 0)
    kg = kc[:, idx].astype(jnp.float32)
    vg = vc[:, idx].astype(jnp.float32)
    qg = q.reshape(Bd, T, KV_HEADS, Q_PER_KV, HEAD_DIM).astype(jnp.float32)
    s = jnp.einsum('btkgd,btnkd->btkgn', qg, kg) * SCALE
    s = jnp.where(valid[None, :, None, None, :], s, -jnp.inf)
    lse = jax.nn.logsumexp(s, axis=-1)
    p = jnp.exp(s - lse[..., None])
    o = jnp.einsum('btkgn,btnkd->btkgd', p, vg).reshape(Bd, T, HEADS, HEAD_DIM)
    return o, lse.reshape(Bd, T, HEADS)

def merge_groups(res, z, w_out):
    outs = jnp.stack([r[0] for r in res], axis=0)
    lses = jnp.stack([r[1] for r in res], axis=0)
    alpha = jax.nn.softmax(lses, axis=0)
    o = jnp.sum(alpha[..., None] * outs, axis=0)
    Bx, T = z.shape[:2]
    o = o.reshape(Bx, T, ATTN_WIDTH).astype(z.dtype)
    return (o * jax.nn.silu(z)) @ w_out

def setup_inputs(seed: int = 0) -> dict:
    key = jax.random.key(seed)
    ks = jax.random.split(key, 20)
    D = D_MODEL

    def nrm(k, shape, scale=1.0):
        return jax.random.normal(k, shape, jnp.float32) * scale

    return {
        "x_prompt": nrm(ks[0], (BATCH, SEQ, D)),
        "x_sample": nrm(ks[1], (DEC_BATCH, DEC_SEQ, D)),
        "state_conv": nrm(ks[2], (N_A, DEC_BATCH, CONV_W - 1, D)),
        "cache_kv_g0": nrm(ks[3], (DEC_BATCH, min(WINDOWS[0], PAST_LEN), 2, KV_HEADS, HEAD_DIM)),
        "cache_kv_g1": nrm(ks[4], (DEC_BATCH, min(WINDOWS[1], PAST_LEN), 2, KV_HEADS, HEAD_DIM)),
        "cache_kv_g2": nrm(ks[5], (DEC_BATCH, min(WINDOWS[2], PAST_LEN), 2, KV_HEADS, HEAD_DIM)),
        "a_norm_pre": 1.0 + nrm(ks[6], (N_A, D), 0.05),
        "a_w_in": nrm(ks[7], (N_A, D, 4 * D), D ** -0.5),
        "a_conv": nrm(ks[8], (N_A, CONV_W, D), CONV_W ** -0.5),
        "a_w_out": nrm(ks[9], (N_A, D, D), D ** -0.5),
        "a_norm_post": 1.0 + nrm(ks[10], (N_A, D), 0.05),
        "kv_norm": 1.0 + nrm(ks[11], (D,), 0.05),
        "w_kv": nrm(ks[12], (D, KV_WIDTH), D ** -0.5),
        "b_norm_pre": 1.0 + nrm(ks[13], (N_B, D), 0.05),
        "b_w_in": nrm(ks[14], (N_B, D, Q_WIDTH + ATTN_WIDTH), D ** -0.5),
        "b_w_out": nrm(ks[15], (N_B, ATTN_WIDTH, D), ATTN_WIDTH ** -0.5),
        "b_norm_post": 1.0 + nrm(ks[16], (N_B, D), 0.05),
    }

def reference(x_prompt, x_sample, state_conv, cache_kv_g0, cache_kv_g1, cache_kv_g2,
              a_norm_pre, a_w_in, a_conv, a_w_out, a_norm_post,
              kv_norm, w_kv, b_norm_pre, b_w_in, b_w_out, b_norm_post):
    seq = x_prompt.shape[1]
    dec_seq = x_sample.shape[1]
    pos_p = jnp.arange(seq)
    pos_s = PAST_LEN + jnp.arange(dec_seq)
    caches = (cache_kv_g0, cache_kv_g1, cache_kv_g2)
    hp, hs = x_prompt, x_sample
    conv_p, conv_s = [], []
    for layer in range(DEPTH):
        if layer < N_A:
            zero_past = jnp.zeros((hp.shape[0], CONV_W - 1, D_MODEL), hp.dtype)
            hp, st_p = conv_layer(hp, zero_past, a_norm_pre[layer], a_w_in[layer],
                                  a_conv[layer], a_w_out[layer], a_norm_post[layer])
            hs, st_s = conv_layer(hs, state_conv[layer], a_norm_pre[layer], a_w_in[layer],
                                  a_conv[layer], a_w_out[layer], a_norm_post[layer])
            conv_p.append(st_p)
            conv_s.append(st_s)
            continue
        if layer == N_A:
            k_p, v_p = shared_kv(hp, kv_norm, w_kv, pos_p)
            k_s, v_s = shared_kv(hs, kv_norm, w_kv, pos_s)
            kc_s = [jnp.concatenate([caches[g][:, :, 0], k_s[:, :, g]], axis=1) for g in range(N_GROUPS)]
            vc_s = [jnp.concatenate([caches[g][:, :, 1], v_s[:, :, g]], axis=1) for g in range(N_GROUPS)]
            kv_new_p = [jnp.stack([k_p[:, :, g], v_p[:, :, g]], axis=2)[:, -min(WINDOWS[g], seq):]
                        for g in range(N_GROUPS)]
            kv_new_s = [jnp.stack([kc_s[g], vc_s[g]], axis=2)[:, -min(WINDOWS[g], caches[g].shape[1] + dec_seq):]
                        for g in range(N_GROUPS)]
        j = layer - N_A
        q, z = b_queries(rms_norm(hp, b_norm_pre[j]), b_w_in[j], pos_p)
        res = [band_attn_prompt(q[:, :, g], k_p[:, :, g], v_p[:, :, g], WINDOWS[g], DILATIONS[g])
               for g in range(N_GROUPS)]
        hp = hp + rms_norm(merge_groups(res, z, b_w_out[j]), b_norm_post[j])
        q, z = b_queries(rms_norm(hs, b_norm_pre[j]), b_w_in[j], pos_s)
        res = [window_attn_sample(q[:, :, g], kc_s[g], vc_s[g], caches[g].shape[1], WINDOWS[g], DILATIONS[g])
               for g in range(N_GROUPS)]
        hs = hs + rms_norm(merge_groups(res, z, b_w_out[j]), b_norm_post[j])
    return (hp, hs, jnp.stack(conv_p, axis=0), kv_new_p[0], kv_new_p[1], kv_new_p[2],
            jnp.stack(conv_s, axis=0), kv_new_s[0], kv_new_s[1], kv_new_s[2])


_drawn_inputs = setup_inputs


def setup_inputs(seed=0):
    import zlib

    import numpy as np

    out = dict(_drawn_inputs(seed))
    spreads = {}
    factors = {}
    for name, (base, spread) in spreads.items():
        noise = np.random.default_rng([zlib.crc32(name.encode()), seed]).standard_normal(out[name].shape)
        drawn = base * np.exp(spread * noise) if base else spread * noise
        out[name] = __import__('jax').numpy.asarray(drawn.astype(out[name].dtype))
    for name, factor in factors.items():
        out[name] = (out[name] * factor).astype(out[name].dtype)
    return out
```

```python
from contextlib import ExitStack

import numpy as np

import concourse.bass as bass
from concourse import mybir

F32 = mybir.dt.float32
F32R = mybir.dt.float32r
BF16 = mybir.dt.bfloat16
ALU = mybir.AluOpType
ACT = mybir.ActivationFunctionType
AX_X = mybir.AxisListType.X

P = 128
D = 1024
KT = D // P
SEQ = 2048
NS = 8
TOK = SEQ + NS
NT = SEQ // P
BANK = 512
EPS = 1e-6


def row_tile(t):
    return P if t < NT else NS


def reciprocal_root(dve, done, before, square_sum, root, scratch, out):
    mean, r, e = scratch[:, 0:1], scratch[:, 1:2], scratch[:, 2:3]
    nc = dve.bass
    nc.vector.tensor_scalar(mean, square_sum, 1.0 / D, EPS, ALU.mult, ALU.add).then_inc(done, 1)
    nc.vector.reciprocal(r, root).then_inc(done, 1)
    dve.wait_ge(done, before + 2)
    nc.vector.tensor_tensor(e, r, r, ALU.mult).then_inc(done, 1)
    dve.wait_ge(done, before + 3)
    nc.vector.tensor_tensor(e, e, mean, ALU.mult).then_inc(done, 1)
    dve.wait_ge(done, before + 4)
    nc.vector.tensor_scalar(e, e, -0.5, 1.5, ALU.mult, ALU.add).then_inc(done, 1)
    dve.wait_ge(done, before + 5)
    nc.vector.tensor_tensor(out, r, e, ALU.mult).then_inc(done, 1)


def conv_projection_phase(nc, x_prompt, x_sample, state_conv, norm_pre, w_in, w_conv,
                          y_t, state_out_prompt, state_out_sample, caches, caches_out):
    CHUNK = 412
    NCH = -(-TOK // CHUNK)
    size = [min(CHUNK, TOK - c * CHUNK) for c in range(NCH)]
    LAST = size[-1] - NS
    NF = D // P
    GATES = (1, 2, 0, 3)
    JOBS = 2 * NCH

    with ExitStack() as ctx:
        def sb(name, shape, dt=F32):
            return ctx.enter_context(nc.sbuf_tensor(name, shape, dt))

        def sem(name):
            return nc.alloc_semaphore(name)

        ht_hi = sb("a_ht_hi", [P, KT, TOK], F32R)
        ht_lo = sb("a_ht_lo", [P, KT, TOK], F32R)
        w_raw = [sb(f"a_w_raw{b}", [P, KT, P]) for b in range(2)]
        w_hi = [sb(f"a_w_hi{k}", [P, KT, P], F32R) for k in range(4)]
        w_lo = [sb(f"a_w_lo{k}", [P, KT, P], F32R) for k in range(4)]
        u_buf = [sb(f"a_u{b}", [P, 2 + CHUNK]) for b in range(2)]
        conv = sb("a_conved", [P, TOK])
        c_sb = [sb(f"a_c{b}", [P, CHUNK]) for b in range(2)]
        silu_z = [sb(f"a_silu_z{b}", [P, CHUNK]) for b in range(2)]
        y_buf = [sb(f"a_y{b}", [P, CHUNK]) for b in range(2)]
        x_buf = [sb(f"a_x{b}", [P, D]) for b in range(2)]
        gain = sb("a_gain", [P, D])
        ident = sb("a_ident", [P, P])
        stat = sb("a_stat", [P, 3, NT + 1])
        eps = sb("a_eps", [P, 1])
        scratch = sb("a_scratch", [P, 3])
        rows = x_buf[1]
        col_all = sb("a_col_all", [P, NF, 19])
        col = sb("a_col", [P, 19])
        last_u = sb("a_last_u", [P, NF, 2 + NS])
        state_rows = x_buf[0]

        pair = [ctx.enter_context(nc.psum_tensor(f"a_pair{b}", [P, 2, BANK], F32)) for b in range(2)]
        tps = [ctx.enter_context(nc.psum_tensor(f"a_tps{b}", [P, BANK], F32)) for b in range(2)]
        square = ctx.enter_context(nc.psum_tensor("a_square", [P, D], F32))

        s_const = sem("a_const")
        s_rows = sem("a_rows")
        s_ident = sem("a_ident_ready")
        s_eps = sem("a_eps_ready")
        s_x = [sem(f"a_x_landed{b}") for b in range(2)]
        s_sumsq = sem("a_sumsq")
        s_root = sem("a_root")
        s_rstd = sem("a_rstd")
        s_xn = sem("a_xn")
        s_tr = sem("a_transposed")
        s_tr_hi = sem("a_transposed_hi")
        s_tr_free = sem("a_transpose_evacuated")
        s_col = sem("a_col_ready")
        s_wraw = [sem(f"a_w_landed{b}") for b in range(2)]
        s_whi = sem("a_w_hi_ready")
        s_wlo = sem("a_w_lo_ready")
        s_pair = sem("a_pair_ready")
        s_c = sem("a_c_copied")
        s_z = sem("a_silu_ready")
        s_free = sem("a_pair_evacuated")
        s_halo = sem("a_halo")
        s_tap0 = sem("a_tap0")
        s_tap1 = sem("a_tap1")
        s_tap2 = sem("a_tap2")
        s_stap = sem("a_sample_taps")
        s_lastu = sem("a_last_u_kept")
        s_y = sem("a_y_ready")
        s_ystore = [sem(f"a_y_stored{b}") for b in range(2)]
        s_out = sem("a_state_stored")
        s_moved = sem("a_cache_moved")

        w_view = w_in.rearrange("(k p) (g n) -> p k g n", p=P, g=4)

        block = ctx.enter_context(nc.Block())

        def x_tile(t):
            return x_prompt[t * P:(t + 1) * P, :] if t < NT else x_sample

        STATE_JOB = 1 + 2 * (NT + 1)

        @block.sync
        def _(sp):
            def load_w(i, half):
                if not isinstance(i, int) or i + half > 0:
                    sp.wait_ge(s_wlo, 4 * i + 2 * half)
                for k in (2 * half + 1, 2 * half):
                    src = w_view[:, :, GATES[k], bass.ds(i * P, P)]
                    sp.dma_start(w_raw[k % 2][:], src).then_inc(s_wraw[k % 2], 16)

            def load_x(t):
                if t >= 2:
                    sp.wait_ge(s_tr, 1 + 2 * (t - 2) + 2)
                elif t == 1:
                    sp.wait_ge(s_tr, 1)
                sp.dma_start(x_buf[t % 2][0:row_tile(t), :], x_tile(t)).then_inc(s_x[t % 2], 16)

            def store_y(i, c):
                b = (NCH + c) % 2
                sp.wait_ge(s_const, 16)
                sp.wait_ge(s_y, NCH * i + c + 1)
                sp.dma_start(y_t[bass.ds(i * P, P), c * CHUNK:c * CHUNK + size[c]],
                             y_buf[b][:, 0:size[c]]).then_inc(s_ystore[b], 16)

            def move_cache(i, c):
                for cache, moved in zip(caches, caches_out):
                    rows_all = cache.shape[1] - 1
                    per = -(-rows_all // NCH)
                    if rows_all < 1024:
                        if c > 0:
                            continue
                        per = rows_all
                    first, count = c * per, min(per, rows_all - c * per)
                    seq = bass.ds(i, 1)
                    sp.dma_start(moved[seq, first:first + count, :], cache[seq, first + 1:first + 1 + count, :])\
                      .then_inc(s_moved, 16)

            load_x(0)
            sp.dma_start(gain[:], norm_pre.partition_broadcast(P)).then_inc(s_const, 16)
            sp.dma_start(rows[0:16, :], state_conv).then_inc(s_rows, 16)
            sp.dma_start(rows[16:19, :], w_conv).then_inc(s_rows, 16)
            load_w(0, 0)
            for t in range(1, NT + 1):
                load_x(t)
                if t == 5:
                    load_w(0, 1)
            with sp.Fori(0, NF - 1) as i:
                for half in range(2):
                    load_w(i + 1, half)
                for c in range(NCH):
                    store_y(i, c)
                    move_cache(i, c)
            for c in range(NCH):
                store_y(NF - 1, c)
                move_cache(NF - 1, c)
            sp.dma_start(state_out_sample[:, 0, :],
                         state_conv.rearrange("(s j) d -> s j d", j=2)[:, 1, :]).then_inc(s_out, 16)
            sp.wait_ge(s_tr_free, STATE_JOB + 2)
            sp.dma_start(state_out_prompt, state_rows[0:2, :]).then_inc(s_out, 16)
            sp.dma_start(state_out_sample[:, 1, :], state_rows[2:2 + NS, :]).then_inc(s_out, 16)
            sp.wait_ge(s_out, 48)
            sp.wait_ge(s_moved, 16 * NS * (NCH + 2))
            for b in range(2):
                sp.wait_ge(s_ystore[b], 16 * NF * len([c for c in range(NCH) if (NCH + c) % 2 == b]))

        @block.gpsimd
        def _(pool):
            nc.gpsimd.memset(ident[:], 0.0).then_inc(s_ident, 1)
            pool.wait_ge(s_ident, 1)
            nc.gpsimd.affine_select(out=ident[:], in_=ident[:], compare_op=ALU.not_equal, fill=1.0, base=0,
                                    pattern=[[-1, P]], channel_multiplier=1).then_inc(s_ident, 1)

            def split_w_lo(i, k):
                pool.wait_ge(s_whi, 4 * i + k + 1)
                nc.gpsimd.tensor_tensor(w_lo[k][:], w_raw[k % 2][:], w_hi[k][:].bitcast(F32),
                                        ALU.subtract).then_inc(s_wlo, 1)

            for k in range(4):
                split_w_lo(0, k)
            with pool.Fori(1, NF) as i:
                for k in range(4):
                    split_w_lo(i, k)

        @block.tensor
        def _(pe):
            def transpose_tile(t):
                n = row_tile(t)
                pe.wait_ge(s_xn, t + 1)
                for half in range(2):
                    job = 1 + 2 * t + half
                    if job >= 2:
                        pe.wait_ge(s_tr_free, job - 1)
                    for k in range(4):
                        last = nc.tensor.transpose(tps[job % 2][:, k * n:(k + 1) * n],
                                                   x_buf[t % 2][0:n, (4 * half + k) * P:(4 * half + k + 1) * P],
                                                   ident[0:n, 0:n])
                    last.then_inc(s_tr, 1)

            def product_pair(i, half, c, tiles=()):
                job = JOBS * i + NCH * half + c
                slot = (NCH * half + c) % 2
                if not isinstance(job, int) or job >= 2:
                    pe.wait_ge(s_free, job - 1)
                pe.wait_ge(s_wlo, 4 * i + 2 * half + 2)
                cols = slice(c * CHUNK, c * CHUNK + size[c])
                for g in range(2):
                    out = pair[slot][:, g, 0:size[c]]
                    for k in range(KT):
                        if (g * KT + k) % 4 == 1 and (g * KT + k) // 4 < len(tiles):
                            transpose_tile(tiles[(g * KT + k) // 4])
                        hi, lo = w_hi[2 * half + g][:, k, :], w_lo[2 * half + g][:, k, :]
                        nc.tensor.matmul(out, hi, ht_hi[:, k, cols], start=(k == 0), stop=False)
                        nc.tensor.matmul(out, hi, ht_lo[:, k, cols], start=False, stop=False)
                        last = nc.tensor.matmul(out, lo, ht_hi[:, k, cols], start=False, stop=(k == KT - 1))
                last.then_inc(s_pair, 1)

            pe.wait_ge(s_ident, 2)
            pe.wait_ge(s_rows, 32)
            for k in range(KT):
                last = nc.tensor.transpose(tps[0][:, 19 * k:19 * k + 19], rows[0:19, k * P:(k + 1) * P],
                                           ident[0:19, 0:19])
            last.then_inc(s_tr, 1)
            need = [min(NT + 1, -(-(c * CHUNK + size[c]) // P)) for c in range(NCH)]
            for t in range(need[0]):
                transpose_tile(t)
            for c in range(NCH):
                pe.wait_ge(s_tr_free, 1 + 2 * need[c])
                product_pair(0, 0, c, range(need[c], need[min(c + 1, NCH - 1)]))
            with pe.Fori(1, NF) as i:
                for c in range(NCH):
                    product_pair(i - 1, 1, c)
                for c in range(NCH):
                    product_pair(i, 0, c)
            for c in range(NCH):
                product_pair(NF - 1, 1, c)
            pe.wait_ge(s_lastu, NF)
            for half in range(2):
                job = STATE_JOB + half
                for k in range(4):
                    last = nc.tensor.transpose(tps[job % 2][0:2 + NS, k * P:(k + 1) * P],
                                               last_u[:, 4 * half + k, :], ident[:])
                last.then_inc(s_tr, 1)

        @block.scalar
        def _(act):
            def norm_stats(t):
                n = row_tile(t)
                act.wait_ge(s_x[t % 2], 16 * (t // 2 + 1))
                nc.scalar.activation(square[0:n, :], x_buf[t % 2][0:n, :], ACT.Square,
                                     accum_out=stat[0:n, 0, t:t + 1]).then_inc(s_sumsq, 1)
                act.wait_ge(s_sumsq, t + 1)
                nc.scalar.activation(stat[0:n, 1, t:t + 1], stat[0:n, 0, t:t + 1], ACT.Sqrt,
                                     scale=1.0 / D, bias=eps[0:n, :]).then_inc(s_root, 1)

            def tokens_hi(t):
                n = row_tile(t)
                for half in range(2):
                    job = 1 + 2 * t + half
                    act.wait_ge(s_tr, job + 1)
                    nc.scalar.activation(ht_hi[:, 4 * half:4 * half + 4, t * P:t * P + n],
                                         tps[job % 2][:, 0:4 * n].rearrange("p (k n) -> p k n", k=4),
                                         ACT.Copy).then_inc(s_tr_hi, 1)

            def split_w_hi(i, k):
                act.wait_ge(s_wraw[k % 2], 16 * (2 * i + k // 2 + 1))
                if not isinstance(i, int) or i > 0:
                    act.wait_ge(s_pair, JOBS * (i - 1) + (NCH if k < 2 else JOBS))
                nc.scalar.activation(w_hi[k][:], w_raw[k % 2][:], ACT.Copy).then_inc(s_whi, 1)

            def copy_c(i, c):
                act.wait_ge(s_pair, JOBS * i + c + 1)
                nc.scalar.activation(c_sb[c % 2][:, 0:size[c]], pair[c % 2][:, 0, 0:size[c]],
                                     ACT.Copy).then_inc(s_c, 1)

            def tap0(i, c):
                n = size[c] if c < NCH - 1 else LAST
                act.wait_ge(s_halo, NCH * i + c + 1)
                act.wait_ge(s_free, JOBS * i + c + 1)
                nc.scalar.activation(conv[:, c * CHUNK:c * CHUNK + n], u_buf[c % 2][:, 0:n], ACT.Copy,
                                     scale=col[:, 16:17]).then_inc(s_tap0, 1)

            def gate_z(i, c):
                b = (NCH + c) % 2
                act.wait_ge(s_pair, JOBS * i + NCH + c + 1)
                read = NCH * i + max(c - 1, 0)
                if not isinstance(i, int) or read > 0:
                    act.wait_ge(s_y, read)
                nc.scalar.activation(silu_z[b][:, 0:size[c]], pair[b][:, 1, 0:size[c]],
                                     ACT.Silu).then_inc(s_z, 1)

            act.wait_ge(s_eps, 1)
            norm_stats(0)
            split_w_hi(0, 0)
            split_w_hi(0, 1)
            norm_stats(1)
            done = 0
            for c in range(NCH):
                need = min(NT + 1, -(-(c * CHUNK + size[c]) // P))
                for t in range(done, need):
                    tokens_hi(t)
                    if t + 2 <= NT:
                        norm_stats(t + 2)
                done = need
                if c >= 1:
                    copy_c(0, c - 1)
                    tap0(0, c - 1)
                    if c == 2:
                        split_w_hi(0, 2)
                        split_w_hi(0, 3)
            copy_c(0, NCH - 1)
            tap0(0, NCH - 1)
            with act.Fori(1, NF) as i:
                for c in range(NCH):
                    gate_z(i - 1, c)
                    if c == 0:
                        split_w_hi(i, 0)
                        split_w_hi(i, 1)
                for c in range(NCH):
                    copy_c(i, c)
                    tap0(i, c)
                    if c == 0:
                        split_w_hi(i, 2)
                        split_w_hi(i, 3)
            for c in range(NCH):
                gate_z(NF - 1, c)
            act.wait_ge(s_tr, STATE_JOB + 1)
            nc.scalar.activation(state_rows[0:2 + NS, 0:BANK], tps[STATE_JOB % 2][0:2 + NS, :],
                                 ACT.Copy).then_inc(s_tr_free, 1)

        @block.vector
        def _(dve):
            def normalise(t):
                n = row_tile(t)
                dve.wait_ge(s_root, t + 1)
                reciprocal_root(dve, s_rstd, 6 * t, stat[0:n, 0, t:t + 1], stat[0:n, 1, t:t + 1],
                                scratch[0:n, :], stat[0:n, 2, t:t + 1])
                if t == 0:
                    dve.wait_ge(s_const, 16)
                dve.wait_ge(s_rstd, 6 * t + 6)
                nc.vector.scalar_tensor_tensor(out=x_buf[t % 2][0:n, :], in0=x_buf[t % 2][0:n, :],
                                               scalar=stat[0:n, 2, t:t + 1], in1=gain[0:n, :],
                                               op0=ALU.mult, op1=ALU.mult).then_inc(s_xn, 1)

            def tokens_lo(t):
                n = row_tile(t)
                for half in range(2):
                    job = 1 + 2 * t + half
                    dve.wait_ge(s_tr_hi, 2 * t + half + 1)
                    cols = (slice(None), slice(4 * half, 4 * half + 4), slice(t * P, t * P + n))
                    nc.vector.tensor_tensor(ht_lo[cols],
                                            tps[job % 2][:, 0:4 * n].rearrange("p (k n) -> p k n", k=4),
                                            ht_hi[cols].bitcast(F32), ALU.subtract).then_inc(s_tr_free, 1)

            def load_columns(i):
                dve.wait_ge(s_tr_free, 1)
                nc.vector.tensor_copy(col[:], col_all[:, bass.ds(i, 1), :].rearrange("p a c -> p (a c)"))\
                  .then_inc(s_col, 1)

            def conv_inputs(i, c):
                b, n = c % 2, size[c] if c < NCH - 1 else LAST
                if c == 0:
                    nc.vector.memset(u_buf[0][:, 0:2], 0.0).then_inc(s_halo, 1)
                else:
                    nc.vector.tensor_copy(u_buf[b][:, 0:2], u_buf[1 - b][:, CHUNK:CHUNK + 2]).then_inc(s_halo, 1)
                dve.wait_ge(s_c, NCH * i + c + 1)
                nc.vector.tensor_tensor(u_buf[b][:, 2:2 + size[c]], c_sb[b][:, 0:size[c]],
                                        pair[b][:, 1, 0:size[c]], ALU.mult).then_inc(s_free, 1)
                dve.wait_ge(s_free, JOBS * i + c + 1)
                out = conv[:, c * CHUNK:c * CHUNK + n]
                if c == 0:
                    dve.wait_ge(s_col, i + 1)
                dve.wait_ge(s_halo, NCH * i + c + 1)
                dve.wait_ge(s_tap0, NCH * i + c + 1)
                nc.vector.scalar_tensor_tensor(out=out, in0=u_buf[b][:, 1:1 + n], scalar=col[:, 17:18], in1=out,
                                               op0=ALU.mult, op1=ALU.add).then_inc(s_tap1, 1)
                dve.wait_ge(s_tap1, NCH * i + c + 1)
                nc.vector.scalar_tensor_tensor(out=out, in0=u_buf[b][:, 2:2 + n], scalar=col[:, 18:19], in1=out,
                                               op0=ALU.mult, op1=ALU.add).then_inc(s_tap2, 1)
                if c < NCH - 1:
                    return
                past = col[:, 0:2 * NS].rearrange("p (s j) -> p s j", j=2)
                out = conv[:, SEQ:TOK]
                nc.vector.tensor_scalar(out, past[:, :, 0], col[:, 16:17], None, ALU.mult).then_inc(s_stap, 1)
                for tap, src in ((1, past[:, :, 1]), (2, u_buf[b][:, 2 + LAST:2 + LAST + NS])):
                    dve.wait_ge(s_stap, 3 * i + tap)
                    nc.vector.scalar_tensor_tensor(out=out, in0=src, scalar=col[:, 16 + tap:17 + tap], in1=out,
                                                   op0=ALU.mult, op1=ALU.add).then_inc(s_stap, 1)
                nc.vector.tensor_copy(last_u[:, bass.ds(i, 1), :].rearrange("p a c -> p (a c)"),
                                      u_buf[b][:, LAST:LAST + 2 + NS]).then_inc(s_lastu, 1)

            def gated(i, c):
                b = (NCH + c) % 2
                cols = slice(c * CHUNK, c * CHUNK + size[c])
                dve.wait_ge(s_z, NCH * i + c + 1)
                if c == 0:
                    dve.wait_ge(s_stap, 3 * i + 3)
                    dve.wait_ge(s_tap2, NCH * i + NCH)
                count = [k for k in range(NCH) if (NCH + k) % 2 == b]
                stored = len(count) * i + count.index(c)
                if not isinstance(i, int) or stored > 0:
                    dve.wait_ge(s_ystore[b], 16 * stored)
                nc.vector.tensor_tensor(y_buf[b][:, 0:size[c]], pair[b][:, 0, 0:size[c]], conv[:, cols],
                                        ALU.mult).then_inc(s_free, 1)
                dve.wait_ge(s_free, JOBS * i + NCH + c + 1)
                nc.vector.tensor_tensor(y_buf[b][:, 0:size[c]], y_buf[b][:, 0:size[c]],
                                        silu_z[b][:, 0:size[c]], ALU.mult).then_inc(s_y, 1)

            nc.vector.memset(eps[:], EPS).then_inc(s_eps, 1)
            normalise(0)
            dve.wait_ge(s_tr, 1)
            nc.vector.tensor_copy(col_all[:].rearrange("p k c -> p (k c)"), tps[0][:, 0:19 * KT]).then_inc(s_tr_free, 1)
            load_columns(0)
            normalise(1)
            done = 0
            for c in range(NCH):
                need = min(NT + 1, -(-(c * CHUNK + size[c]) // P))
                for t in range(done, need):
                    tokens_lo(t)
                    if t + 2 <= NT:
                        normalise(t + 2)
                done = need
                if c >= 1:
                    conv_inputs(0, c - 1)
            conv_inputs(0, NCH - 1)
            with dve.Fori(1, NF) as i:
                for c in range(NCH):
                    gated(i - 1, c)
                load_columns(i)
                for c in range(NCH):
                    conv_inputs(i, c)
            for c in range(NCH):
                gated(NF - 1, c)
            dve.wait_ge(s_tr, STATE_JOB + 2)
            nc.vector.tensor_copy(state_rows[0:2 + NS, BANK:D], tps[(STATE_JOB + 1) % 2][0:2 + NS, :])\
              .then_inc(s_tr_free, 1)


def conv_output_phase(nc, x_prompt, x_sample, y_t, w_out, norm_post, h_rows, hn_rows):
    HALVES = D // BANK

    with ExitStack() as ctx:
        def sb(name, shape, dt=F32):
            return ctx.enter_context(nc.sbuf_tensor(name, shape, dt))

        def sem(name):
            return nc.alloc_semaphore(name)

        w_raw = [sb(f"b_w_raw{b}", [P, D]) for b in range(2)]
        w_hi = sb("b_w_hi", [P, KT, D], F32R)
        w_lo = sb("b_w_lo", [P, KT, D], F32R)
        y_raw = [sb(f"b_y_raw{b}", [P, KT, P]) for b in range(2)]
        y_hi = [sb(f"b_y_hi{b}", [P, KT, P], F32R) for b in range(2)]
        y_lo = [sb(f"b_y_lo{b}", [P, KT, P], F32R) for b in range(2)]
        x_buf = [sb(f"b_x{b}", [P, D]) for b in range(2)]
        normed = sb("b_normed", [P, D])
        h_buf = [sb(f"b_h{b}", [P, D]) for b in range(2)]
        hn_buf = [sb(f"b_hn{b}", [P, D]) for b in range(2)]
        gain = sb("b_gain", [P, D])
        eps = sb("b_eps", [P, 1])
        stat = [sb(f"b_stat{b}", [P, 6]) for b in range(2)]
        scratch = sb("b_scratch", [P, 3])

        out_ps = [ctx.enter_context(nc.psum_tensor(f"b_out{b}", [P, D], F32)) for b in range(2)]
        square = ctx.enter_context(nc.psum_tensor("b_square", [P, D], F32))

        s_gain = sem("b_gain_landed")
        s_eps = sem("b_eps_ready")
        s_wraw = [sem(f"b_w_landed{b}") for b in range(2)]
        s_whi = sem("b_w_hi_ready")
        s_wlo = sem("b_w_lo_ready")
        s_y = [sem(f"b_y_landed{b}") for b in range(2)]
        s_x = [sem(f"b_x_landed{b}") for b in range(2)]
        s_yhi = sem("b_y_hi_ready")
        s_ylo = sem("b_y_lo_ready")
        s_out = sem("b_product_ready")
        s_square = sem("b_squares")
        s_root = sem("b_roots")
        s_rstd = sem("b_rstd_steps")
        s_normed = sem("b_normed_ready")
        s_h = sem("b_h_ready")
        s_hn = sem("b_hn_ready")
        s_hstore = [sem(f"b_h_stored{b}") for b in range(2)]
        s_hnstore = [sem(f"b_hn_stored{b}") for b in range(2)]

        w_view = w_out.rearrange("(k p) n -> p k n", p=P)
        y_view = y_t.rearrange("(k p) t -> p k t", p=P)
        block = ctx.enter_context(nc.Block())
        LOOPS = NT // 2 - 1
        TAIL = range(2 * LOOPS, NT + 1)

        @block.sync
        def _(sp):
            def load(t, u, i):
                n = NS if isinstance(t, int) and t == NT else P
                if not isinstance(t, int) or t >= 2:
                    sp.wait_ge(s_gain, 16)
                    sp.wait_ge(s_ylo, t - 1)
                sp.dma_start(y_raw[u][:, :, 0:n], y_view[:, :, bass.ds(t * P, n)]).then_inc(s_y[u], 16)
                if not isinstance(t, int) or t >= 2:
                    sp.wait_ge(s_gain, 16)
                    sp.wait_ge(s_h, t - 1)
                src = x_sample if n == NS else x_prompt[bass.ds(t * P, P), :]
                sp.dma_start(x_buf[u][0:n, :], src).then_inc(s_x[u], 16)

            def store(t, u):
                n = NS if isinstance(t, int) and t == NT else P
                sp.wait_ge(s_gain, 16)
                sp.wait_ge(s_h, t + 1)
                sp.dma_start(h_rows[bass.ds(t * P, n), :], h_buf[u][0:n, :]).then_inc(s_hstore[u], 16)
                sp.wait_ge(s_gain, 16)
                sp.wait_ge(s_hn, t + 1)
                sp.dma_start(hn_rows[bass.ds(t * P, n), :], hn_buf[u][0:n, :]).then_inc(s_hnstore[u], 16)

            for k in range(KT):
                if k >= 2:
                    sp.wait_ge(s_wlo, k - 1)
                if k == 1:
                    load(0, 0, 0)
                if k == 4:
                    sp.dma_start(gain[:], norm_post.partition_broadcast(P)).then_inc(s_gain, 16)
                sp.dma_start(w_raw[k % 2][:], w_view[:, k, :]).then_inc(s_wraw[k % 2], 16)
            load(1, 1, 0)
            with sp.Fori(0, LOOPS) as i:
                for u in range(2):
                    load(2 * i + u + 2, u, i + 1)
                    store(2 * i + u, u)
            load(NT, 0, NT // 2)
            for t in TAIL:
                store(t, t % 2)
            for b in range(2):
                sp.wait_ge(s_hstore[b], 16 * (NT // 2 + (b == 0)))
                sp.wait_ge(s_hnstore[b], 16 * (NT // 2 + (b == 0)))

        @block.tensor
        def _(pe):
            def product(t, u):
                n = NS if isinstance(t, int) and t == NT else P
                pe.wait_ge(s_ylo, t + 1)
                if not isinstance(t, int) or t >= 2:
                    pe.wait_ge(s_normed, t - 1)
                for k in range(KT):
                    if isinstance(t, int) and t == 0:
                        pe.wait_ge(s_wlo, k + 1)
                    for c in range(HALVES):
                        out, cols = out_ps[u][0:n, c * BANK:(c + 1) * BANK], slice(c * BANK, (c + 1) * BANK)
                        hi, lo = y_hi[u][:, k, 0:n], y_lo[u][:, k, 0:n]
                        nc.tensor.matmul(out, hi, w_hi[:, k, cols], start=(k == 0), stop=False)
                        nc.tensor.matmul(out, hi, w_lo[:, k, cols], start=False, stop=False)
                        last = nc.tensor.matmul(out, lo, w_hi[:, k, cols], start=False, stop=(k == KT - 1))
                last.then_inc(s_out, 1)

            product(0, 0)
            product(1, 1)
            with pe.Fori(1, LOOPS) as i:
                for u in range(2):
                    product(2 * i + u, u)
            for t in TAIL:
                product(t, t % 2)

        @block.scalar
        def _(act):
            def y_high(t, u, i):
                n = NS if isinstance(t, int) and t == NT else P
                act.wait_ge(s_y[u], 16 * i + 16)
                if not isinstance(t, int) or t >= 2:
                    act.wait_ge(s_out, t - 1)
                nc.scalar.activation(y_hi[u][:, :, 0:n], y_raw[u][:, :, 0:n], ACT.Copy).then_inc(s_yhi, 1)

            def norms(t, u, i, ahead=True):
                n = NS if isinstance(t, int) and t == NT else P
                act.wait_ge(s_out, t + 1)
                nc.scalar.activation(square[0:n, :], out_ps[u][0:n, :], ACT.Square,
                                     accum_out=stat[u][0:n, 0:1]).then_inc(s_square, 1)
                act.wait_ge(s_square, 2 * t + 1)
                nc.scalar.activation(stat[u][0:n, 1:2], stat[u][0:n, 0:1], ACT.Sqrt, scale=1.0 / D,
                                     bias=eps[0:n, :]).then_inc(s_root, 1)
                if ahead:
                    y_high(t + 2, u, i + 1)
                act.wait_ge(s_h, t + 1)
                nc.scalar.activation(square[0:n, :], h_buf[u][0:n, :], ACT.Square,
                                     accum_out=stat[u][0:n, 3:4]).then_inc(s_square, 1)
                act.wait_ge(s_square, 2 * t + 2)
                nc.scalar.activation(stat[u][0:n, 4:5], stat[u][0:n, 3:4], ACT.Sqrt, scale=1.0 / D,
                                     bias=eps[0:n, :]).then_inc(s_root, 1)
                act.wait_ge(s_rstd, 12 * t + 12)
                act.wait_ge(s_hnstore[u], 16 * i)
                nc.scalar.activation(hn_buf[u][0:n, :], h_buf[u][0:n, :], ACT.Copy,
                                     scale=stat[u][0:n, 5:6]).then_inc(s_hn, 1)

            y_high(0, 0, 0)
            act.wait_ge(s_eps, 1)
            for k in range(KT):
                act.wait_ge(s_wraw[k % 2], 16 * (k // 2 + 1))
                nc.scalar.activation(w_hi[:, k, :], w_raw[k % 2][:], ACT.Copy).then_inc(s_whi, 1)
            y_high(1, 1, 0)
            with act.Fori(0, LOOPS) as i:
                for u in range(2):
                    norms(2 * i + u, u, i)
            for t in TAIL:
                norms(t, t % 2, t // 2, ahead=t + 2 <= NT)

        @block.vector
        def _(dve):
            def y_low(t, u):
                n = NS if isinstance(t, int) and t == NT else P
                dve.wait_ge(s_yhi, t + 1)
                nc.vector.tensor_tensor(y_lo[u][:, :, 0:n], y_raw[u][:, :, 0:n], y_hi[u][:, :, 0:n].bitcast(F32),
                                        ALU.subtract).then_inc(s_ylo, 1)

            def norms(t, u, ahead=True):
                n = NS if isinstance(t, int) and t == NT else P
                dve.wait_ge(s_root, 2 * t + 1)
                reciprocal_root(dve, s_rstd, 12 * t, stat[u][0:n, 0:1], stat[u][0:n, 1:2],
                                scratch[0:n, :], stat[u][0:n, 2:3])
                if isinstance(t, int) and t == 0:
                    dve.wait_ge(s_gain, 16)
                dve.wait_ge(s_h, t)
                dve.wait_ge(s_rstd, 12 * t + 6)
                nc.vector.scalar_tensor_tensor(out=normed[0:n, :], in0=out_ps[u][0:n, :],
                                               scalar=stat[u][0:n, 2:3], in1=gain[0:n, :],
                                               op0=ALU.mult, op1=ALU.mult).then_inc(s_normed, 1)
                if ahead:
                    y_low(t + 2, u)
                dve.wait_ge(s_root, 2 * t + 2)
                reciprocal_root(dve, s_rstd, 12 * t + 6, stat[u][0:n, 3:4], stat[u][0:n, 4:5],
                                scratch[0:n, :], stat[u][0:n, 5:6])

            nc.vector.memset(eps[:], EPS).then_inc(s_eps, 1)
            y_low(0, 0)
            for k in range(KT):
                dve.wait_ge(s_whi, k + 1)
                nc.vector.tensor_tensor(w_lo[:, k, :], w_raw[k % 2][:], w_hi[:, k, :].bitcast(F32),
                                        ALU.subtract).then_inc(s_wlo, 1)
            y_low(1, 1)
            with dve.Fori(0, LOOPS) as i:
                for u in range(2):
                    norms(2 * i + u, u)
            for t in TAIL:
                norms(t, t % 2, ahead=t + 2 <= NT)

        @block.gpsimd
        def _(pool):
            def add(t, u, i):
                n = NS if isinstance(t, int) and t == NT else P
                pool.wait_ge(s_x[u], 16 * i + 16)
                pool.wait_ge(s_hstore[u], 16 * i)
                pool.wait_ge(s_hnstore[u], 16 * i)
                pool.wait_ge(s_normed, t + 1)
                nc.gpsimd.tensor_tensor(h_buf[u][0:n, :], x_buf[u][0:n, :], normed[0:n, :],
                                        ALU.add).then_inc(s_h, 1)

            with pool.Fori(0, LOOPS) as i:
                for u in range(2):
                    add(2 * i + u, u, i)
            for t in TAIL:
                add(t, t % 2, t // 2)


HD = 128
HEADS = 8
KVH = 2
QPK = HEADS // KVH
KVW = KVH * HD
GROUPS = 3
WINDOWS = (128, 512, 2048)
DILATIONS = (1, 4, 16)
ROPE_THETA = 10000.0
SCALE = HD ** -0.5
MASKED = -1e30
OMW = D + 2 * HEADS


def group_phase(nc, g, hn_rows, w_kv, w_q, kv_gain, q_gain, rope_rows,
                partial, cache_out, q_sample, kv_sample):
    TILES = SEQ // P
    UN = 4
    BODIES = TILES // UN
    STEP = DILATIONS[g]
    ROW_I, ROW_U = ((UN * P, P), (1, UN * P), (UN, 1))[g]
    KW = KVW + KVW + D
    BANK_COLS = [slice(b * BANK, (b + 1) * BANK) for b in range(3)]

    def has_before(u):
        return g == 0 or (g == 1 and u > 0)

    def names(u, last):
        probs = ("a", "b") if has_before(u) else ("a",)
        tokens = () if last and u >= 2 else ("h0", "h1")
        return ["q0", "k", "q1", *tokens, *("p0" + x for x in probs), *("p1" + x for x in probs)]

    FIRST_JOBS = 6
    PER_BODY = sum(len(names(u, False)) for u in range(UN))
    assert PER_BODY % 2 == 0

    def job(i, u, name, last):
        before = sum(len(names(v, last)) for v in range(u)) + names(u, last).index(name)
        return FIRST_JOBS + before + PER_BODY * i, (FIRST_JOBS + before) % 2

    with ExitStack() as ctx:
        def sb(name, shape, dt=F32):
            return ctx.enter_context(nc.sbuf_tensor(f"g{g}_{name}", shape, dt))

        def ps(name, shape):
            return ctx.enter_context(nc.psum_tensor(f"g{g}_{name}", shape, F32))

        def sem(name):
            return nc.alloc_semaphore(f"g{g}_{name}")

        w_raw = [sb(f"w_raw{b}", [P, KW]) for b in range(2)]
        w_hi = sb("w_hi", [P, KT, KW], F32R)
        w_lo = sb("w_lo", [P, KT, KW], F32R)
        gains = sb("gains", [P, 2, KT])
        tok = [sb(f"tok{b}", [P, D]) for b in range(2)]
        ht_hi = [sb(f"ht_hi{b}", [P, KT, P], F32R) for b in range(2)]
        ht_lo = [sb(f"ht_lo{b}", [P, KT, P], F32R) for b in range(2)]
        trig = [sb(f"trig{b}", [P, 3, HD // 2]) for b in range(2)]
        rot_a = [sb(f"rot_a{b}", [P, BANK]) for b in range(3)]
        rot_b = [sb(f"rot_b{b}", [P, BANK]) for b in range(3)]
        q_rot = [sb(f"q_rot{n}", [P, BANK]) for n in range(KVH)]
        kv_rows = [sb(f"kv_rows{b}", [P, 2 * KVW]) for b in range(2)]
        qt_hi = [sb(f"qt_hi{n}", [P, BANK], F32R) for n in range(KVH)]
        qt_lo = [sb(f"qt_lo{n}", [P, BANK], F32R) for n in range(KVH)]
        kt_hi = sb("kt_hi", [P, KVH, 2 * P], F32R)
        kt_lo = sb("kt_lo", [P, KVH, 2 * P], F32R)
        v_hi = [sb(f"v_hi{b}", [P, KVW], F32R) for b in range(2)]
        v_lo = [sb(f"v_lo{b}", [P, KVW], F32R) for b in range(2)]
        probs = sb("probs", [P, QPK, 2 * P])
        pt_hi = sb("pt_hi", [P, 2 * BANK], F32R)
        pt_lo = sb("pt_lo", [P, 2 * BANK], F32R)
        minus_max = sb("minus_max", [P, QPK])
        part = [sb(f"part{b}", [P, OMW]) for b in range(2)]
        mask_f = sb("mask_f", [P, 3, P])
        mask = sb("mask", [P, (3 + 2 * BODIES) * P], BF16)
        ident = sb("ident", [P, P])
        ident_b = sb("ident_b", [P, P], BF16)

        proj = ps("proj", [P, 3, BANK])
        score = ps("score", [P, QPK, 2 * P])
        tps = [ps(f"tps{b}", [P, BANK]) for b in range(2)]
        out_ps = ps("out", [P, BANK])

        s_gains = sem("gains_landed")
        s_ident = sem("ident_ready")
        s_mask = sem("mask_ready")
        s_wraw = [sem(f"w_landed{b}") for b in range(2)]
        s_whi = sem("w_hi_ready")
        s_wlo = sem("w_lo_ready")
        s_tok = [sem(f"tok_landed{b}") for b in range(2)]
        s_trig = [sem(f"trig_landed{b}") for b in range(2)]
        s_tr = sem("transposed")
        s_tr_hi = sem("transposed_hi")
        s_tr_free = sem("transpose_evacuated")
        s_proj = sem("projected")
        s_rope = sem("rope_products")
        s_rot = sem("rotated")
        s_v = sem("v_copied")
        s_vhi = sem("v_hi_ready")
        s_vlo = sem("v_lo_ready")
        s_score = sem("scores_ready")
        s_max = sem("max_ready")
        s_bias = sem("bias_ready")
        s_exp = sem("exps_ready")
        s_pv = sem("pv_ready")
        s_part = sem("partial_ready")
        s_kvstore = [sem(f"kv_stored{b}") for b in range(2)]
        s_partstore = [sem(f"partial_stored{b}") for b in range(2)]
        s_sstore = sem("sample_stored")

        kv_view = w_kv.rearrange("(k p) (j g n) -> p k j g n", p=P, j=2, g=GROUPS)
        q_view = w_q.rearrange("(k p) n -> p k n", p=P)
        block = ctx.enter_context(nc.Block())

        def rows(i, u):
            i, u = i + u // UN, u % UN
            return bass.ds(ROW_I * i + ROW_U * u, P, step=STEP)


        @block.sync
        def _(sp):
            def load_tokens(i, u):
                b = (u + 1) % 2
                sp.dma_start(tok[b][:], hn_rows[rows(i, u), :]).then_inc(s_tok[b], 16)

            def load_trig(i, u):
                b = (u + 1) % 2
                sp.dma_start(trig[b][:], rope_rows[rows(i, u), :].rearrange("t (c n) -> t c n", c=3))\
                  .then_inc(s_trig[b], 16)

            def step(i, u, last=False):
                a = UN * i + u
                if not last or u < 2:
                    sp.wait_ge(s_gains, 32)
                    sp.wait_ge(s_rope, 3 * a + 6)
                    load_trig(i, u + 2)
                b = (u + 1) % 2
                if g == 2 or (g == 1 and u == UN - 1) or (g == 0 and last and u == UN - 1):
                    sp.wait_ge(s_v, a + 2)
                    sp.wait_ge(s_gains, 32)
                    sp.wait_ge(s_rot, 3 * (a + 1) + 1)
                    dst = {0: cache_out, 1: cache_out[bass.ds(i, P, step=STEP), :] if g == 1 else None,
                           2: cache_out[rows(i, u), :] if g == 2 else None}[g]
                    sp.dma_start(dst, kv_rows[b][:]).then_inc(s_kvstore[b], 16)
                if not last:
                    sp.wait_ge(s_gains, 32)
                    sp.wait_ge(s_tr, job(i, u, "h1", last)[0] + 1)
                    load_tokens(i, u + 4)
                sp.wait_ge(s_gains, 32)
                sp.wait_ge(s_part, 2 * a + 2)
                sp.dma_start(partial[rows(i, u), :], part[u % 2][:]).then_inc(s_partstore[u % 2], 16)

            sp.dma_start(tok[0][0:NS, :], hn_rows[SEQ:TOK, :]).then_inc(s_tok[0], 16)
            sp.dma_start(gains[:, 0, :], kv_gain.rearrange("(k p) -> p k", p=P),
                         allow_slow_non_contiguous=True).then_inc(s_gains, 16)
            sp.dma_start(gains[:, 1, :], q_gain.rearrange("(k p) -> p k", p=P),
                         allow_slow_non_contiguous=True).then_inc(s_gains, 16)
            for k in range(KT):
                if k >= 2:
                    sp.wait_ge(s_wlo, k - 1)
                raw, landed = w_raw[k % 2], s_wraw[k % 2]
                sp.dma_start(raw[:, 0:2 * KVW].rearrange("p (j n) -> p j n", j=2),
                             kv_view[:, k, :, g, :]).then_inc(landed, 16)
                sp.dma_start(raw[:, 2 * KVW:KW], q_view[:, k, g * D:(g + 1) * D]).then_inc(landed, 16)
                if k == 1:
                    sp.dma_start(trig[0][0:NS], rope_rows[SEQ:SEQ + 1, :].rearrange("a (c n) -> a c n", c=3)
                                 .to_broadcast([NS, 3, HD // 2])).then_inc(s_trig[0], 16)
                    load_tokens(0, 0)
                    load_trig(0, 0)
            sp.wait_ge(s_tr, 2)
            load_tokens(0, 1)
            sp.wait_ge(s_rope, 3)
            load_trig(0, 1)
            sp.wait_ge(s_rot, 3)
            sp.wait_ge(s_v, 1)
            sp.dma_start(kv_sample, kv_rows[0][0:NS, :]).then_inc(s_sstore, 16)
            for n in range(KVH):
                sp.dma_start(q_sample[:, n * BANK:(n + 1) * BANK], q_rot[n][0:NS, :]).then_inc(s_sstore, 16)
            for u in (2, 3):
                sp.wait_ge(s_tr, 2 * u)
                load_tokens(0, u)
            with sp.Fori(0, BODIES - 1) as i:
                for u in range(UN):
                    step(i, u)
            for u in range(UN):
                step(BODIES - 1, u, last=True)
            for b in range(2):
                sp.wait_ge(s_partstore[b], 16 * TILES // 2)
            if g == 2:
                for b in range(2):
                    sp.wait_ge(s_kvstore[b], 16 * TILES // 2)
            else:
                sp.wait_ge(s_kvstore[0], 16 * (BODIES if g == 1 else 1))

        @block.tensor
        def _(pe):
            def bank_wait(number):
                if not isinstance(number, int) or number >= 2:
                    pe.wait_ge(s_tr_free, number - 1)

            def turn(number, bank, src, blocks, n=P):
                bank_wait(number)
                for x, first in enumerate(blocks):
                    t = nc.tensor.transpose(tps[bank][:, x * n:(x + 1) * n], src[0:n, first:first + P],
                                            ident[0:n, 0:n])
                t.then_inc(s_tr, 1)

            def turn_tokens(e, b, numbers, n=P, landed=1):
                pe.wait_ge(s_tok[b], 16 * landed)
                for half in range(2):
                    turn(*numbers[half], tok[b], [(4 * half + k) * P for k in range(4)], n)

            def product(e, b, bank, k, n=P):
                out, cols = proj[0:n, bank, :], BANK_COLS[bank]
                hi, lo = ht_hi[b][:, k, 0:n], ht_lo[b][:, k, 0:n]
                nc.tensor.matmul(out, hi, w_hi[:, k, cols], start=(k == 0), stop=False)
                nc.tensor.matmul(out, hi, w_lo[:, k, cols], start=False, stop=False)
                last = nc.tensor.matmul(out, lo, w_hi[:, k, cols], start=False, stop=(k == KT - 1))
                if k == KT - 1:
                    last.then_inc(s_proj, 1)

            def project(e, b, bank, k0, k1):
                if k0 == 0:
                    pe.wait_ge(s_rope, 3 * e - 2 + bank)
                for k in range(k0, k1):
                    product(e, b, bank, k)

            def scores(i, u, n, last):
                a = UN * i + u
                before = has_before(u)
                pe.wait_ge(s_tr_free, job(i, u, ("k", "q1")[n], last)[0] + 1)
                pe.wait_ge(s_exp, 8 * a + 4 * n)
                width = 2 * P if before else P
                cols = slice(0, 2 * P) if before else slice((u % 2) * P, (u % 2 + 1) * P)
                if g == 0 and u == 0:
                    m = mask[:, bass.ds((3 + 2 * i) * P, width)]
                elif before and u % 2:
                    m = mask[:, P:3 * P]
                else:
                    m = mask[:, 0:width]
                for h in range(QPK):
                    if h % 2 == 0:
                        nc.tensor.matmul(score[:, h:h + 2, cols], ident_b[:],
                                         m.unsqueeze(1).to_broadcast([P, 2, width]), start=True, stop=False,
                                         skip_group_check=True)
                    q, out = slice(h * P, (h + 1) * P), score[:, h, cols]
                    nc.tensor.matmul(out, qt_hi[n][:, q], kt_hi[:, n, cols], start=False, stop=False,
                                     skip_group_check=True)
                    nc.tensor.matmul(out, qt_hi[n][:, q], kt_lo[:, n, cols], start=False, stop=False,
                                     skip_group_check=True)
                    t = nc.tensor.matmul(out, qt_lo[n][:, q], kt_hi[:, n, cols], start=False,
                                         stop=True, skip_group_check=True)
                t.then_inc(s_score, 1)

            def turn_probs(i, u, n, last):
                pe.wait_ge(s_exp, 8 * (UN * i + u) + 4 * n + 4)
                src = probs[:].rearrange("p h k -> p (h k)")
                if has_before(u):
                    for x, name in enumerate("ab"):
                        turn(*job(i, u, f"p{n}{name}", last), src, [(4 * x + y) * P for y in range(4)])
                else:
                    turn(*job(i, u, f"p{n}a", last), src, [(2 * h + u % 2) * P for h in range(QPK)])

            def values(i, u, n, last):
                a = UN * i + u
                parities = (0, 1) if has_before(u) else (u % 2,)
                name = f"p{n}" + ("b" if has_before(u) else "a")
                pe.wait_ge(s_tr_free, job(i, u, name, last)[0] + 1)
                pe.wait_ge(s_vlo, a + 1)
                pe.wait_ge(s_part, 2 * a + n)
                v = slice(n * HD, (n + 1) * HD)
                for h in range(QPK):
                    out = out_ps[:, h * P:(h + 1) * P]
                    for y, par in enumerate(parities):
                        at = (len(parities) * h + y) * P
                        first, final = h + y == 0, y == len(parities) - 1
                        hi, lo = pt_hi[:, at:at + P], pt_lo[:, at:at + P]
                        nc.tensor.matmul(out, hi, v_hi[par][:, v], start=first, stop=False, skip_group_check=True)
                        nc.tensor.matmul(out, hi, v_lo[par][:, v], start=False, stop=False, skip_group_check=True)
                        t = nc.tensor.matmul(out, lo, v_hi[par][:, v], start=False, stop=final,
                                             skip_group_check=True)
                t.then_inc(s_pv, 1)

            def step(i, u, last=False):
                a, b = UN * i + u, (u + 1) % 2
                e, eb = a + 2, u % 2
                more = not last or u < UN - 1
                pe.wait_ge(s_rot, 3 * (a + 1) + 3)
                turn(*job(i, u, "q0", last), q_rot[0], [h * P for h in range(QPK)])
                turn(*job(i, u, "k", last), kv_rows[b], [n * P for n in range(KVH)])
                if more:
                    project(e, eb, 0, 0, KT)
                scores(i, u, 0, last)
                turn(*job(i, u, "q1", last), q_rot[1], [h * P for h in range(QPK)])
                if more:
                    project(e, eb, 1, 0, 4)
                if "h0" in names(u, last):
                    turn_tokens(a + 3, b, [job(i, u, "h0", last), job(i, u, "h1", last)],
                                landed=2 * i + (u + 3) // 2 + 1)
                if more:
                    project(e, eb, 1, 4, KT)
                turn_probs(i, u, 0, last)
                scores(i, u, 1, last)
                if more:
                    project(e, eb, 2, 0, 5)
                values(i, u, 0, last)
                turn_probs(i, u, 1, last)
                if more:
                    project(e, eb, 2, 5, KT)
                values(i, u, 1, last)

            pe.wait_ge(s_ident, 2)
            turn_tokens(0, 0, [(0, 0), (1, 1)], NS)
            turn_tokens(1, 1, [(2, 0), (3, 1)])
            for k in range(KT):
                pe.wait_ge(s_wlo, k + 1)
                for bank in range(3):
                    product(0, 0, bank, k, NS)
            turn_tokens(2, 0, [(4, 0), (5, 1)], landed=2)
            for bank in range(3):
                project(1, 1, bank, 0, KT)
            pe.wait_ge(s_mask, 4)
            with pe.Fori(0, BODIES - 1) as i:
                for u in range(UN):
                    step(i, u)
            for u in range(UN):
                step(BODIES - 1, u, last=True)

        def evacuations(i, u, last):
            b = (u + 1) % 2
            par = slice((u % 2) * P, (u % 2 + 1) * P)
            to = {"q0": (BANK, qt_hi[0][:], qt_lo[0][:]), "q1": (BANK, qt_hi[1][:], qt_lo[1][:]),
                  "k": (KVW, kt_hi[:, :, par], kt_lo[:, :, par])}
            for half in range(2):
                k = slice(4 * half, 4 * half + 4)
                to[f"h{half}"] = (BANK, ht_hi[b][:, k, :], ht_lo[b][:, k, :])
            for n in range(KVH):
                for x, name in enumerate("ab"):
                    cols = slice(x * BANK, (x + 1) * BANK)
                    to[f"p{n}{name}"] = (BANK, pt_hi[:, cols], pt_lo[:, cols])
            return {name: (job(i, u, name, last), *to[name]) for name in names(u, last)}

        def bank_view(bank, width, like):
            src = tps[bank][:, 0:width]
            return src.rearrange("p (a b) -> p a b", a=like.shape[1]) if len(like.shape) == 3 else src

        @block.scalar
        def _(act):
            def high(number, bank, width, hi, lo):
                act.wait_ge(s_tr, number + 1)
                nc.scalar.activation(hi, bank_view(bank, width, hi), ACT.Copy).then_inc(s_tr_hi, 1)

            def copy_v(e, b, n=P):
                act.wait_ge(s_proj, 3 * e + 1)
                if not isinstance(e, int) or e >= 2:
                    act.wait_ge(s_vlo, e - 2)
                nc.scalar.activation(kv_rows[b][0:n, KVW:2 * KVW], proj[0:n, 0, KVW:2 * KVW],
                                     ACT.Copy).then_inc(s_v, 1)

            def exponentials(i, u, n):
                a = UN * i + u
                act.wait_ge(s_bias, 2 * a + n + 1)
                cols = slice(0, 2 * P) if has_before(u) else slice((u % 2) * P, (u % 2 + 1) * P)
                for h in range(QPK):
                    x = QPK * n + h
                    nc.scalar.activation(probs[:, h, cols], score[:, h, cols], ACT.Exp,
                                         bias=part[u % 2][:, D + x:D + x + 1], scale=SCALE,
                                         accum_out=part[u % 2][:, D + HEADS + x:D + HEADS + x + 1])\
                      .then_inc(s_exp, 1)

            def copy_sums(i, u, n):
                act.wait_ge(s_pv, 2 * (UN * i + u) + n + 1)
                nc.scalar.activation(part[u % 2][:, n * BANK:(n + 1) * BANK], out_ps[:], ACT.Copy).then_inc(s_part, 1)

            def step(i, u, last=False):
                a, b, ev = UN * i + u, (u + 1) % 2, evacuations(i, u, last)
                split = lambda name: name in ev and high(*ev[name][0], *ev[name][1:])
                split("q0")
                split("k")
                act.wait_ge(s_v, a + 2)
                nc.scalar.activation(v_hi[u % 2][:], kv_rows[b][:, KVW:2 * KVW], ACT.Copy).then_inc(s_vhi, 1)
                if not last or u < UN - 1:
                    if g == 2 or (g == 1 and u == 0):
                        act.wait_ge(s_kvstore[u % 2], 16 * (2 * i + (u + 1) // 2 if g == 2 else i))
                    copy_v(a + 2, u % 2)
                exponentials(i, u, 0)
                for name in ("q1", "h0", "h1", "p0a", "p0b"):
                    split(name)
                exponentials(i, u, 1)
                copy_sums(i, u, 0)
                split("p1a")
                split("p1b")
                copy_sums(i, u, 1)

            def tokens_high(e, numbers, n=P):
                for half, number in enumerate(numbers):
                    k = slice(4 * half, 4 * half + 4)
                    high(number, half, 4 * n, ht_hi[e % 2][:, k, 0:n], None)

            tokens_high(0, (0, 1), NS)
            tokens_high(1, (2, 3))
            act.wait_ge(s_gains, 32)
            for k in range(KT):
                act.wait_ge(s_wraw[k % 2], 32 * (k // 2 + 1))
                for x, cols in enumerate((slice(0, 2 * KVW), slice(2 * KVW, KW))):
                    nc.scalar.activation(w_hi[:, k, cols], w_raw[k % 2][:, cols], ACT.Copy,
                                         scale=gains[:, x, k:k + 1]).then_inc(s_whi, 1)
            copy_v(0, 0, NS)
            tokens_high(2, (4, 5))
            copy_v(1, 1)
            act.wait_ge(s_sstore, 48)
            with act.Fori(0, BODIES - 1) as i:
                for u in range(UN):
                    step(i, u)
            for u in range(UN):
                step(BODIES - 1, u, last=True)

        @block.vector
        def _(dve):
            def low(number, bank, width, hi, lo):
                dve.wait_ge(s_tr_hi, number + 1)
                nc.vector.tensor_tensor(lo, bank_view(bank, width, hi), hi.bitcast(F32),
                                        ALU.subtract).then_inc(s_tr_free, 1)

            def rope(e, b, bank, landed, n=P):
                heads = KVH if bank == 0 else QPK
                dve.wait_ge(s_proj, 3 * e + bank + 1)
                if bank == 0:
                    dve.wait_ge(s_v, e + 1)
                dve.wait_ge(s_trig[b], 16 * landed)
                if not isinstance(e, int) or e > 0:
                    dve.wait_ge(s_rot, 3 * e + bank - 2)
                src = proj[0:n, bank, 0:heads * HD].rearrange("p (h c x) -> p h c x", h=heads, c=2)
                a, c = (x[bank][0:n, 0:heads * HD].rearrange("p (h c x) -> p h c x", h=heads, c=2)
                        for x in (rot_a, rot_b))
                shape = [n, heads, 2, HD // 2]
                nc.vector.tensor_tensor(a, src, trig[b][0:n, 0:1, :].unsqueeze(1).to_broadcast(shape), ALU.mult)
                nc.vector.tensor_tensor(c, src[:, :, ::-1, :],
                                        trig[b][0:n, 1:3, :].unsqueeze(1).to_broadcast(shape),
                                        ALU.mult).then_inc(s_rope, 1)

            def maxima(i, u, n):
                a = UN * i + u
                cols = slice(0, 2 * P) if has_before(u) else slice((u % 2) * P, (u % 2 + 1) * P)
                dve.wait_ge(s_score, 2 * a + n + 1)
                nc.vector.tensor_reduce(minus_max[:], score[:, :, cols], AX_X, ALU.max, negate=True)\
                  .then_inc(s_max, 1)
                dve.wait_ge(s_partstore[u % 2], 16 * (2 * i + u // 2))
                dve.wait_ge(s_max, 2 * a + n + 1)
                nc.vector.tensor_scalar(part[u % 2][:, D + QPK * n:D + QPK * (n + 1)], minus_max[:], SCALE, None,
                                        ALU.mult).then_inc(s_bias, 1)

            def step(i, u, last=False):
                a, ev = UN * i + u, evacuations(i, u, last)
                split = lambda name: name in ev and low(*ev[name][0], *ev[name][1:])
                more, landed = not last or u < UN - 1, 2 * i + (u + 2) // 2 + 1
                split("q0")
                split("k")
                maxima(i, u, 0)
                if more:
                    rope(a + 2, u % 2, 0, landed)
                for name in ("q1", "h0", "h1"):
                    split(name)
                if more:
                    rope(a + 2, u % 2, 1, landed)
                split("p0a")
                split("p0b")
                maxima(i, u, 1)
                split("p1a")
                split("p1b")
                if more:
                    rope(a + 2, u % 2, 2, landed)

            def tokens_low(e, numbers, n=P):
                for half, number in enumerate(numbers):
                    k = slice(4 * half, 4 * half + 4)
                    low(number, half, 4 * n, ht_hi[e % 2][:, k, 0:n], ht_lo[e % 2][:, k, 0:n])

            tokens_low(0, (0, 1), NS)
            tokens_low(1, (2, 3))
            for k in range(KT):
                for x, cols in enumerate((slice(0, 2 * KVW), slice(2 * KVW, KW))):
                    dve.wait_ge(s_whi, 2 * k + x + 1)
                    t = nc.vector.scalar_tensor_tensor(out=w_lo[:, k, cols], in0=w_raw[k % 2][:, cols],
                                                       scalar=gains[:, x, k:k + 1],
                                                       in1=w_hi[:, k, cols].bitcast(F32),
                                                       op0=ALU.mult, op1=ALU.subtract)
                t.then_inc(s_wlo, 1)
            for bank in range(3):
                rope(0, 0, bank, 1, NS)
            tokens_low(2, (4, 5))
            for bank in range(3):
                rope(1, 1, bank, 1)
            with dve.Fori(0, BODIES - 1) as i:
                for u in range(UN):
                    step(i, u)
            for u in range(UN):
                step(BODIES - 1, u, last=True)

        @block.gpsimd
        def _(pool):
            def rotated(e, b, bank, n=P):
                heads = KVH if bank == 0 else QPK
                dst = kv_rows[b] if bank == 0 else q_rot[bank - 1]
                pool.wait_ge(s_rope, 3 * e + bank + 1)
                nc.gpsimd.tensor_tensor(dst[0:n, 0:heads * HD], rot_a[bank][0:n, 0:heads * HD],
                                        rot_b[bank][0:n, 0:heads * HD], ALU.add).then_inc(s_rot, 1)

            def step(i, u, last=False):
                a, b = UN * i + u, (u + 1) % 2
                pool.wait_ge(s_vhi, a + 1)
                nc.gpsimd.tensor_tensor(v_lo[u % 2][:], kv_rows[b][:, KVW:2 * KVW], v_hi[u % 2][:].bitcast(F32),
                                        ALU.subtract).then_inc(s_vlo, 1)
                if last and u == UN - 1:
                    return
                if g == 2 or (g == 1 and u == 0):
                    pool.wait_ge(s_kvstore[u % 2], 16 * (2 * i + (u + 1) // 2 if g == 2 else i))
                for bank in range(3):
                    rotated(a + 2, u % 2, bank)

            nc.gpsimd.memset(ident[:], 0.0).then_inc(s_ident, 1)
            pool.wait_ge(s_ident, 1)
            nc.gpsimd.affine_select(out=ident[:], in_=ident[:], compare_op=ALU.not_equal, fill=1.0, base=0,
                                    pattern=[[-1, P]], channel_multiplier=1).then_inc(s_ident, 1)
            nc.gpsimd.memset(mask_f[:, 0:2, :], 0.0)
            nc.gpsimd.memset(mask_f[:, 2, :], MASKED).then_inc(s_mask, 1)
            pool.wait_ge(s_mask, 1)
            nc.gpsimd.affine_select(out=mask_f[:, 0, :], in_=mask_f[:, 0, :], compare_op=ALU.is_ge, fill=MASKED,
                                    base=0, pattern=[[-1, P]], channel_multiplier=1).then_inc(s_mask, 1)
            nc.gpsimd.affine_select(out=mask_f[:, 1, :], in_=mask_f[:, 1, :], compare_op=ALU.is_ge, fill=MASKED,
                                    base=0, pattern=[[1, P]], channel_multiplier=-1).then_inc(s_mask, 1)
            if g == 0:
                for zero in (kt_hi[:, :, P:2 * P], kt_lo[:, :, P:2 * P], v_hi[1][:], v_lo[1][:]):
                    nc.gpsimd.memset(zero.bitcast(F32), 0.0)
            pool.wait_ge(s_ident, 2)
            pool.wait_ge(s_mask, 3)
            nc.gpsimd.tensor_copy(ident_b[:], ident[:])
            for x, kind in enumerate([0, 1, 0] + [0, 2] + [0, 1] * (BODIES - 1)):
                t = nc.gpsimd.tensor_copy(mask[:, x * P:(x + 1) * P], mask_f[:, kind, :])
            t.then_inc(s_mask, 1)
            for bank in range(3):
                rotated(0, 0, bank, NS)
            pool.wait_ge(s_sstore, 48)
            for bank in range(3):
                rotated(1, 1, bank)
            with pool.Fori(0, BODIES - 1) as i:
                for u in range(UN):
                    step(i, u)
            for u in range(UN):
                step(BODIES - 1, u, last=True)


def sample_attention_phase(nc, q_sample, kv_sample, caches, o_sample, caches_out):
    R = NS * HEADS
    KEYS = P

    with ExitStack() as ctx:
        def sb(name, shape, dt=F32):
            return ctx.enter_context(nc.sbuf_tensor(f"s_{name}", shape, dt))

        def ps(name, shape):
            return ctx.enter_context(nc.psum_tensor(f"s_{name}", shape, F32))

        def sem(name):
            return nc.alloc_semaphore(f"s_{name}")

        cache = [sb(f"cache{b}", [P, NS // 2, 2 * KVW]) for b in range(4)]
        q_rows = sb("q_rows", [R, GROUPS, HD])
        kv_rows = sb("kv_rows", [R, GROUPS, 2, HD])
        qt = sb("qt", [P, GROUPS, R])
        keys_t = [sb(f"keys_t{b}", [P, 4, P]) for b in range(2)]
        score_t = sb("score_t", [P, R])
        score = sb("score", [R, KEYS + 1])
        prob = sb("prob", [R, KEYS + 1])
        prob_t = sb("prob_t", [P, R])
        sum_t = sb("sum_t", [P, R])
        product = sb("product", [R, HD])
        sums = sb("sums", [R, GROUPS, HD])
        stat = sb("stat", [R, 4, GROUPS])
        small = sb("small", [R, 4])
        merged = sb("merged", [R, HD])
        ident = sb("ident", [P, P])

        tps = [ps(f"tps{b}", [P, 4, P]) for b in range(2)]
        one = ps("one", [P, BANK])[:, 0:P]
        st_ps = ps("scores_t", [P, BANK])[:, 0:R]
        ot_ps = ps("sums_t", [P, BANK])[:, 0:R]

        s_ident = sem("ident_ready")
        s_q = sem("queries_landed")
        s_rows = [sem(f"new_rows_landed{g}") for g in range(GROUPS)]
        s_cache = [sem(f"cache_landed{b}") for b in range(4)]
        s_keys = sem("keys_turned")
        s_keys_sb = sem("keys_copied")
        s_one = sem("single_turned")
        s_one_sb = sem("single_copied")
        s_st = sem("scores_t_ready")
        s_st_sb = sem("scores_t_copied")
        s_new = sem("new_score")
        s_bias = sem("bias_steps")
        s_exp = sem("exps_ready")
        s_ot = sem("sums_t_ready")
        s_ot_sb = sem("sums_t_copied")
        s_sum = sem("sums_ready")
        s_w = sem("weights_ready")
        s_step = sem("merge_steps")
        s_out = sem("stored")

        block = ctx.enter_context(nc.Block())

        SINGLE = 4

        @block.sync
        def _(sp):
            def load_new_rows():
                for g in range(GROUPS):
                    new = kv_sample[g].rearrange("b (j n d) -> b j n d", j=2, d=HD)
                    for x in range(HEADS):
                        sp.dma_start(kv_rows[x:R:HEADS, g, :, :], new[:, :, x // QPK, :]).then_inc(s_rows[g], 16)

            for g in range(GROUPS):
                sp.dma_start(q_rows[:, g, :], q_sample[g].rearrange("b (x d) -> (b x) d", d=HD)).then_inc(s_q, 16)
            for g in range(GROUPS):
                d = DILATIONS[g]
                cached = caches[g].rearrange("b (k d) c -> k d b c", d=d)[:, 0, :, :]
                for half in range(2):
                    n = 2 * g + half
                    if n >= 4:
                        sp.wait_ge(s_ot, g - 1)
                    sp.dma_start(cache[n % 4][:], cached[:, half * 4:half * 4 + 4, :]).then_inc(s_cache[n % 4], 16)
                if g == 1:
                    load_new_rows()
            for g in range(GROUPS):
                sp.dma_start(caches_out[g][:, caches_out[g].shape[1] - 1, :], kv_sample[g]).then_inc(s_out, 16)
            sp.wait_ge(s_step, 10)
            sp.dma_start(o_sample.rearrange("b (x d) -> (b x) d", d=HD), merged[:]).then_inc(s_out, 16)
            sp.wait_ge(s_out, 16 * (GROUPS + 1))

        @block.gpsimd
        def _(pool):
            nc.gpsimd.memset(ident[:], 0.0).then_inc(s_ident, 1)
            pool.wait_ge(s_ident, 1)
            nc.gpsimd.affine_select(out=ident[:], in_=ident[:], compare_op=ALU.not_equal, fill=1.0, base=0,
                                    pattern=[[-1, P]], channel_multiplier=1).then_inc(s_ident, 1)

        @block.tensor
        def _(pe):
            pe.wait_ge(s_ident, 2)
            pe.wait_ge(s_q, 16 * GROUPS)
            for g in range(GROUPS):
                def single(n, dst, src, rows):
                    if SINGLE * g + n > 0:
                        pe.wait_ge(s_one_sb, SINGLE * g + n)
                    nc.tensor.transpose(dst, src, ident[0:rows, 0:rows]).then_inc(s_one, 1)

                def turn_keys(quad):
                    n = 4 * g + quad
                    c = 2 * g + quad // 2
                    pe.wait_ge(s_cache[c % 4], 16 * (c // 4 + 1))
                    if n >= 2:
                        pe.wait_ge(s_keys_sb, n - 1)
                    for x in range(4):
                        t = nc.tensor.transpose(tps[n % 2][:, x, :],
                                                cache[c % 4][:, 2 * (quad % 2) + x // 2, (x % 2) * HD:(x % 2 + 1) * HD],
                                                ident[:])
                    t.then_inc(s_keys, 1)
                single(0, one[:, 0:R], q_rows[:, g, :], R)
                turn_keys(0)
                pe.wait_ge(s_one_sb, SINGLE * g + 1)
                if g > 0:
                    pe.wait_ge(s_st_sb, g)
                for quad in range(4):
                    n = 4 * g + quad
                    if quad < 3:
                        turn_keys(quad + 1)
                    pe.wait_ge(s_keys_sb, n + 1)
                    for x in range(4):
                        row = (4 * quad + x) * QPK
                        t = nc.tensor.matmul(st_ps[:, row:row + QPK], keys_t[n % 2][:, x, :],
                                             qt[:, g, row:row + QPK], start=True, stop=True)
                t.then_inc(s_st, 1)
                pe.wait_ge(s_st_sb, g + 1)
                single(1, one[0:R, :], score_t[:], P)
                pe.wait_ge(s_exp, g + 1)
                single(2, one[:, 0:R], prob[:, 0:KEYS], R)
                pe.wait_ge(s_one_sb, SINGLE * g + 3)
                if g > 0:
                    pe.wait_ge(s_ot_sb, g)
                for pair in range(NS * KVH):
                    seq, n = pair // KVH, pair % KVH
                    c = 2 * g + seq // 4
                    t = nc.tensor.matmul(ot_ps[:, pair * QPK:(pair + 1) * QPK],
                                         cache[c % 4][:, seq % 4, KVW + n * HD:KVW + (n + 1) * HD],
                                         prob_t[:, pair * QPK:(pair + 1) * QPK], start=True, stop=True)
                t.then_inc(s_ot, 1)
                pe.wait_ge(s_ot_sb, g + 1)
                single(3, one[0:R, :], sum_t[:], P)

        @block.scalar
        def _(act):
            for g in range(GROUPS):
                act.wait_ge(s_one, SINGLE * g + 1)
                nc.scalar.activation(qt[:, g, :], one[:, 0:R], ACT.Copy).then_inc(s_one_sb, 1)
                for quad in range(4):
                    n = 4 * g + quad
                    act.wait_ge(s_keys, n + 1)
                    nc.scalar.activation(keys_t[n % 2][:], tps[n % 2][:], ACT.Copy).then_inc(s_keys_sb, 1)
                act.wait_ge(s_st, g + 1)
                nc.scalar.activation(score_t[:], st_ps, ACT.Copy).then_inc(s_st_sb, 1)
                act.wait_ge(s_one, SINGLE * g + 2)
                nc.scalar.activation(score[:, 0:KEYS], one[0:R, :], ACT.Copy).then_inc(s_one_sb, 1)
                act.wait_ge(s_bias, 2 * g + 2)
                nc.scalar.activation(prob[:], score[:], ACT.Exp, bias=stat[:, 0, g:g + 1], scale=SCALE,
                                     accum_out=stat[:, 1, g:g + 1]).then_inc(s_exp, 1)
                act.wait_ge(s_one, SINGLE * g + 3)
                nc.scalar.activation(prob_t[:], one[:, 0:R], ACT.Copy).then_inc(s_one_sb, 1)
                act.wait_ge(s_ot, g + 1)
                nc.scalar.activation(sum_t[:], ot_ps, ACT.Copy).then_inc(s_ot_sb, 1)
            act.wait_ge(s_step, 3)
            nc.scalar.activation(stat[:, 2, :], stat[:, 3, :], ACT.Exp).then_inc(s_w, 1)

        @block.vector
        def _(dve):
            dve.wait_ge(s_q, 16 * GROUPS)
            for g in range(GROUPS):
                if g > 0:
                    dve.wait_ge(s_exp, g)
                    dve.wait_ge(s_new, g)
                dve.wait_ge(s_rows[g], 16 * HEADS)
                nc.vector.tensor_tensor_reduce(out=product[:], in0=q_rows[:, g, :], in1=kv_rows[:, g, 0, :],
                                               scale=1.0, scalar=0.0, op0=ALU.mult, op1=ALU.add,
                                               accum_out=score[:, KEYS:KEYS + 1]).then_inc(s_new, 1)
                dve.wait_ge(s_new, g + 1)
                dve.wait_ge(s_one_sb, SINGLE * g + 2)
                nc.vector.tensor_reduce(small[:, 0:1], score[:], AX_X, ALU.max, negate=True).then_inc(s_bias, 1)
                dve.wait_ge(s_bias, 2 * g + 1)
                nc.vector.tensor_scalar(stat[:, 0, g:g + 1], small[:, 0:1], SCALE, None, ALU.mult).then_inc(s_bias, 1)
                dve.wait_ge(s_one, SINGLE * g + 4)
                nc.vector.scalar_tensor_tensor(out=sums[:, g, :], in0=kv_rows[:, g, 1, :],
                                               scalar=prob[:, KEYS:KEYS + 1], in1=one[0:R, :],
                                               op0=ALU.mult, op1=ALU.add).then_inc(s_one_sb, 1)
            least, total, inverse = small[:, 1:2], small[:, 2:3], small[:, 3:4]
            dve.wait_ge(s_bias, 2 * GROUPS)
            nc.vector.tensor_reduce(least, stat[:, 0, :], AX_X, ALU.min).then_inc(s_step, 1)
            dve.wait_ge(s_step, 1)
            nc.vector.tensor_scalar(stat[:, 3, :], stat[:, 0, :], least, None, ALU.subtract).then_inc(s_step, 1)
            dve.wait_ge(s_step, 2)
            nc.vector.tensor_scalar(stat[:, 3, :], stat[:, 3, :], -1.0, None, ALU.mult).then_inc(s_step, 1)
            dve.wait_ge(s_w, 1)
            nc.vector.tensor_tensor(stat[:, 3, :], stat[:, 2, :], stat[:, 1, :], ALU.mult).then_inc(s_step, 1)
            dve.wait_ge(s_step, 4)
            nc.vector.tensor_reduce(total, stat[:, 3, :], AX_X, ALU.add).then_inc(s_step, 1)
            dve.wait_ge(s_step, 5)
            nc.vector.reciprocal(inverse, total).then_inc(s_step, 1)
            dve.wait_ge(s_step, 6)
            nc.vector.tensor_scalar(stat[:, 3, :], stat[:, 2, :], inverse, None, ALU.mult).then_inc(s_step, 1)
            dve.wait_ge(s_one_sb, SINGLE * GROUPS)
            dve.wait_ge(s_step, 7)
            nc.vector.tensor_scalar(merged[:], sums[:, 0, :], stat[:, 3, 0:1], None, ALU.mult).then_inc(s_step, 1)
            for g in (1, 2):
                dve.wait_ge(s_step, 7 + g)
                nc.vector.scalar_tensor_tensor(out=merged[:], in0=sums[:, g, :], scalar=stat[:, 3, g:g + 1],
                                               in1=merged[:], op0=ALU.mult, op1=ALU.add).then_inc(s_step, 1)


def attention_output_phase(nc, hn_rows, h_rows, partials, o_sample, w_z, w_out, pre_gain, norm_post,
                           y_prompt, y_sample):
    UN = 2
    BODIES = (NT - 3) // UN
    TAIL = range(UN * BODIES + 1, NT + 1)

    with ExitStack() as ctx:
        def sb(name, shape, dt=F32):
            return ctx.enter_context(nc.sbuf_tensor(f"d_{name}", shape, dt))

        def ps(name, shape):
            return ctx.enter_context(nc.psum_tensor(f"d_{name}", shape, F32))

        def sem(name):
            return nc.alloc_semaphore(f"d_{name}")

        w_raw = [sb(f"w_raw{b}", [P, D]) for b in range(2)]
        w_hi = sb("w_hi", [P, 2, KT, D], F32R)
        w_lo = sb("w_lo", [P, 2, KT, D], F32R)
        tok = [sb(f"tok{b}", [P, D]) for b in range(2)]
        ht_hi = sb("ht_hi", [P, KT, P], F32R)
        ht_lo = sb("ht_lo", [P, KT, P], F32R)
        gt_hi = sb("gt_hi", [P, KT, P], F32R)
        gt_lo = sb("gt_lo", [P, KT, P], F32R)
        part = [sb(f"part{b}", [P, GROUPS, OMW]) for b in range(2)]
        silu_z = sb("silu_z", [P, D])
        normed = sb("normed", [P, D])
        h_buf = [sb(f"h{b}", [P, D]) for b in range(2)]
        post_gain = sb("post_gain", [P, D])
        gains = sb("gains", [P, KT])
        coef = sb("coef", [P, 3, GROUPS, HEADS])
        small = sb("small", [P, 3, HEADS])
        eps = sb("eps", [P, 1])
        stat = sb("stat", [P, 3])
        scratch = sb("scratch", [P, 3])
        ident = sb("ident", [P, P])

        z_ps = ps("z", [P, D])
        out_ps = ps("out", [P, D])
        square = ps("square", [P, D])
        tps = [ps(f"tps{b}", [P, BANK]) for b in range(2)]

        s_const = sem("gains_landed")
        s_ident = sem("ident_ready")
        s_eps = sem("eps_ready")
        s_wraw = [sem(f"w_landed{b}") for b in range(2)]
        s_whi = sem("w_hi_ready")
        s_wlo = sem("w_lo_ready")
        s_tok = [sem(f"tok_landed{b}") for b in range(2)]
        s_h = [sem(f"h_landed{b}") for b in range(2)]
        s_p = [sem(f"partials_landed{b}") for b in range(2)]
        s_tr = sem("transposed")
        s_tr_hi = sem("transposed_hi")
        s_tr_free = sem("transpose_evacuated")
        s_z = sem("z_ready")
        s_silu = sem("silu_ready")
        s_diff = sem("merge_steps")
        s_exp = sem("weights_ready")
        s_mul = sem("weighted")
        s_mul2 = sem("weighted_last")
        s_gated = sem("gated_ready")
        s_out = sem("product_ready")
        s_square = sem("squares")
        s_root = sem("roots")
        s_rstd = sem("rstd_steps")
        s_normed = sem("normed_ready")
        s_y = sem("y_ready")
        s_ystore = [sem(f"y_stored{b}") for b in range(2)]

        block = ctx.enter_context(nc.Block())

        def tile(i, u, k=0):
            return 2 * i + 1 + u + k, (1 + u + k) % 2, i + (1 + u + k) // 2

        def height(t):
            return NS if isinstance(t, int) and t == NT else P

        def above(value, bound):
            return not isinstance(value, int) or value >= bound

        def token_job(t):
            return 0 if isinstance(t, int) and t == 0 else 4 * t - 2

        def gated_job(t):
            return 4 * t + 2 if isinstance(t, int) and t == NT else 4 * t + 4

        def run_steps(engine, step):
            step(0, -1)
            with engine.Fori(0, BODIES) as i:
                for u in range(UN):
                    step(i, u)
            for t in TAIL:
                step(0, t - 1)

        @block.sync
        def _(sp):
            def load_tokens(t, b):
                n = height(t)
                sp.dma_start(tok[b][0:n, :], hn_rows[bass.ds(t * P, n), :]).then_inc(s_tok[b], 16)

            def load_parts(t, b):
                if height(t) == NS:
                    sp.dma_start(part[b][0:NS, 0, 0:D], o_sample).then_inc(s_p[b], 16)
                    return
                for g in range(GROUPS):
                    sp.dma_start(part[b][:, g, :], partials[g][bass.ds(t * P, P), :]).then_inc(s_p[b], 16)

            def step(i, u):
                t, b, m = tile(i, u)
                if not isinstance(t, int) or t + 3 <= NT:
                    if above(t, 0):
                        sp.wait_ge(s_const, 16)
                        sp.wait_ge(s_tr, token_job(t + 1) + 2)
                    load_tokens(*tile(i, u, 3)[:2])
                n = height(t)
                if above(t, 2):
                    sp.wait_ge(s_const, 16)
                    sp.wait_ge(s_ystore[b], 16 * m)
                sp.dma_start(h_buf[b][0:n, :], h_rows[bass.ds(t * P, n), :]).then_inc(s_h[b], 16)
                if not isinstance(t, int) or t + 2 <= NT:
                    sp.wait_ge(s_const, 16)
                    sp.wait_ge(s_tr, gated_job(t) + 2)
                    load_parts(t + 2, b)
                if above(t, 1):
                    store(*tile(i, u, -1)[:2])

            def store(t, b):
                n = height(t)
                sp.wait_ge(s_const, 16)
                sp.wait_ge(s_y, t + 1)
                dst = y_sample if n == NS else y_prompt[bass.ds(t * P, P), :]
                sp.dma_start(dst, h_buf[b][0:n, :]).then_inc(s_ystore[b], 16)

            load_tokens(0, 0)
            sp.dma_start(gains[:], pre_gain.rearrange("(k p) -> p k", p=P),
                         allow_slow_non_contiguous=True).then_inc(s_const, 16)
            for k in range(2 * KT):
                if k >= 2:
                    sp.wait_ge(s_wlo, k - 1)
                src = (w_z, w_out)[k // KT].rearrange("(k p) n -> p k n", p=P)[:, k % KT, :]
                sp.dma_start(w_raw[k % 2][:], src).then_inc(s_wraw[k % 2], 16)
                if k == 2:
                    load_tokens(1, 1)
                    load_parts(0, 0)
                if k == KT:
                    load_parts(1, 1)
                    sp.wait_ge(s_tr, 2)
                    load_tokens(2, 0)
                    sp.dma_start(post_gain[:], norm_post.partition_broadcast(P)).then_inc(s_const, 16)
            run_steps(sp, step)
            store(NT, NT % 2)
            for b in range(2):
                sp.wait_ge(s_ystore[b], 16 * (NT // 2 + (b == 0)))

        @block.tensor
        def _(pe):
            def turn(number, bank, src, first, n):
                if above(number, 2):
                    pe.wait_ge(s_tr_free, number - 1)
                for x in range(4):
                    last = nc.tensor.transpose(tps[bank][:, x * n:(x + 1) * n],
                                               src[0:n, first + x * P:first + (x + 1) * P], ident[0:n, 0:n])
                last.then_inc(s_tr, 1)

            def turn_tokens(t, b, m):
                pe.wait_ge(s_tok[b], 16 * m + 16)
                for half in range(2):
                    turn(token_job(t) + half, half, tok[b], half * BANK, height(t))

            def turn_gated(t, b):
                pe.wait_ge(s_gated, t + 1)
                for half in range(2):
                    turn(gated_job(t) + half, half, part[b][:, 0, :], half * BANK, height(t))

            def product(dst, which, hi_t, lo_t, ks, n, weights=False):
                for k in ks:
                    if weights:
                        pe.wait_ge(s_wlo, which * KT + k + 1)
                    for c in range(D // BANK):
                        cols = slice(c * BANK, (c + 1) * BANK)
                        hi, lo = hi_t[:, k, 0:n], lo_t[:, k, 0:n]
                        nc.tensor.matmul(dst[0:n, cols], hi, w_hi[:, which, k, cols], start=(k == 0), stop=False)
                        nc.tensor.matmul(dst[0:n, cols], hi, w_lo[:, which, k, cols], start=False, stop=False)
                        last = nc.tensor.matmul(dst[0:n, cols], lo, w_hi[:, which, k, cols], start=False,
                                                stop=(k == KT - 1))
                return last

            def z_product(t):
                pe.wait_ge(s_tr_free, token_job(t) + 2)
                if above(t, 1):
                    pe.wait_ge(s_silu, t)
                product(z_ps, 0, ht_hi, ht_lo, range(KT), height(t),
                        weights=isinstance(t, int) and t == 0).then_inc(s_z, 1)

            def step(i, u):
                t, b, m = tile(i, u)
                turn_gated(t, b)
                if not isinstance(t, int) or t < NT:
                    z_product(t + 1)
                pe.wait_ge(s_tr_free, gated_job(t) + 2)
                if above(t, 1):
                    pe.wait_ge(s_normed, t)
                first = isinstance(t, int) and t == 0
                product(out_ps, 1, gt_hi, gt_lo, range(0, KT // 2), height(t), weights=first)
                if not isinstance(t, int) or t + 2 <= NT:
                    turn_tokens(*tile(i, u, 2))
                product(out_ps, 1, gt_hi, gt_lo, range(KT // 2, KT), height(t), weights=first).then_inc(s_out, 1)

            pe.wait_ge(s_ident, 2)
            turn_tokens(0, 0, 0)
            z_product(0)
            turn_tokens(1, 1, 0)
            run_steps(pe, step)

        def halves(hi_t, lo_t, n):
            return [(hi_t[:, 4 * x:4 * x + 4, 0:n], lo_t[:, 4 * x:4 * x + 4, 0:n]) for x in range(2)]

        def bank_view(x, n):
            return tps[x][:, 0:4 * n].rearrange("p (k n) -> p k n", k=4)

        @block.scalar
        def _(act):
            def high(number, hi_t, lo_t, n):
                for x, (hi, _lo) in enumerate(halves(hi_t, lo_t, n)):
                    act.wait_ge(s_tr, number + x + 1)
                    nc.scalar.activation(hi, bank_view(x, n), ACT.Copy).then_inc(s_tr_hi, 1)

            def split_w(k):
                act.wait_ge(s_wraw[k % 2], 16 * (k // 2 + 1))
                nc.scalar.activation(w_hi[:, k // KT, k % KT, :], w_raw[k % 2][:], ACT.Copy,
                                     scale=gains[:, k:k + 1] if k < KT else 1.0).then_inc(s_whi, 1)

            def root(t):
                n = height(t)
                act.wait_ge(s_out, t + 1)
                if above(t, 1):
                    act.wait_ge(s_rstd, 6 * t)
                nc.scalar.activation(square[0:n, :], out_ps[0:n, :], ACT.Square,
                                     accum_out=stat[0:n, 0:1]).then_inc(s_square, 1)
                act.wait_ge(s_square, t + 1)
                nc.scalar.activation(stat[0:n, 1:2], stat[0:n, 0:1], ACT.Sqrt, scale=1.0 / D,
                                     bias=eps[0:n, :]).then_inc(s_root, 1)

            def weights(t):
                act.wait_ge(s_diff, 6 * t + 2)
                nc.scalar.activation(coef[:, 1, :, :], coef[:, 0, :, :], ACT.Exp).then_inc(s_exp, 1)

            def gate(t):
                n = height(t)
                act.wait_ge(s_z, t + 1)
                if above(t, 1):
                    act.wait_ge(s_gated, t)
                nc.scalar.activation(silu_z[0:n, :], z_ps[0:n, :], ACT.Silu).then_inc(s_silu, 1)

            def step(i, u):
                t, b, m = tile(i, u)
                high(gated_job(t), gt_hi, gt_lo, height(t))
                if above(t, 1):
                    root(t - 1)
                if not isinstance(t, int) or t + 1 < NT:
                    weights(t + 1)
                if not isinstance(t, int) or t < NT:
                    gate(t + 1)
                if not isinstance(t, int) or t + 2 <= NT:
                    high(token_job(t + 2), ht_hi, ht_lo, height(t + 2))

            high(0, ht_hi, ht_lo, P)
            act.wait_ge(s_const, 16)
            for k in range(KT):
                split_w(k)
            weights(0)
            gate(0)
            high(token_job(1), ht_hi, ht_lo, P)
            for k in range(KT, 2 * KT):
                split_w(k)
            act.wait_ge(s_eps, 1)
            run_steps(act, step)
            root(NT)

        def weigh(engine, b, g):
            x = part[b][:, g, 0:D].rearrange("p (h d) -> p h d", d=HD)
            return engine.tensor_tensor(x, x, coef[:, 2, g, :].unsqueeze(2).to_broadcast([P, HEADS, HD]), ALU.mult)

        @block.vector
        def _(dve):
            def low(number, hi_t, lo_t, n):
                for x, (hi, lo) in enumerate(halves(hi_t, lo_t, n)):
                    dve.wait_ge(s_tr_hi, number + x + 1)
                    nc.vector.tensor_tensor(lo, bank_view(x, n), hi.bitcast(F32), ALU.subtract).then_inc(s_tr_free, 1)

            def split_w(k):
                dve.wait_ge(s_whi, k + 1)
                hi, lo = w_hi[:, k // KT, k % KT, :].bitcast(F32), w_lo[:, k // KT, k % KT, :]
                if k < KT:
                    nc.vector.scalar_tensor_tensor(out=lo, in0=w_raw[k % 2][:], scalar=gains[:, k:k + 1], in1=hi,
                                                   op0=ALU.mult, op1=ALU.subtract).then_inc(s_wlo, 1)
                else:
                    nc.vector.tensor_tensor(lo, w_raw[k % 2][:], hi, ALU.subtract).then_inc(s_wlo, 1)

            def normalise(t):
                n = height(t)
                dve.wait_ge(s_root, t + 1)
                reciprocal_root(dve, s_rstd, 6 * t, stat[0:n, 0:1], stat[0:n, 1:2], scratch[0:n, :], stat[0:n, 2:3])
                if above(t, 1):
                    dve.wait_ge(s_y, t)
                dve.wait_ge(s_rstd, 6 * t + 6)
                nc.vector.scalar_tensor_tensor(out=normed[0:n, :], in0=out_ps[0:n, :], scalar=stat[0:n, 2:3],
                                               in1=post_gain[0:n, :], op0=ALU.mult, op1=ALU.mult)\
                  .then_inc(s_normed, 1)

            def coefficients(t, b, m):
                bias, denominators = (part[b][:, :, first:first + HEADS] for first in (D, D + HEADS))
                dve.wait_ge(s_p[b], 16 * GROUPS * m + 16 * GROUPS)
                if above(t, 1):
                    dve.wait_ge(s_mul, 2 * t)
                    dve.wait_ge(s_mul2, 3 * t)
                nc.vector.tensor_reduce(small[:, 0, :], bias.rearrange("p g h -> p h g"), AX_X, ALU.min)\
                  .then_inc(s_diff, 1)
                dve.wait_ge(s_diff, 6 * t + 1)
                shape = [P, GROUPS, HEADS]
                nc.vector.tensor_tensor(coef[:, 0, :, :], small[:, 0:1, :].to_broadcast(shape), bias,
                                        ALU.subtract).then_inc(s_diff, 1)
                dve.wait_ge(s_exp, t + 1)
                nc.vector.tensor_tensor(coef[:, 0, :, :], coef[:, 1, :, :], denominators, ALU.mult).then_inc(s_diff, 1)
                dve.wait_ge(s_diff, 6 * t + 3)
                nc.vector.tensor_reduce(small[:, 1, :], coef[:, 0, :, :].rearrange("p g h -> p h g"), AX_X,
                                        ALU.add).then_inc(s_diff, 1)
                dve.wait_ge(s_diff, 6 * t + 4)
                nc.vector.reciprocal(small[:, 2, :], small[:, 1, :]).then_inc(s_diff, 1)
                dve.wait_ge(s_diff, 6 * t + 5)
                nc.vector.tensor_tensor(coef[:, 2, :, :], coef[:, 1, :, :], small[:, 2:3, :].to_broadcast(shape),
                                        ALU.mult).then_inc(s_diff, 1)

            def merge(t, b, m):
                n = height(t)
                groups = [part[b][0:n, g, 0:D] for g in range(GROUPS)]
                if n == P:
                    coefficients(t, b, m)
                    dve.wait_ge(s_diff, 6 * t + 6)
                    weigh(nc.vector, b, 2).then_inc(s_mul2, 1)
                    dve.wait_ge(s_mul, 2 * t + 2)
                    nc.vector.tensor_tensor(groups[0], groups[0], groups[1], ALU.add).then_inc(s_mul2, 1)
                    dve.wait_ge(s_mul2, 3 * t + 2)
                    nc.vector.tensor_tensor(groups[0], groups[0], groups[2], ALU.add).then_inc(s_mul2, 1)
                    dve.wait_ge(s_mul2, 3 * t + 3)
                else:
                    dve.wait_ge(s_p[b], 16 * GROUPS * m + 16)
                dve.wait_ge(s_silu, t + 1)
                nc.vector.tensor_tensor(groups[0], groups[0], silu_z[0:n, :], ALU.mult).then_inc(s_gated, 1)

            def step(i, u):
                t, b, m = tile(i, u)
                low(gated_job(t), gt_hi, gt_lo, height(t))
                if above(t, 1):
                    normalise(t - 1)
                if not isinstance(t, int) or t < NT:
                    merge(*tile(i, u, 1))
                if not isinstance(t, int) or t + 2 <= NT:
                    low(token_job(t + 2), ht_hi, ht_lo, height(t + 2))

            nc.vector.memset(eps[:], EPS).then_inc(s_eps, 1)
            low(0, ht_hi, ht_lo, P)
            dve.wait_ge(s_const, 16)
            for k in range(KT):
                split_w(k)
            merge(0, 0, 0)
            low(token_job(1), ht_hi, ht_lo, P)
            for k in range(KT, 2 * KT):
                split_w(k)
            dve.wait_ge(s_const, 32)
            run_steps(dve, step)
            normalise(NT)

        @block.gpsimd
        def _(pool):
            def add(t, b, m):
                n = height(t)
                pool.wait_ge(s_h[b], 16 * m + 16)
                pool.wait_ge(s_normed, t + 1)
                nc.gpsimd.tensor_tensor(h_buf[b][0:n, :], h_buf[b][0:n, :], normed[0:n, :], ALU.add).then_inc(s_y, 1)

            def weigh_two(t, b):
                pool.wait_ge(s_diff, 6 * t + 6)
                for g in range(2):
                    weigh(nc.gpsimd, b, g).then_inc(s_mul, 1)

            def step(i, u):
                t, b, m = tile(i, u)
                if above(t, 1):
                    add(*tile(i, u, -1))
                if not isinstance(t, int) or t + 1 < NT:
                    weigh_two(*tile(i, u, 1)[:2])

            nc.gpsimd.memset(ident[:], 0.0).then_inc(s_ident, 1)
            pool.wait_ge(s_ident, 1)
            nc.gpsimd.affine_select(out=ident[:], in_=ident[:], compare_op=ALU.not_equal, fill=1.0, base=0,
                                    pattern=[[-1, P]], channel_multiplier=1).then_inc(s_ident, 1)
            weigh_two(0, 0)
            run_steps(pool, step)
            add(NT, 0, NT // 2)


def decoder_program(nc, ins, outs, scratch):
    with nc.cleanup_on_exit():
        conv_projection_phase(nc, ins["x_prompt"], ins["x_sample"], ins["state_conv"], ins["a_norm_pre"],
                              ins["a_w_in"], ins["a_conv"], scratch["y_t"], outs["state_conv_prompt"],
                              outs["state_conv_sample"], [ins[f"cache_kv_g{g}"] for g in range(GROUPS)],
                              [outs[f"cache_kv_g{g}_sample"] for g in range(GROUPS)])
    with nc.cleanup_on_exit():
        conv_output_phase(nc, ins["x_prompt"], ins["x_sample"], scratch["y_t"], ins["a_w_out"], ins["a_norm_post"],
                          scratch["h_rows"], scratch["hn_rows"])
    for g in range(GROUPS):
        with nc.cleanup_on_exit():
            group_phase(nc, g, scratch["hn_rows"], ins["w_kv"], ins["b_w_in"], ins["kv_norm"], ins["b_norm_pre"],
                        ins["rope_rows"], scratch[f"partial{g}"], outs[f"cache_kv_g{g}_prompt"],
                        scratch[f"q_sample{g}"], scratch[f"kv_sample{g}"])
    with nc.cleanup_on_exit():
        sample_attention_phase(nc, [scratch[f"q_sample{g}"] for g in range(GROUPS)],
                               [scratch[f"kv_sample{g}"] for g in range(GROUPS)],
                               [ins[f"cache_kv_g{g}"] for g in range(GROUPS)], scratch["o_sample"],
                               [outs[f"cache_kv_g{g}_sample"] for g in range(GROUPS)])
    with nc.cleanup_on_exit():
        attention_output_phase(nc, scratch["hn_rows"], scratch["h_rows"],
                               [scratch[f"partial{g}"] for g in range(GROUPS)], scratch["o_sample"],
                               ins["b_w_in"][:, GROUPS * D:(GROUPS + 1) * D], ins["b_w_out"], ins["b_norm_pre"],
                               ins["b_norm_post"], outs["y_prompt"], outs["y_sample"])


def rope_table():
    exponent = -np.arange(HD // 2, dtype=np.float32) * np.float32(2.0) / np.float32(HD)
    frequency = (ROPE_THETA ** exponent.astype(np.float64)).astype(np.float32)
    angle = np.arange(SEQ + 1, dtype=np.float32)[:, None] * frequency[None, :]
    angle = angle.astype(np.float64)
    return np.concatenate([np.cos(angle), -np.sin(angle), np.sin(angle)], axis=1).astype(np.float32)


INPUT_SHAPES = {
    "x_prompt": (SEQ, D), "x_sample": (NS, D), "state_conv": (2 * NS, D),
    **{f"cache_kv_g{g}": (NS, WINDOWS[g], 2 * KVW) for g in range(GROUPS)},
    "a_norm_pre": (D,), "a_w_in": (D, 4 * D), "a_conv": (3, D), "a_w_out": (D, D), "a_norm_post": (D,),
    "kv_norm": (D,), "w_kv": (D, 2 * GROUPS * KVW), "b_norm_pre": (D,), "b_w_in": (D, (GROUPS + 1) * D),
    "b_w_out": (D, D), "b_norm_post": (D,),
}
OUTPUT_SHAPES = {
    "y_prompt": ((SEQ, D), (1, SEQ, D)),
    "y_sample": ((NS, D), (NS, 1, D)),
    "state_conv_prompt": ((2, D), (1, 1, 2, D)),
    **{f"cache_kv_g{g}_prompt": ((WINDOWS[g], 2 * KVW), (1, WINDOWS[g], 2, KVH, HD)) for g in range(GROUPS)},
    "state_conv_sample": ((NS, 2, D), (1, NS, 2, D)),
    **{f"cache_kv_g{g}_sample": ((NS, WINDOWS[g], 2 * KVW), (NS, WINDOWS[g], 2, KVH, HD)) for g in range(GROUPS)},
}
SCRATCH_SHAPES = {
    "y_t": (D, TOK), "h_rows": (TOK, D), "hn_rows": (TOK, D), "o_sample": (NS, D),
    **{f"partial{g}": (SEQ, OMW) for g in range(GROUPS)},
    **{f"q_sample{g}": (NS, D) for g in range(GROUPS)},
    **{f"kv_sample{g}": (NS, 2 * KVW) for g in range(GROUPS)},
}


def kernel(**inputs):
    import concourse.bacc as bacc
    from concourse.bass_utils import run_bass_kernel_spmd

    nc = bacc.Bacc("TRN2", target_bir_lowering=False, num_devices=1)
    arrays = {name: np.ascontiguousarray(inputs[name]).reshape(shape) for name, shape in INPUT_SHAPES.items()}
    arrays["rope_rows"] = rope_table()
    ins = {name: nc.dram_tensor(name, list(a.shape), F32, kind="ExternalInput").ap() for name, a in arrays.items()}
    outs = {name: nc.dram_tensor(f"out_{name}", list(shape), F32, kind="ExternalOutput").ap()
            for name, (shape, _) in OUTPUT_SHAPES.items()}
    scratch = {name: nc.dram_tensor(f"scratch_{name}", list(shape), F32, kind="Internal").ap()
               for name, shape in SCRATCH_SHAPES.items()}
    decoder_program(nc, ins, outs, scratch)
    results = run_bass_kernel_spmd(nc, [arrays], core_ids=[0]).results[0]
    return tuple(np.asarray(results[f"out_{name}"]).reshape(shape) for name, (_, shape) in OUTPUT_SHAPES.items())
```

```python
from contextlib import ExitStack

import numpy as np

import concourse.bass as bass
from concourse import mybir

F32 = mybir.dt.float32
F32R = mybir.dt.float32r
BF16 = mybir.dt.bfloat16
ALU = mybir.AluOpType
ACT = mybir.ActivationFunctionType
AX_X = mybir.AxisListType.X

P = 128
D = 1024
KT = D // P
SEQ = 2048
NS = 8
TOK = SEQ + NS
NT = SEQ // P
BANK = 512
EPS = 1e-6


def row_tile(t):
    return P if t < NT else NS


def reciprocal_root(dve, done, before, square_sum, root, scratch, out):
    mean, r, e = scratch[:, 0:1], scratch[:, 1:2], scratch[:, 2:3]
    nc = dve.bass
    nc.vector.tensor_scalar(mean, square_sum, 1.0 / D, EPS, ALU.mult, ALU.add).then_inc(done, 1)
    nc.vector.reciprocal(r, root).then_inc(done, 1)
    dve.wait_ge(done, before + 2)
    nc.vector.tensor_tensor(e, r, r, ALU.mult).then_inc(done, 1)
    dve.wait_ge(done, before + 3)
    nc.vector.tensor_tensor(e, e, mean, ALU.mult).then_inc(done, 1)
    dve.wait_ge(done, before + 4)
    nc.vector.tensor_scalar(e, e, -0.5, 1.5, ALU.mult, ALU.add).then_inc(done, 1)
    dve.wait_ge(done, before + 5)
    nc.vector.tensor_tensor(out, r, e, ALU.mult).then_inc(done, 1)


def conv_projection_phase(nc, x_prompt, x_sample, state_conv, norm_pre, w_in, w_conv,
                          y_t, state_out_prompt, state_out_sample, caches, caches_out):
    CHUNK = 412
    NCH = -(-TOK // CHUNK)
    size = [min(CHUNK, TOK - c * CHUNK) for c in range(NCH)]
    LAST = size[-1] - NS
    NF = D // P
    GATES = (1, 2, 0, 3)
    JOBS = 2 * NCH

    with ExitStack() as ctx:
        def sb(name, shape, dt=F32):
            return ctx.enter_context(nc.sbuf_tensor(name, shape, dt))

        def sem(name):
            return nc.alloc_semaphore(name)

        ht_hi = sb("a_ht_hi", [P, KT, TOK], F32R)
        ht_lo = sb("a_ht_lo", [P, KT, TOK], F32R)
        w_raw = [sb(f"a_w_raw{b}", [P, KT, P]) for b in range(2)]
        w_hi = [sb(f"a_w_hi{k}", [P, KT, P], F32R) for k in range(4)]
        w_lo = [sb(f"a_w_lo{k}", [P, KT, P], F32R) for k in range(4)]
        u_buf = [sb(f"a_u{b}", [P, 2 + CHUNK]) for b in range(2)]
        conv = sb("a_conved", [P, TOK])
        c_sb = [sb(f"a_c{b}", [P, CHUNK]) for b in range(2)]
        silu_z = [sb(f"a_silu_z{b}", [P, CHUNK]) for b in range(2)]
        y_buf = [sb(f"a_y{b}", [P, CHUNK]) for b in range(2)]
        x_buf = [sb(f"a_x{b}", [P, D]) for b in range(2)]
        gain = sb("a_gain", [P, D])
        ident = sb("a_ident", [P, P])
        stat = sb("a_stat", [P, 3, NT + 1])
        eps = sb("a_eps", [P, 1])
        scratch = sb("a_scratch", [P, 3])
        rows = x_buf[1]
        col_all = sb("a_col_all", [P, NF, 19])
        col = sb("a_col", [P, 19])
        last_u = sb("a_last_u", [P, NF, 2 + NS])
        state_rows = x_buf[0]

        pair = [ctx.enter_context(nc.psum_tensor(f"a_pair{b}", [P, 2, BANK], F32)) for b in range(2)]
        tps = [ctx.enter_context(nc.psum_tensor(f"a_tps{b}", [P, BANK], F32)) for b in range(2)]
        square = ctx.enter_context(nc.psum_tensor("a_square", [P, D], F32))

        s_const = sem("a_const")
        s_rows = sem("a_rows")
        s_ident = sem("a_ident_ready")
        s_eps = sem("a_eps_ready")
        s_x = [sem(f"a_x_landed{b}") for b in range(2)]
        s_sumsq = sem("a_sumsq")
        s_root = sem("a_root")
        s_rstd = sem("a_rstd")
        s_xn = sem("a_xn")
        s_tr = sem("a_transposed")
        s_tr_hi = sem("a_transposed_hi")
        s_tr_free = sem("a_transpose_evacuated")
        s_col = sem("a_col_ready")
        s_wraw = [sem(f"a_w_landed{b}") for b in range(2)]
        s_whi = sem("a_w_hi_ready")
        s_wlo = sem("a_w_lo_ready")
        s_pair = sem("a_pair_ready")
        s_c = sem("a_c_copied")
        s_z = sem("a_silu_ready")
        s_free = sem("a_pair_evacuated")
        s_halo = sem("a_halo")
        s_tap0 = sem("a_tap0")
        s_tap1 = sem("a_tap1")
        s_tap2 = sem("a_tap2")
        s_stap = sem("a_sample_taps")
        s_lastu = sem("a_last_u_kept")
        s_y = sem("a_y_ready")
        s_ystore = [sem(f"a_y_stored{b}") for b in range(2)]
        s_out = sem("a_state_stored")
        s_moved = sem("a_cache_moved")

        w_view = w_in.rearrange("(k p) (g n) -> p k g n", p=P, g=4)

        block = ctx.enter_context(nc.Block())

        def x_tile(t):
            return x_prompt[t * P:(t + 1) * P, :] if t < NT else x_sample

        STATE_JOB = 1 + 2 * (NT + 1)

        @block.sync
        def _(sp):
            def load_w(i, half):
                if not isinstance(i, int) or i + half > 0:
                    sp.wait_ge(s_wlo, 4 * i + 2 * half)
                for k in (2 * half + 1, 2 * half):
                    src = w_view[:, :, GATES[k], bass.ds(i * P, P)]
                    sp.dma_start(w_raw[k % 2][:], src).then_inc(s_wraw[k % 2], 16)

            def load_x(t):
                if t >= 2:
                    sp.wait_ge(s_tr, 1 + 2 * (t - 2) + 2)
                elif t == 1:
                    sp.wait_ge(s_tr, 1)
                sp.dma_start(x_buf[t % 2][0:row_tile(t), :], x_tile(t)).then_inc(s_x[t % 2], 16)

            def store_y(i, c):
                b = (NCH + c) % 2
                sp.wait_ge(s_const, 16)
                sp.wait_ge(s_y, NCH * i + c + 1)
                sp.dma_start(y_t[bass.ds(i * P, P), c * CHUNK:c * CHUNK + size[c]],
                             y_buf[b][:, 0:size[c]]).then_inc(s_ystore[b], 16)

            def move_cache(i, c):
                for cache, moved in zip(caches, caches_out):
                    rows_all = cache.shape[1] - 1
                    per = -(-rows_all // NCH)
                    if rows_all < 1024:
                        if c > 0:
                            continue
                        per = rows_all
                    first, count = c * per, min(per, rows_all - c * per)
                    seq = bass.ds(i, 1)
                    sp.dma_start(moved[seq, first:first + count, :], cache[seq, first + 1:first + 1 + count, :])\
                      .then_inc(s_moved, 16)

            load_x(0)
            sp.dma_start(gain[:], norm_pre.partition_broadcast(P)).then_inc(s_const, 16)
            sp.dma_start(rows[0:16, :], state_conv).then_inc(s_rows, 16)
            sp.dma_start(rows[16:19, :], w_conv).then_inc(s_rows, 16)
            load_w(0, 0)
            for t in range(1, NT + 1):
                load_x(t)
                if t == 5:
                    load_w(0, 1)
            with sp.Fori(0, NF - 1) as i:
                for half in range(2):
                    load_w(i + 1, half)
                for c in range(NCH):
                    store_y(i, c)
                    move_cache(i, c)
            for c in range(NCH):
                store_y(NF - 1, c)
                move_cache(NF - 1, c)
            sp.dma_start(state_out_sample[:, 0, :],
                         state_conv.rearrange("(s j) d -> s j d", j=2)[:, 1, :]).then_inc(s_out, 16)
            sp.wait_ge(s_tr_free, STATE_JOB + 2)
            sp.dma_start(state_out_prompt, state_rows[0:2, :]).then_inc(s_out, 16)
            sp.dma_start(state_out_sample[:, 1, :], state_rows[2:2 + NS, :]).then_inc(s_out, 16)
            sp.wait_ge(s_out, 48)
            sp.wait_ge(s_moved, 16 * NS * (NCH + 2))
            for b in range(2):
                sp.wait_ge(s_ystore[b], 16 * NF * len([c for c in range(NCH) if (NCH + c) % 2 == b]))

        @block.gpsimd
        def _(pool):
            nc.gpsimd.memset(ident[:], 0.0).then_inc(s_ident, 1)
            pool.wait_ge(s_ident, 1)
            nc.gpsimd.affine_select(out=ident[:], in_=ident[:], compare_op=ALU.not_equal, fill=1.0, base=0,
                                    pattern=[[-1, P]], channel_multiplier=1).then_inc(s_ident, 1)

            def split_w_lo(i, k):
                pool.wait_ge(s_whi, 4 * i + k + 1)
                nc.gpsimd.tensor_tensor(w_lo[k][:], w_raw[k % 2][:], w_hi[k][:].bitcast(F32),
                                        ALU.subtract).then_inc(s_wlo, 1)

            for k in range(4):
                split_w_lo(0, k)
            with pool.Fori(1, NF) as i:
                for k in range(4):
                    split_w_lo(i, k)

        @block.tensor
        def _(pe):
            def transpose_tile(t):
                n = row_tile(t)
                pe.wait_ge(s_xn, t + 1)
                for half in range(2):
                    job = 1 + 2 * t + half
                    if job >= 2:
                        pe.wait_ge(s_tr_free, job - 1)
                    for k in range(4):
                        last = nc.tensor.transpose(tps[job % 2][:, k * n:(k + 1) * n],
                                                   x_buf[t % 2][0:n, (4 * half + k) * P:(4 * half + k + 1) * P],
                                                   ident[0:n, 0:n])
                    last.then_inc(s_tr, 1)

            def product_pair(i, half, c, tiles=()):
                job = JOBS * i + NCH * half + c
                slot = (NCH * half + c) % 2
                if not isinstance(job, int) or job >= 2:
                    pe.wait_ge(s_free, job - 1)
                pe.wait_ge(s_wlo, 4 * i + 2 * half + 2)
                cols = slice(c * CHUNK, c * CHUNK + size[c])
                for g in range(2):
                    out = pair[slot][:, g, 0:size[c]]
                    for k in range(KT):
                        if (g * KT + k) % 4 == 1 and (g * KT + k) // 4 < len(tiles):
                            transpose_tile(tiles[(g * KT + k) // 4])
                        hi, lo = w_hi[2 * half + g][:, k, :], w_lo[2 * half + g][:, k, :]
                        nc.tensor.matmul(out, hi, ht_hi[:, k, cols], start=(k == 0), stop=False)
                        nc.tensor.matmul(out, hi, ht_lo[:, k, cols], start=False, stop=False)
                        last = nc.tensor.matmul(out, lo, ht_hi[:, k, cols], start=False, stop=(k == KT - 1))
                last.then_inc(s_pair, 1)

            pe.wait_ge(s_ident, 2)
            pe.wait_ge(s_rows, 32)
            for k in range(KT):
                last = nc.tensor.transpose(tps[0][:, 19 * k:19 * k + 19], rows[0:19, k * P:(k + 1) * P],
                                           ident[0:19, 0:19])
            last.then_inc(s_tr, 1)
            need = [min(NT + 1, -(-(c * CHUNK + size[c]) // P)) for c in range(NCH)]
            for t in range(need[0]):
                transpose_tile(t)
            for c in range(NCH):
                pe.wait_ge(s_tr_free, 1 + 2 * need[c])
                product_pair(0, 0, c, range(need[c], need[min(c + 1, NCH - 1)]))
            with pe.Fori(1, NF) as i:
                for c in range(NCH):
                    product_pair(i - 1, 1, c)
                for c in range(NCH):
                    product_pair(i, 0, c)
            for c in range(NCH):
                product_pair(NF - 1, 1, c)
            pe.wait_ge(s_lastu, NF)
            for half in range(2):
                job = STATE_JOB + half
                for k in range(4):
                    last = nc.tensor.transpose(tps[job % 2][0:2 + NS, k * P:(k + 1) * P],
                                               last_u[:, 4 * half + k, :], ident[:])
                last.then_inc(s_tr, 1)

        @block.scalar
        def _(act):
            def norm_stats(t):
                n = row_tile(t)
                act.wait_ge(s_x[t % 2], 16 * (t // 2 + 1))
                nc.scalar.activation(square[0:n, :], x_buf[t % 2][0:n, :], ACT.Square,
                                     accum_out=stat[0:n, 0, t:t + 1]).then_inc(s_sumsq, 1)
                act.wait_ge(s_sumsq, t + 1)
                nc.scalar.activation(stat[0:n, 1, t:t + 1], stat[0:n, 0, t:t + 1], ACT.Sqrt,
                                     scale=1.0 / D, bias=eps[0:n, :]).then_inc(s_root, 1)

            def tokens_hi(t):
                n = row_tile(t)
                for half in range(2):
                    job = 1 + 2 * t + half
                    act.wait_ge(s_tr, job + 1)
                    nc.scalar.activation(ht_hi[:, 4 * half:4 * half + 4, t * P:t * P + n],
                                         tps[job % 2][:, 0:4 * n].rearrange("p (k n) -> p k n", k=4),
                                         ACT.Copy).then_inc(s_tr_hi, 1)

            def split_w_hi(i, k):
                act.wait_ge(s_wraw[k % 2], 16 * (2 * i + k // 2 + 1))
                if not isinstance(i, int) or i > 0:
                    act.wait_ge(s_pair, JOBS * (i - 1) + (NCH if k < 2 else JOBS))
                nc.scalar.activation(w_hi[k][:], w_raw[k % 2][:], ACT.Copy).then_inc(s_whi, 1)

            def copy_c(i, c):
                act.wait_ge(s_pair, JOBS * i + c + 1)
                nc.scalar.activation(c_sb[c % 2][:, 0:size[c]], pair[c % 2][:, 0, 0:size[c]],
                                     ACT.Copy).then_inc(s_c, 1)

            def tap0(i, c):
                n = size[c] if c < NCH - 1 else LAST
                act.wait_ge(s_halo, NCH * i + c + 1)
                act.wait_ge(s_free, JOBS * i + c + 1)
                nc.scalar.activation(conv[:, c * CHUNK:c * CHUNK + n], u_buf[c % 2][:, 0:n], ACT.Copy,
                                     scale=col[:, 16:17]).then_inc(s_tap0, 1)

            def gate_z(i, c):
                b = (NCH + c) % 2
                act.wait_ge(s_pair, JOBS * i + NCH + c + 1)
                read = NCH * i + max(c - 1, 0)
                if not isinstance(i, int) or read > 0:
                    act.wait_ge(s_y, read)
                nc.scalar.activation(silu_z[b][:, 0:size[c]], pair[b][:, 1, 0:size[c]],
                                     ACT.Silu).then_inc(s_z, 1)

            act.wait_ge(s_eps, 1)
            norm_stats(0)
            split_w_hi(0, 0)
            split_w_hi(0, 1)
            norm_stats(1)
            done = 0
            for c in range(NCH):
                need = min(NT + 1, -(-(c * CHUNK + size[c]) // P))
                for t in range(done, need):
                    tokens_hi(t)
                    if t + 2 <= NT:
                        norm_stats(t + 2)
                done = need
                if c >= 1:
                    copy_c(0, c - 1)
                    tap0(0, c - 1)
                    if c == 2:
                        split_w_hi(0, 2)
                        split_w_hi(0, 3)
            copy_c(0, NCH - 1)
            tap0(0, NCH - 1)
            with act.Fori(1, NF) as i:
                for c in range(NCH):
                    gate_z(i - 1, c)
                    if c == 0:
                        split_w_hi(i, 0)
                        split_w_hi(i, 1)
                for c in range(NCH):
                    copy_c(i, c)
                    tap0(i, c)
                    if c == 0:
                        split_w_hi(i, 2)
                        split_w_hi(i, 3)
            for c in range(NCH):
                gate_z(NF - 1, c)
            act.wait_ge(s_tr, STATE_JOB + 1)
            nc.scalar.activation(state_rows[0:2 + NS, 0:BANK], tps[STATE_JOB % 2][0:2 + NS, :],
                                 ACT.Copy).then_inc(s_tr_free, 1)

        @block.vector
        def _(dve):
            def normalise(t):
                n = row_tile(t)
                dve.wait_ge(s_root, t + 1)
                reciprocal_root(dve, s_rstd, 6 * t, stat[0:n, 0, t:t + 1], stat[0:n, 1, t:t + 1],
                                scratch[0:n, :], stat[0:n, 2, t:t + 1])
                if t == 0:
                    dve.wait_ge(s_const, 16)
                dve.wait_ge(s_rstd, 6 * t + 6)
                nc.vector.scalar_tensor_tensor(out=x_buf[t % 2][0:n, :], in0=x_buf[t % 2][0:n, :],
                                               scalar=stat[0:n, 2, t:t + 1], in1=gain[0:n, :],
                                               op0=ALU.mult, op1=ALU.mult).then_inc(s_xn, 1)

            def tokens_lo(t):
                n = row_tile(t)
                for half in range(2):
                    job = 1 + 2 * t + half
                    dve.wait_ge(s_tr_hi, 2 * t + half + 1)
                    cols = (slice(None), slice(4 * half, 4 * half + 4), slice(t * P, t * P + n))
                    nc.vector.tensor_tensor(ht_lo[cols],
                                            tps[job % 2][:, 0:4 * n].rearrange("p (k n) -> p k n", k=4),
                                            ht_hi[cols].bitcast(F32), ALU.subtract).then_inc(s_tr_free, 1)

            def load_columns(i):
                dve.wait_ge(s_tr_free, 1)
                nc.vector.tensor_copy(col[:], col_all[:, bass.ds(i, 1), :].rearrange("p a c -> p (a c)"))\
                  .then_inc(s_col, 1)

            def conv_inputs(i, c):
                b, n = c % 2, size[c] if c < NCH - 1 else LAST
                if c == 0:
                    nc.vector.memset(u_buf[0][:, 0:2], 0.0).then_inc(s_halo, 1)
                else:
                    nc.vector.tensor_copy(u_buf[b][:, 0:2], u_buf[1 - b][:, CHUNK:CHUNK + 2]).then_inc(s_halo, 1)
                dve.wait_ge(s_c, NCH * i + c + 1)
                nc.vector.tensor_tensor(u_buf[b][:, 2:2 + size[c]], c_sb[b][:, 0:size[c]],
                                        pair[b][:, 1, 0:size[c]], ALU.mult).then_inc(s_free, 1)
                dve.wait_ge(s_free, JOBS * i + c + 1)
                out = conv[:, c * CHUNK:c * CHUNK + n]
                if c == 0:
                    dve.wait_ge(s_col, i + 1)
                dve.wait_ge(s_halo, NCH * i + c + 1)
                dve.wait_ge(s_tap0, NCH * i + c + 1)
                nc.vector.scalar_tensor_tensor(out=out, in0=u_buf[b][:, 1:1 + n], scalar=col[:, 17:18], in1=out,
                                               op0=ALU.mult, op1=ALU.add).then_inc(s_tap1, 1)
                dve.wait_ge(s_tap1, NCH * i + c + 1)
                nc.vector.scalar_tensor_tensor(out=out, in0=u_buf[b][:, 2:2 + n], scalar=col[:, 18:19], in1=out,
                                               op0=ALU.mult, op1=ALU.add).then_inc(s_tap2, 1)
                if c < NCH - 1:
                    return
                past = col[:, 0:2 * NS].rearrange("p (s j) -> p s j", j=2)
                out = conv[:, SEQ:TOK]
                nc.vector.tensor_scalar(out, past[:, :, 0], col[:, 16:17], None, ALU.mult).then_inc(s_stap, 1)
                for tap, src in ((1, past[:, :, 1]), (2, u_buf[b][:, 2 + LAST:2 + LAST + NS])):
                    dve.wait_ge(s_stap, 3 * i + tap)
                    nc.vector.scalar_tensor_tensor(out=out, in0=src, scalar=col[:, 16 + tap:17 + tap], in1=out,
                                                   op0=ALU.mult, op1=ALU.add).then_inc(s_stap, 1)
                nc.vector.tensor_copy(last_u[:, bass.ds(i, 1), :].rearrange("p a c -> p (a c)"),
                                      u_buf[b][:, LAST:LAST + 2 + NS]).then_inc(s_lastu, 1)

            def gated(i, c):
                b = (NCH + c) % 2
                cols = slice(c * CHUNK, c * CHUNK + size[c])
                dve.wait_ge(s_z, NCH * i + c + 1)
                if c == 0:
                    dve.wait_ge(s_stap, 3 * i + 3)
                    dve.wait_ge(s_tap2, NCH * i + NCH)
                count = [k for k in range(NCH) if (NCH + k) % 2 == b]
                stored = len(count) * i + count.index(c)
                if not isinstance(i, int) or stored > 0:
                    dve.wait_ge(s_ystore[b], 16 * stored)
                nc.vector.tensor_tensor(y_buf[b][:, 0:size[c]], pair[b][:, 0, 0:size[c]], conv[:, cols],
                                        ALU.mult).then_inc(s_free, 1)
                dve.wait_ge(s_free, JOBS * i + NCH + c + 1)
                nc.vector.tensor_tensor(y_buf[b][:, 0:size[c]], y_buf[b][:, 0:size[c]],
                                        silu_z[b][:, 0:size[c]], ALU.mult).then_inc(s_y, 1)

            nc.vector.memset(eps[:], EPS).then_inc(s_eps, 1)
            normalise(0)
            dve.wait_ge(s_tr, 1)
            nc.vector.tensor_copy(col_all[:].rearrange("p k c -> p (k c)"), tps[0][:, 0:19 * KT]).then_inc(s_tr_free, 1)
            load_columns(0)
            normalise(1)
            done = 0
            for c in range(NCH):
                need = min(NT + 1, -(-(c * CHUNK + size[c]) // P))
                for t in range(done, need):
                    tokens_lo(t)
                    if t + 2 <= NT:
                        normalise(t + 2)
                done = need
                if c >= 1:
                    conv_inputs(0, c - 1)
            conv_inputs(0, NCH - 1)
            with dve.Fori(1, NF) as i:
                for c in range(NCH):
                    gated(i - 1, c)
                load_columns(i)
                for c in range(NCH):
                    conv_inputs(i, c)
            for c in range(NCH):
                gated(NF - 1, c)
            dve.wait_ge(s_tr, STATE_JOB + 2)
            nc.vector.tensor_copy(state_rows[0:2 + NS, BANK:D], tps[(STATE_JOB + 1) % 2][0:2 + NS, :])\
              .then_inc(s_tr_free, 1)


def conv_output_phase(nc, x_prompt, x_sample, y_t, w_out, norm_post, h_rows, hn_rows):
    HALVES = D // BANK
    RAW = 4

    with ExitStack() as ctx:
        def sb(name, shape, dt=F32):
            return ctx.enter_context(nc.sbuf_tensor(name, shape, dt))

        def sem(name):
            return nc.alloc_semaphore(name)

        w_raw = [sb(f"b_w_raw{b}", [P, D]) for b in range(RAW)]
        w_hi = sb("b_w_hi", [P, KT, D], F32R)
        w_lo = sb("b_w_lo", [P, KT, D], F32R)
        y_raw = [sb(f"b_y_raw{b}", [P, KT, P]) for b in range(2)]
        y_hi = [sb(f"b_y_hi{b}", [P, KT, P], F32R) for b in range(2)]
        y_lo = [sb(f"b_y_lo{b}", [P, KT, P], F32R) for b in range(2)]
        x_buf = [sb(f"b_x{b}", [P, D]) for b in range(2)]
        normed = sb("b_normed", [P, D])
        h_buf = [sb(f"b_h{b}", [P, D]) for b in range(2)]
        hn_buf = [sb(f"b_hn{b}", [P, D]) for b in range(2)]
        gain = sb("b_gain", [P, D])
        eps = sb("b_eps", [P, 1])
        stat = [sb(f"b_stat{b}", [P, 6]) for b in range(2)]
        scratch = sb("b_scratch", [P, 3])

        out_ps = [ctx.enter_context(nc.psum_tensor(f"b_out{b}", [P, D], F32)) for b in range(2)]
        square = ctx.enter_context(nc.psum_tensor("b_square", [P, D], F32))

        s_gain = sem("b_gain_landed")
        s_eps = sem("b_eps_ready")
        s_wraw = [sem(f"b_w_landed{b}") for b in range(RAW)]
        s_whi = sem("b_w_hi_ready")
        s_wlo = sem("b_w_lo_ready")
        s_y = [sem(f"b_y_landed{b}") for b in range(2)]
        s_x = [sem(f"b_x_landed{b}") for b in range(2)]
        s_yhi = sem("b_y_hi_ready")
        s_ylo = sem("b_y_lo_ready")
        s_out = sem("b_product_ready")
        s_square = sem("b_squares")
        s_root = sem("b_roots")
        s_rstd = sem("b_rstd_steps")
        s_normed = sem("b_normed_ready")
        s_h = sem("b_h_ready")
        s_hn = sem("b_hn_ready")
        s_hstore = [sem(f"b_h_stored{b}") for b in range(2)]
        s_hnstore = [sem(f"b_hn_stored{b}") for b in range(2)]

        w_view = w_out.rearrange("(k p) n -> p k n", p=P)
        y_view = y_t.rearrange("(k p) t -> p k t", p=P)
        block = ctx.enter_context(nc.Block())
        LOOPS = NT // 2 - 1
        TAIL = range(2 * LOOPS, NT + 1)

        @block.sync
        def _(sp):
            def load(t, u, i):
                n = NS if isinstance(t, int) and t == NT else P
                if not isinstance(t, int) or t >= 2:
                    sp.wait_ge(s_gain, 16)
                    sp.wait_ge(s_ylo, t - 1)
                sp.dma_start(y_raw[u][:, :, 0:n], y_view[:, :, bass.ds(t * P, n)]).then_inc(s_y[u], 16)
                if not isinstance(t, int) or t >= 2:
                    sp.wait_ge(s_gain, 16)
                    sp.wait_ge(s_h, t - 1)
                src = x_sample if n == NS else x_prompt[bass.ds(t * P, P), :]
                sp.dma_start(x_buf[u][0:n, :], src).then_inc(s_x[u], 16)

            def store(t, u):
                n = NS if isinstance(t, int) and t == NT else P
                sp.wait_ge(s_gain, 16)
                sp.wait_ge(s_h, t + 1)
                sp.dma_start(h_rows[bass.ds(t * P, n), :], h_buf[u][0:n, :]).then_inc(s_hstore[u], 16)
                sp.wait_ge(s_gain, 16)
                sp.wait_ge(s_hn, t + 1)
                sp.dma_start(hn_rows[bass.ds(t * P, n), :], hn_buf[u][0:n, :]).then_inc(s_hnstore[u], 16)

            for k in range(KT):
                if k >= RAW:
                    sp.wait_ge(s_wlo, k - RAW + 1)
                if k == 1:
                    load(0, 0, 0)
                if k == 4:
                    sp.dma_start(gain[:], norm_post.partition_broadcast(P)).then_inc(s_gain, 16)
                sp.dma_start(w_raw[k % RAW][:], w_view[:, k, :]).then_inc(s_wraw[k % RAW], 16)
            load(1, 1, 0)
            with sp.Fori(0, LOOPS) as i:
                for u in range(2):
                    load(2 * i + u + 2, u, i + 1)
                    store(2 * i + u, u)
            load(NT, 0, NT // 2)
            for t in TAIL:
                store(t, t % 2)
            for b in range(2):
                sp.wait_ge(s_hstore[b], 16 * (NT // 2 + (b == 0)))
                sp.wait_ge(s_hnstore[b], 16 * (NT // 2 + (b == 0)))

        @block.tensor
        def _(pe):
            def product(t, u):
                n = NS if isinstance(t, int) and t == NT else P
                pe.wait_ge(s_ylo, t + 1)
                if not isinstance(t, int) or t >= 2:
                    pe.wait_ge(s_normed, t - 1)
                for k in range(KT):
                    if isinstance(t, int) and t == 0:
                        pe.wait_ge(s_wlo, k + 1)
                    for c in range(HALVES):
                        out, cols = out_ps[u][0:n, c * BANK:(c + 1) * BANK], slice(c * BANK, (c + 1) * BANK)
                        hi, lo = y_hi[u][:, k, 0:n], y_lo[u][:, k, 0:n]
                        nc.tensor.matmul(out, hi, w_hi[:, k, cols], start=(k == 0), stop=False)
                        nc.tensor.matmul(out, hi, w_lo[:, k, cols], start=False, stop=False)
                        last = nc.tensor.matmul(out, lo, w_hi[:, k, cols], start=False, stop=(k == KT - 1))
                last.then_inc(s_out, 1)

            product(0, 0)
            product(1, 1)
            with pe.Fori(1, LOOPS) as i:
                for u in range(2):
                    product(2 * i + u, u)
            for t in TAIL:
                product(t, t % 2)

        @block.scalar
        def _(act):
            def y_high(t, u, i):
                n = NS if isinstance(t, int) and t == NT else P
                act.wait_ge(s_y[u], 16 * i + 16)
                if not isinstance(t, int) or t >= 2:
                    act.wait_ge(s_out, t - 1)
                nc.scalar.activation(y_hi[u][:, :, 0:n], y_raw[u][:, :, 0:n], ACT.Copy).then_inc(s_yhi, 1)

            def norms(t, u, i, ahead=True):
                n = NS if isinstance(t, int) and t == NT else P
                act.wait_ge(s_out, t + 1)
                nc.scalar.activation(square[0:n, :], out_ps[u][0:n, :], ACT.Square,
                                     accum_out=stat[u][0:n, 0:1]).then_inc(s_square, 1)
                act.wait_ge(s_square, 2 * t + 1)
                nc.scalar.activation(stat[u][0:n, 1:2], stat[u][0:n, 0:1], ACT.Sqrt, scale=1.0 / D,
                                     bias=eps[0:n, :]).then_inc(s_root, 1)
                if ahead:
                    y_high(t + 2, u, i + 1)
                act.wait_ge(s_h, t + 1)
                nc.scalar.activation(square[0:n, :], h_buf[u][0:n, :], ACT.Square,
                                     accum_out=stat[u][0:n, 3:4]).then_inc(s_square, 1)
                act.wait_ge(s_square, 2 * t + 2)
                nc.scalar.activation(stat[u][0:n, 4:5], stat[u][0:n, 3:4], ACT.Sqrt, scale=1.0 / D,
                                     bias=eps[0:n, :]).then_inc(s_root, 1)
                act.wait_ge(s_rstd, 12 * t + 12)
                act.wait_ge(s_hnstore[u], 16 * i)
                nc.scalar.activation(hn_buf[u][0:n, :], h_buf[u][0:n, :], ACT.Copy,
                                     scale=stat[u][0:n, 5:6]).then_inc(s_hn, 1)

            y_high(0, 0, 0)
            act.wait_ge(s_eps, 1)
            for k in range(KT):
                act.wait_ge(s_wraw[k % RAW], 16 * (k // RAW + 1))
                nc.scalar.activation(w_hi[:, k, :], w_raw[k % RAW][:], ACT.Copy).then_inc(s_whi, 1)
            y_high(1, 1, 0)
            with act.Fori(0, LOOPS) as i:
                for u in range(2):
                    norms(2 * i + u, u, i)
            for t in TAIL:
                norms(t, t % 2, t // 2, ahead=t + 2 <= NT)

        @block.vector
        def _(dve):
            def y_low(t, u):
                n = NS if isinstance(t, int) and t == NT else P
                dve.wait_ge(s_yhi, t + 1)
                nc.vector.tensor_tensor(y_lo[u][:, :, 0:n], y_raw[u][:, :, 0:n], y_hi[u][:, :, 0:n].bitcast(F32),
                                        ALU.subtract).then_inc(s_ylo, 1)

            def norms(t, u, ahead=True):
                n = NS if isinstance(t, int) and t == NT else P
                dve.wait_ge(s_root, 2 * t + 1)
                reciprocal_root(dve, s_rstd, 12 * t, stat[u][0:n, 0:1], stat[u][0:n, 1:2],
                                scratch[0:n, :], stat[u][0:n, 2:3])
                if isinstance(t, int) and t == 0:
                    dve.wait_ge(s_gain, 16)
                dve.wait_ge(s_h, t)
                dve.wait_ge(s_rstd, 12 * t + 6)
                nc.vector.scalar_tensor_tensor(out=normed[0:n, :], in0=out_ps[u][0:n, :],
                                               scalar=stat[u][0:n, 2:3], in1=gain[0:n, :],
                                               op0=ALU.mult, op1=ALU.mult).then_inc(s_normed, 1)
                if ahead:
                    y_low(t + 2, u)
                dve.wait_ge(s_root, 2 * t + 2)
                reciprocal_root(dve, s_rstd, 12 * t + 6, stat[u][0:n, 3:4], stat[u][0:n, 4:5],
                                scratch[0:n, :], stat[u][0:n, 5:6])

            nc.vector.memset(eps[:], EPS).then_inc(s_eps, 1)
            y_low(0, 0)
            for k in range(KT):
                dve.wait_ge(s_whi, k + 1)
                nc.vector.tensor_tensor(w_lo[:, k, :], w_raw[k % RAW][:], w_hi[:, k, :].bitcast(F32),
                                        ALU.subtract).then_inc(s_wlo, 1)
            y_low(1, 1)
            with dve.Fori(0, LOOPS) as i:
                for u in range(2):
                    norms(2 * i + u, u)
            for t in TAIL:
                norms(t, t % 2, ahead=t + 2 <= NT)

        @block.gpsimd
        def _(pool):
            def add(t, u, i):
                n = NS if isinstance(t, int) and t == NT else P
                pool.wait_ge(s_x[u], 16 * i + 16)
                pool.wait_ge(s_hstore[u], 16 * i)
                pool.wait_ge(s_hnstore[u], 16 * i)
                pool.wait_ge(s_normed, t + 1)
                nc.gpsimd.tensor_tensor(h_buf[u][0:n, :], x_buf[u][0:n, :], normed[0:n, :],
                                        ALU.add).then_inc(s_h, 1)

            with pool.Fori(0, LOOPS) as i:
                for u in range(2):
                    add(2 * i + u, u, i)
            for t in TAIL:
                add(t, t % 2, t // 2)


HD = 128
HEADS = 8
KVH = 2
QPK = HEADS // KVH
KVW = KVH * HD
GROUPS = 3
WINDOWS = (128, 512, 2048)
DILATIONS = (1, 4, 16)
ROPE_THETA = 10000.0
SCALE = HD ** -0.5
MASKED = -1e30
OMW = D + 2 * HEADS


def group_phase(nc, g, hn_rows, w_kv, w_q, kv_gain, q_gain, rope_rows,
                partial, cache_out, q_sample, new_rows, newest):
    TILES = SEQ // P
    UN = 4
    BODIES = TILES // UN
    STEP = DILATIONS[g]
    ROW_I, ROW_U = ((UN * P, P), (1, UN * P), (UN, 1))[g]
    KW = KVW + KVW + D
    BANK_COLS = [slice(b * BANK, (b + 1) * BANK) for b in range(3)]

    def has_before(u):
        return g == 0 or (g == 1 and u > 0)

    def names(u, last):
        probs = ("a", "b") if has_before(u) else ("a",)
        tokens = () if last and u >= 2 else ("h0", "h1")
        return ["q0", "k", "q1", *tokens, *("p0" + x for x in probs), *("p1" + x for x in probs), "o0", "o1"]

    FIRST_JOBS = 6
    PER_BODY = sum(len(names(u, False)) for u in range(UN))
    assert PER_BODY % 2 == 0

    def job(i, u, name, last):
        before = sum(len(names(v, last)) for v in range(u)) + names(u, last).index(name)
        return FIRST_JOBS + before + PER_BODY * i, (FIRST_JOBS + before) % 2

    with ExitStack() as ctx:
        def sb(name, shape, dt=F32):
            return ctx.enter_context(nc.sbuf_tensor(f"g{g}_{name}", shape, dt))

        def ps(name, shape):
            return ctx.enter_context(nc.psum_tensor(f"g{g}_{name}", shape, F32))

        def sem(name):
            return nc.alloc_semaphore(f"g{g}_{name}")

        w_raw = [sb(f"w_raw{b}", [P, KW]) for b in range(2)]
        w_hi = sb("w_hi", [P, KT, KW], F32R)
        w_lo = sb("w_lo", [P, KT, KW], F32R)
        gains = sb("gains", [P, 2, KT])
        tok = [sb(f"tok{b}", [P, D]) for b in range(2)]
        ht_hi = [sb(f"ht_hi{b}", [P, KT, P], F32R) for b in range(2)]
        ht_lo = [sb(f"ht_lo{b}", [P, KT, P], F32R) for b in range(2)]
        trig = [sb(f"trig{b}", [P, 3, HD // 2]) for b in range(2)]
        rot_a = sb("rot_a", [P, 3, BANK])
        rot_b = sb("rot_b", [P, 3, BANK])
        raw = [w_raw[0][:], w_raw[1][:], *(x[:].rearrange("p b n -> p (b n)") for x in (rot_a, rot_b))]
        RAW = len(raw)
        q_rot = [sb(f"q_rot{n}", [P, BANK]) for n in range(KVH)]
        kv_rows = [sb(f"kv_rows{b}", [P, 2 * KVW]) for b in range(2)]
        qt_hi = [sb(f"qt_hi{n}", [P, BANK], F32R) for n in range(KVH)]
        qt_lo = [sb(f"qt_lo{n}", [P, BANK], F32R) for n in range(KVH)]
        kt_hi = sb("kt_hi", [P, KVH, 2 * P], F32R)
        kt_lo = sb("kt_lo", [P, KVH, 2 * P], F32R)
        v_hi = [sb(f"v_hi{b}", [P, KVW], F32R) for b in range(2)]
        v_lo = [sb(f"v_lo{b}", [P, KVW], F32R) for b in range(2)]
        probs = sb("probs", [P, QPK, 2 * P])
        pt_hi = sb("pt_hi", [P, 2 * BANK], F32R)
        pt_lo = sb("pt_lo", [P, 2 * BANK], F32R)
        sum_t = [sb(f"sum_t{n}", [P, BANK]) for n in range(KVH)]
        minus_max = sb("minus_max", [P, QPK])
        part = [sb(f"part{b}", [P, OMW]) for b in range(2)]
        mask_f = sb("mask_f", [P, 3, P])
        mask = sb("mask", [P, (3 + 2 * BODIES) * P], BF16)
        ident = sb("ident", [P, P])
        ident_b = sb("ident_b", [P, P], BF16)

        proj = ps("proj", [P, 3, BANK])
        score = ps("score", [P, QPK, 2 * P])
        tps = [ps(f"tps{b}", [P, BANK]) for b in range(2)]
        out_ps = ps("out", [P, BANK])

        s_gains = sem("gains_landed")
        s_ident = sem("ident_ready")
        s_mask = sem("mask_ready")
        s_wraw = [sem(f"w_landed{b}") for b in range(RAW)]
        s_whi = sem("w_hi_ready")
        s_wlo = sem("w_lo_ready")
        s_tok = [sem(f"tok_landed{b}") for b in range(2)]
        s_trig = [sem(f"trig_landed{b}") for b in range(2)]
        s_tr = sem("transposed")
        s_tr_hi = sem("transposed_hi")
        s_tr_free = sem("transpose_evacuated")
        s_proj = sem("projected")
        s_rope = sem("rope_products")
        s_rot = sem("rotated")
        s_v = sem("v_copied")
        s_vhi = sem("v_hi_ready")
        s_vlo = sem("v_lo_ready")
        s_score = sem("scores_ready")
        s_max = sem("max_ready")
        s_bias = sem("bias_ready")
        s_exp = sem("exps_ready")
        s_pv = sem("pv_ready")
        s_sum_t = sem("sums_t_copied")
        s_kvstore = [sem(f"kv_stored{b}") for b in range(2)]
        s_partstore = [sem(f"partial_stored{b}") for b in range(2)]
        s_sstore = sem("sample_stored")

        SAMPLE_STORES = 16 * (1 + HEADS + KVH)
        kv_view = w_kv.rearrange("(k p) (j g n) -> p k j g n", p=P, j=2, g=GROUPS)
        q_view = w_q.rearrange("(k p) n -> p k n", p=P)
        block = ctx.enter_context(nc.Block())

        def rows(i, u):
            i, u = i + u // UN, u % UN
            return bass.ds(ROW_I * i + ROW_U * u, P, step=STEP)


        @block.sync
        def _(sp):
            def load_tokens(i, u):
                b = (u + 1) % 2
                sp.dma_start(tok[b][:], hn_rows[rows(i, u), :]).then_inc(s_tok[b], 16)

            def load_trig(i, u):
                b = (u + 1) % 2
                sp.dma_start(trig[b][:], rope_rows[rows(i, u), :].rearrange("t (c n) -> t c n", c=3))\
                  .then_inc(s_trig[b], 16)

            def step(i, u, last=False):
                a = UN * i + u
                if not last or u < 2:
                    sp.wait_ge(s_gains, 32)
                    sp.wait_ge(s_rope, 3 * a + 6)
                    load_trig(i, u + 2)
                b = (u + 1) % 2
                if g == 2 or (g == 1 and u == UN - 1) or (g == 0 and last and u == UN - 1):
                    sp.wait_ge(s_v, a + 2)
                    sp.wait_ge(s_gains, 32)
                    sp.wait_ge(s_rot, 3 * (a + 1) + 1)
                    dst = {0: cache_out, 1: cache_out[bass.ds(i, P, step=STEP), :] if g == 1 else None,
                           2: cache_out[rows(i, u), :] if g == 2 else None}[g]
                    sp.dma_start(dst, kv_rows[b][:]).then_inc(s_kvstore[b], 16)
                if not last:
                    sp.wait_ge(s_gains, 32)
                    sp.wait_ge(s_tr, job(i, u, "h1", last)[0] + 1)
                    load_tokens(i, u + 4)
                sp.wait_ge(s_gains, 32)
                sp.wait_ge(s_tr_free, job(i, u, "o1", last)[0] + 1)
                sp.dma_start(partial[rows(i, u), :], part[u % 2][:]).then_inc(s_partstore[u % 2], 16)

            sp.dma_start(tok[0][0:NS, :], hn_rows[SEQ:TOK, :]).then_inc(s_tok[0], 16)
            sp.dma_start(gains[:, 0, :], kv_gain.rearrange("(k p) -> p k", p=P),
                         allow_slow_non_contiguous=True).then_inc(s_gains, 16)
            sp.dma_start(gains[:, 1, :], q_gain.rearrange("(k p) -> p k", p=P),
                         allow_slow_non_contiguous=True).then_inc(s_gains, 16)
            for k in range(KT):
                if k >= RAW:
                    sp.wait_ge(s_wlo, k - RAW + 1)
                landed = s_wraw[k % RAW]
                sp.dma_start(raw[k % RAW][:, 0:2 * KVW].rearrange("p (j n) -> p j n", j=2),
                             kv_view[:, k, :, g, :]).then_inc(landed, 16)
                sp.dma_start(raw[k % RAW][:, 2 * KVW:KW], q_view[:, k, g * D:(g + 1) * D]).then_inc(landed, 16)
                if k == 1:
                    sp.dma_start(trig[0][0:NS], rope_rows[SEQ:SEQ + 1, :].rearrange("a (c n) -> a c n", c=3)
                                 .to_broadcast([NS, 3, HD // 2])).then_inc(s_trig[0], 16)
                    load_tokens(0, 0)
                    load_trig(0, 0)
            sp.wait_ge(s_tr, 2)
            load_tokens(0, 1)
            sp.wait_ge(s_rope, 3)
            load_trig(0, 1)
            sp.wait_ge(s_rot, 3)
            sp.wait_ge(s_v, 1)
            sp.dma_start(newest, kv_rows[0][0:NS, :]).then_inc(s_sstore, 16)
            for x in range(HEADS):
                sp.dma_start(new_rows.rearrange("(b x) (j d) -> b x j d", x=HEADS, j=2)[:, x],
                             kv_rows[0][0:NS, :].rearrange("b (j n d) -> b j n d", j=2, n=KVH)[:, :, x // QPK, :])\
                  .then_inc(s_sstore, 16)
            for n in range(KVH):
                sp.dma_start(q_sample[:, n * BANK:(n + 1) * BANK], q_rot[n][0:NS, :]).then_inc(s_sstore, 16)
            for u in (2, 3):
                sp.wait_ge(s_tr, 2 * u)
                load_tokens(0, u)
            with sp.Fori(0, BODIES - 1) as i:
                for u in range(UN):
                    step(i, u)
            for u in range(UN):
                step(BODIES - 1, u, last=True)
            for b in range(2):
                sp.wait_ge(s_partstore[b], 16 * TILES // 2)
            if g == 2:
                for b in range(2):
                    sp.wait_ge(s_kvstore[b], 16 * TILES // 2)
            else:
                sp.wait_ge(s_kvstore[0], 16 * (BODIES if g == 1 else 1))

        @block.tensor
        def _(pe):
            def bank_wait(number):
                if not isinstance(number, int) or number >= 2:
                    pe.wait_ge(s_tr_free, number - 1)

            def turn(number, bank, src, blocks, n=P):
                bank_wait(number)
                for x, first in enumerate(blocks):
                    t = nc.tensor.transpose(tps[bank][:, x * n:(x + 1) * n], src[0:n, first:first + P],
                                            ident[0:n, 0:n])
                t.then_inc(s_tr, 1)

            def turn_tokens(e, b, numbers, n=P, landed=1):
                pe.wait_ge(s_tok[b], 16 * landed)
                for half in range(2):
                    turn(*numbers[half], tok[b], [(4 * half + k) * P for k in range(4)], n)

            def product(e, b, bank, k, n=P):
                out, cols = proj[0:n, bank, :], BANK_COLS[bank]
                hi, lo = ht_hi[b][:, k, 0:n], ht_lo[b][:, k, 0:n]
                nc.tensor.matmul(out, hi, w_hi[:, k, cols], start=(k == 0), stop=False)
                nc.tensor.matmul(out, hi, w_lo[:, k, cols], start=False, stop=False)
                last = nc.tensor.matmul(out, lo, w_hi[:, k, cols], start=False, stop=(k == KT - 1))
                if k == KT - 1:
                    last.then_inc(s_proj, 1)

            def project(e, b, bank, k0, k1):
                if k0 == 0:
                    pe.wait_ge(s_rope, 3 * e - 2 + bank)
                for k in range(k0, k1):
                    product(e, b, bank, k)

            def scores(i, u, n, last):
                a = UN * i + u
                before = has_before(u)
                pe.wait_ge(s_tr_free, job(i, u, ("k", "q1")[n], last)[0] + 1)
                pe.wait_ge(s_exp, 8 * a + 4 * n)
                width = 2 * P if before else P
                cols = slice(0, 2 * P) if before else slice((u % 2) * P, (u % 2 + 1) * P)
                if g == 0 and u == 0:
                    m = mask[:, bass.ds((3 + 2 * i) * P, width)]
                elif before and u % 2:
                    m = mask[:, P:3 * P]
                else:
                    m = mask[:, 0:width]
                for h in range(QPK):
                    if h % 2 == 0:
                        nc.tensor.matmul(score[:, h:h + 2, cols], ident_b[:],
                                         m.unsqueeze(1).to_broadcast([P, 2, width]), start=True, stop=False,
                                         skip_group_check=True)
                    q, out = slice(h * P, (h + 1) * P), score[:, h, cols]
                    nc.tensor.matmul(out, qt_hi[n][:, q], kt_hi[:, n, cols], start=False, stop=False,
                                     skip_group_check=True)
                    nc.tensor.matmul(out, qt_hi[n][:, q], kt_lo[:, n, cols], start=False, stop=False,
                                     skip_group_check=True)
                    t = nc.tensor.matmul(out, qt_lo[n][:, q], kt_hi[:, n, cols], start=False,
                                         stop=True, skip_group_check=True)
                t.then_inc(s_score, 1)

            def turn_probs(i, u, n, last):
                pe.wait_ge(s_exp, 8 * (UN * i + u) + 4 * n + 4)
                src = probs[:].rearrange("p h k -> p (h k)")
                if has_before(u):
                    for x, name in enumerate("ab"):
                        turn(*job(i, u, f"p{n}{name}", last), src, [(4 * x + y) * P for y in range(4)])
                else:
                    turn(*job(i, u, f"p{n}a", last), src, [(2 * h + u % 2) * P for h in range(QPK)])

            def values(i, u, n, last):
                a = UN * i + u
                parities = (0, 1) if has_before(u) else (u % 2,)
                name = f"p{n}" + ("b" if has_before(u) else "a")
                pe.wait_ge(s_tr_free, job(i, u, name, last)[0] + 1)
                pe.wait_ge(s_vlo, a + 1)
                if not isinstance(a, int) or a > 0 or n > 0:
                    pe.wait_ge(s_sum_t, 2 * a + n)
                v = slice(n * HD, (n + 1) * HD)
                shape = dict(h=QPK, y=len(parities))
                hi, lo = (x[:, 0:len(parities) * BANK].rearrange("p (h y q) -> p y h q", **shape)
                          for x in (pt_hi, pt_lo))
                for y, par in enumerate(parities):
                    first, final = y == 0, y == len(parities) - 1
                    nc.tensor.matmul(out_ps[:], v_hi[par][:, v], hi[:, y], start=first, stop=False)
                    nc.tensor.matmul(out_ps[:], v_lo[par][:, v], hi[:, y], start=False, stop=False)
                    t = nc.tensor.matmul(out_ps[:], v_hi[par][:, v], lo[:, y], start=False, stop=final)
                t.then_inc(s_pv, 1)

            def turn_sums(i, u, n, last):
                pe.wait_ge(s_sum_t, 2 * (UN * i + u) + n + 1)
                turn(*job(i, u, f"o{n}", last), sum_t[n], [h * P for h in range(QPK)])

            def step(i, u, last=False):
                a, b = UN * i + u, (u + 1) % 2
                e, eb = a + 2, u % 2
                more = not last or u < UN - 1
                pe.wait_ge(s_rot, 3 * (a + 1) + 2)
                turn(*job(i, u, "q0", last), q_rot[0], [h * P for h in range(QPK)])
                turn(*job(i, u, "k", last), kv_rows[b], [n * P for n in range(KVH)])
                if more:
                    project(e, eb, 0, 0, KT)
                scores(i, u, 0, last)
                pe.wait_ge(s_rot, 3 * (a + 1) + 3)
                turn(*job(i, u, "q1", last), q_rot[1], [h * P for h in range(QPK)])
                if more:
                    project(e, eb, 1, 0, 4)
                if "h0" in names(u, last):
                    turn_tokens(a + 3, b, [job(i, u, "h0", last), job(i, u, "h1", last)],
                                landed=2 * i + (u + 3) // 2 + 1)
                scores(i, u, 1, last)
                turn_probs(i, u, 0, last)
                if more:
                    project(e, eb, 1, 4, KT)
                    project(e, eb, 2, 0, 1)
                values(i, u, 0, last)
                turn_probs(i, u, 1, last)
                if more:
                    project(e, eb, 2, 1, 5)
                values(i, u, 1, last)
                turn_sums(i, u, 0, last)
                if more:
                    project(e, eb, 2, 5, KT)
                turn_sums(i, u, 1, last)

            pe.wait_ge(s_ident, 2)
            turn_tokens(0, 0, [(0, 0), (1, 1)], NS)
            turn_tokens(1, 1, [(2, 0), (3, 1)])
            for k in range(KT):
                pe.wait_ge(s_wlo, k + 1)
                for bank in range(3):
                    product(0, 0, bank, k, NS)
            turn_tokens(2, 0, [(4, 0), (5, 1)], landed=2)
            for bank in range(3):
                project(1, 1, bank, 0, KT)
            pe.wait_ge(s_mask, 4)
            with pe.Fori(0, BODIES - 1) as i:
                for u in range(UN):
                    step(i, u)
            for u in range(UN):
                step(BODIES - 1, u, last=True)

        def evacuations(i, u, last):
            b = (u + 1) % 2
            par = slice((u % 2) * P, (u % 2 + 1) * P)
            to = {"q0": (BANK, qt_hi[0][:], qt_lo[0][:]), "q1": (BANK, qt_hi[1][:], qt_lo[1][:]),
                  "k": (KVW, kt_hi[:, :, par], kt_lo[:, :, par])}
            for half in range(2):
                k = slice(4 * half, 4 * half + 4)
                to[f"h{half}"] = (BANK, ht_hi[b][:, k, :], ht_lo[b][:, k, :])
            for n in range(KVH):
                for x, name in enumerate("ab"):
                    cols = slice(x * BANK, (x + 1) * BANK)
                    to[f"p{n}{name}"] = (BANK, pt_hi[:, cols], pt_lo[:, cols])
                to[f"o{n}"] = (BANK, part[u % 2][:, n * BANK:n * BANK + BANK // 2],
                               part[u % 2][:, n * BANK + BANK // 2:(n + 1) * BANK])
            return {name: (job(i, u, name, last), *to[name]) for name in names(u, last)}

        def bank_view(bank, width, like):
            src = tps[bank][:, 0:width]
            return src.rearrange("p (a b) -> p a b", a=like.shape[1]) if len(like.shape) == 3 else src

        @block.scalar
        def _(act):
            def high(number, bank, width, hi, lo):
                act.wait_ge(s_tr, number + 1)
                nc.scalar.activation(hi, bank_view(bank, width, hi), ACT.Copy).then_inc(s_tr_hi, 1)

            def sums_left(ev, name):
                (number, bank), _width, left, _right = ev[name]
                act.wait_ge(s_tr, number + 1)
                nc.scalar.activation(left, tps[bank][:, 0:BANK // 2], ACT.Copy).then_inc(s_tr_hi, 1)

            def copy_v(e, b, n=P):
                act.wait_ge(s_proj, 3 * e + 1)
                if not isinstance(e, int) or e >= 2:
                    act.wait_ge(s_vlo, e - 2)
                nc.scalar.activation(kv_rows[b][0:n, KVW:2 * KVW], proj[0:n, 0, KVW:2 * KVW],
                                     ACT.Copy).then_inc(s_v, 1)

            def exponentials(i, u, n):
                a = UN * i + u
                act.wait_ge(s_bias, 2 * a + n + 1)
                cols = slice(0, 2 * P) if has_before(u) else slice((u % 2) * P, (u % 2 + 1) * P)
                for h in range(QPK):
                    x = QPK * n + h
                    nc.scalar.activation(probs[:, h, cols], score[:, h, cols], ACT.Exp,
                                         bias=part[u % 2][:, D + x:D + x + 1], scale=SCALE,
                                         accum_out=part[u % 2][:, D + HEADS + x:D + HEADS + x + 1])\
                      .then_inc(s_exp, 1)

            def copy_sums(i, u, n):
                act.wait_ge(s_pv, 2 * (UN * i + u) + n + 1)
                nc.scalar.activation(sum_t[n][:], out_ps[:], ACT.Copy).then_inc(s_sum_t, 1)

            def step(i, u, last=False):
                a, b, ev = UN * i + u, (u + 1) % 2, evacuations(i, u, last)
                split = lambda name: name in ev and high(*ev[name][0], *ev[name][1:])
                split("q0")
                split("k")
                act.wait_ge(s_v, a + 2)
                nc.scalar.activation(v_hi[u % 2][:], kv_rows[b][:, KVW:2 * KVW], ACT.Copy).then_inc(s_vhi, 1)
                if not last or u < UN - 1:
                    if g == 2 or (g == 1 and u == 0):
                        act.wait_ge(s_kvstore[u % 2], 16 * (2 * i + (u + 1) // 2 if g == 2 else i))
                    copy_v(a + 2, u % 2)
                split("q1")
                exponentials(i, u, 0)
                for name in ("h0", "h1", "p0a", "p0b"):
                    split(name)
                exponentials(i, u, 1)
                copy_sums(i, u, 0)
                split("p1a")
                split("p1b")
                copy_sums(i, u, 1)
                sums_left(ev, "o0")
                sums_left(ev, "o1")

            def tokens_high(e, numbers, n=P):
                for half, number in enumerate(numbers):
                    k = slice(4 * half, 4 * half + 4)
                    high(number, half, 4 * n, ht_hi[e % 2][:, k, 0:n], None)

            tokens_high(0, (0, 1), NS)
            tokens_high(1, (2, 3))
            act.wait_ge(s_gains, 32)
            for k in range(KT):
                act.wait_ge(s_wraw[k % RAW], 32 * (k // RAW + 1))
                for x, cols in enumerate((slice(0, 2 * KVW), slice(2 * KVW, KW))):
                    nc.scalar.activation(w_hi[:, k, cols], raw[k % RAW][:, cols], ACT.Copy,
                                         scale=gains[:, x, k:k + 1]).then_inc(s_whi, 1)
            copy_v(0, 0, NS)
            tokens_high(2, (4, 5))
            copy_v(1, 1)
            act.wait_ge(s_sstore, SAMPLE_STORES)
            with act.Fori(0, BODIES - 1) as i:
                for u in range(UN):
                    step(i, u)
            for u in range(UN):
                step(BODIES - 1, u, last=True)

        @block.vector
        def _(dve):
            def low(number, bank, width, hi, lo):
                dve.wait_ge(s_tr_hi, number + 1)
                nc.vector.tensor_tensor(lo, bank_view(bank, width, hi), hi.bitcast(F32),
                                        ALU.subtract).then_inc(s_tr_free, 1)

            def sums_right(ev, name):
                (number, bank), _width, _left, right = ev[name]
                dve.wait_ge(s_tr_hi, number + 1)
                nc.vector.tensor_copy(right, tps[bank][:, BANK // 2:BANK]).then_inc(s_tr_free, 1)

            def rope(e, b, bank, landed, n=P):
                heads = KVH if bank == 0 else QPK
                dve.wait_ge(s_proj, 3 * e + bank + 1)
                if bank == 0:
                    dve.wait_ge(s_v, e + 1)
                dve.wait_ge(s_trig[b], 16 * landed)
                if isinstance(e, int) and e == 0:
                    dve.wait_ge(s_wlo, KT)
                else:
                    dve.wait_ge(s_rot, 3 * e + bank - 2)
                src = proj[0:n, bank, 0:heads * HD].rearrange("p (h c x) -> p h c x", h=heads, c=2)
                a, c = (x[0:n, bank, 0:heads * HD].rearrange("p (h c x) -> p h c x", h=heads, c=2)
                        for x in (rot_a, rot_b))
                shape = [n, heads, 2, HD // 2]
                nc.vector.tensor_tensor(a, src, trig[b][0:n, 0:1, :].unsqueeze(1).to_broadcast(shape), ALU.mult)
                nc.vector.tensor_tensor(c, src[:, :, ::-1, :],
                                        trig[b][0:n, 1:3, :].unsqueeze(1).to_broadcast(shape),
                                        ALU.mult).then_inc(s_rope, 1)

            def maxima(i, u, n):
                a = UN * i + u
                cols = slice(0, 2 * P) if has_before(u) else slice((u % 2) * P, (u % 2 + 1) * P)
                dve.wait_ge(s_score, 2 * a + n + 1)
                nc.vector.tensor_reduce(minus_max[:], score[:, :, cols], AX_X, ALU.max, negate=True)\
                  .then_inc(s_max, 1)
                dve.wait_ge(s_partstore[u % 2], 16 * (2 * i + u // 2))
                dve.wait_ge(s_max, 2 * a + n + 1)
                nc.vector.tensor_scalar(part[u % 2][:, D + QPK * n:D + QPK * (n + 1)], minus_max[:], SCALE, None,
                                        ALU.mult).then_inc(s_bias, 1)

            def step(i, u, last=False):
                a, ev = UN * i + u, evacuations(i, u, last)
                split = lambda name: name in ev and low(*ev[name][0], *ev[name][1:])
                more, landed = not last or u < UN - 1, 2 * i + (u + 2) // 2 + 1
                split("q0")
                split("k")
                maxima(i, u, 0)
                if more:
                    rope(a + 2, u % 2, 0, landed)
                for name in ("q1", "h0", "h1"):
                    split(name)
                maxima(i, u, 1)
                split("p0a")
                split("p0b")
                if more:
                    rope(a + 2, u % 2, 1, landed)
                split("p1a")
                split("p1b")
                sums_right(ev, "o0")
                if more:
                    rope(a + 2, u % 2, 2, landed)
                sums_right(ev, "o1")

            def tokens_low(e, numbers, n=P):
                for half, number in enumerate(numbers):
                    k = slice(4 * half, 4 * half + 4)
                    low(number, half, 4 * n, ht_hi[e % 2][:, k, 0:n], ht_lo[e % 2][:, k, 0:n])

            tokens_low(0, (0, 1), NS)
            tokens_low(1, (2, 3))
            for k in range(KT):
                for x, cols in enumerate((slice(0, 2 * KVW), slice(2 * KVW, KW))):
                    dve.wait_ge(s_whi, 2 * k + x + 1)
                    t = nc.vector.scalar_tensor_tensor(out=w_lo[:, k, cols], in0=raw[k % RAW][:, cols],
                                                       scalar=gains[:, x, k:k + 1],
                                                       in1=w_hi[:, k, cols].bitcast(F32),
                                                       op0=ALU.mult, op1=ALU.subtract)
                t.then_inc(s_wlo, 1)
            for bank in range(3):
                rope(0, 0, bank, 1, NS)
            tokens_low(2, (4, 5))
            for bank in range(3):
                rope(1, 1, bank, 1)
            with dve.Fori(0, BODIES - 1) as i:
                for u in range(UN):
                    step(i, u)
            for u in range(UN):
                step(BODIES - 1, u, last=True)

        @block.gpsimd
        def _(pool):
            def rotated(e, b, bank, n=P):
                heads = KVH if bank == 0 else QPK
                dst = kv_rows[b] if bank == 0 else q_rot[bank - 1]
                pool.wait_ge(s_rope, 3 * e + bank + 1)
                nc.gpsimd.tensor_tensor(dst[0:n, 0:heads * HD], rot_a[0:n, bank, 0:heads * HD],
                                        rot_b[0:n, bank, 0:heads * HD], ALU.add).then_inc(s_rot, 1)

            def step(i, u, last=False):
                a, b = UN * i + u, (u + 1) % 2
                pool.wait_ge(s_vhi, a + 1)
                nc.gpsimd.tensor_tensor(v_lo[u % 2][:], kv_rows[b][:, KVW:2 * KVW], v_hi[u % 2][:].bitcast(F32),
                                        ALU.subtract).then_inc(s_vlo, 1)
                if last and u == UN - 1:
                    return
                if g == 2 or (g == 1 and u == 0):
                    pool.wait_ge(s_kvstore[u % 2], 16 * (2 * i + (u + 1) // 2 if g == 2 else i))
                for bank in range(3):
                    rotated(a + 2, u % 2, bank)

            nc.gpsimd.memset(ident[:], 0.0).then_inc(s_ident, 1)
            pool.wait_ge(s_ident, 1)
            nc.gpsimd.affine_select(out=ident[:], in_=ident[:], compare_op=ALU.not_equal, fill=1.0, base=0,
                                    pattern=[[-1, P]], channel_multiplier=1).then_inc(s_ident, 1)
            nc.gpsimd.memset(mask_f[:, 0:2, :], 0.0)
            nc.gpsimd.memset(mask_f[:, 2, :], MASKED).then_inc(s_mask, 1)
            pool.wait_ge(s_mask, 1)
            nc.gpsimd.affine_select(out=mask_f[:, 0, :], in_=mask_f[:, 0, :], compare_op=ALU.is_ge, fill=MASKED,
                                    base=0, pattern=[[-1, P]], channel_multiplier=1).then_inc(s_mask, 1)
            nc.gpsimd.affine_select(out=mask_f[:, 1, :], in_=mask_f[:, 1, :], compare_op=ALU.is_ge, fill=MASKED,
                                    base=0, pattern=[[1, P]], channel_multiplier=-1).then_inc(s_mask, 1)
            if g == 0:
                for zero in (kt_hi[:, :, P:2 * P], kt_lo[:, :, P:2 * P], v_hi[1][:], v_lo[1][:]):
                    nc.gpsimd.memset(zero.bitcast(F32), 0.0)
            pool.wait_ge(s_ident, 2)
            pool.wait_ge(s_mask, 3)
            nc.gpsimd.tensor_copy(ident_b[:], ident[:])
            for x, kind in enumerate([0, 1, 0] + [0, 2] + [0, 1] * (BODIES - 1)):
                t = nc.gpsimd.tensor_copy(mask[:, x * P:(x + 1) * P], mask_f[:, kind, :])
            t.then_inc(s_mask, 1)
            for bank in range(3):
                rotated(0, 0, bank, NS)
            pool.wait_ge(s_sstore, SAMPLE_STORES)
            for bank in range(3):
                rotated(1, 1, bank)
            with pool.Fori(0, BODIES - 1) as i:
                for u in range(UN):
                    step(i, u)
            for u in range(UN):
                step(BODIES - 1, u, last=True)


def sample_attention_phase(nc, q_sample, new_rows, caches, o_sample):
    R = NS * HEADS
    KEYS = P

    with ExitStack() as ctx:
        def sb(name, shape, dt=F32):
            return ctx.enter_context(nc.sbuf_tensor(f"s_{name}", shape, dt))

        def ps(name, shape):
            return ctx.enter_context(nc.psum_tensor(f"s_{name}", shape, F32))

        def sem(name):
            return nc.alloc_semaphore(f"s_{name}")

        each = range(GROUPS)
        cache = [sb(f"cache{c}", [P, NS // 2, 2 * KVW]) for c in range(2 * GROUPS)]
        q_rows = sb("q_rows", [R, GROUPS, HD])
        new = sb("new", [R, GROUPS, 2, HD])
        qt = [sb(f"qt{g}", [P, R]) for g in each]
        keys_t = [sb(f"keys_t{b}", [P, 4, P]) for b in range(2)]
        score_t = [sb(f"score_t{g}", [P, R]) for g in each]
        score = [sb(f"score{g}", [R, KEYS + 1]) for g in each]
        prob = [sb(f"prob{g}", [R, KEYS + 1]) for g in each]
        prob_t = [sb(f"prob_t{g}", [P, R]) for g in each]
        sum_t = [sb(f"sum_t{g}", [P, R]) for g in each]
        product = sb("product", [R, HD])
        sums = sb("sums", [R, GROUPS, HD])
        stat = sb("stat", [R, 4, GROUPS])
        small = sb("small", [R, 4])
        merged = sb("merged", [R, HD])
        ident = sb("ident", [P, P])

        tps = [ps(f"tps{b}", [P, 4, P]) for b in range(2)]
        one = [ps(f"one{b}", [P, BANK]) for b in range(2)]
        st_ps = [ps(f"scores_t{b}", [P, BANK]) for b in range(2)]
        ot_ps = [ps(f"sums_t{b}", [P, BANK]) for b in range(2)]

        s_ident = sem("ident_ready")
        s_q = sem("queries_landed")
        s_new_rows = sem("new_rows_landed")
        s_cache = [sem(f"cache_landed{c}") for c in range(2 * GROUPS)]
        s_keys = sem("keys_turned")
        s_keys_sb = sem("keys_copied")
        s_one = sem("single_turned")
        s_one_sb = sem("single_copied")
        s_st = sem("scores_t_ready")
        s_st_sb = sem("scores_t_copied")
        s_new = sem("new_score")
        s_bias = sem("bias_steps")
        s_exp = sem("exps_ready")
        s_ot = sem("sums_t_ready")
        s_ot_sb = sem("sums_t_copied")
        s_w = sem("weights_ready")
        s_step = sem("merge_steps")
        s_out = sem("stored")

        block = ctx.enter_context(nc.Block())

        SINGLES = [("q", 0), ("q", 1), ("q", 2), ("score", 0), ("score", 1), ("prob", 0),
                   ("score", 2), ("prob", 1), ("sum", 0), ("prob", 2), ("sum", 1), ("sum", 2)]

        def bank(kind, g):
            return one[SINGLES.index((kind, g)) % 2]

        def done(kind, g):
            return SINGLES.index((kind, g)) + 1

        @block.sync
        def _(sp):
            for g in each:
                sp.dma_start(q_rows[:, g, :], q_sample[g].rearrange("b (x d) -> (b x) d", d=HD)).then_inc(s_q, 16)
            for g in each:
                cached = caches[g].rearrange("b (k d) c -> k d b c", d=DILATIONS[g])[:, 0, :, :]
                for half in range(2):
                    sp.dma_start(cache[2 * g + half][:], cached[:, half * 4:half * 4 + 4, :])\
                      .then_inc(s_cache[2 * g + half], 16)
                if g == 0:
                    for x in each:
                        sp.dma_start(new[:, x, :, :], new_rows[x].rearrange("r (j d) -> r j d", j=2))\
                          .then_inc(s_new_rows, 16)
            sp.wait_ge(s_step, 10)
            sp.dma_start(o_sample.rearrange("b (x d) -> (b x) d", d=HD), merged[:]).then_inc(s_out, 16)
            sp.wait_ge(s_out, 16)

        @block.gpsimd
        def _(pool):
            nc.gpsimd.memset(ident[:], 0.0).then_inc(s_ident, 1)
            pool.wait_ge(s_ident, 1)
            nc.gpsimd.affine_select(out=ident[:], in_=ident[:], compare_op=ALU.not_equal, fill=1.0, base=0,
                                    pattern=[[-1, P]], channel_multiplier=1).then_inc(s_ident, 1)

        @block.tensor
        def _(pe):
            def single(kind, g, src, rows):
                n = SINGLES.index((kind, g))
                if n >= 2:
                    pe.wait_ge(s_one_sb, n - 1)
                nc.tensor.transpose(one[n % 2][0:src.shape[1], 0:rows], src, ident[0:rows, 0:rows]).then_inc(s_one, 1)

            def turn_keys(g, quad):
                n, c = 4 * g + quad, 2 * g + quad // 2
                pe.wait_ge(s_cache[c], 16)
                if n >= 2:
                    pe.wait_ge(s_keys_sb, n - 1)
                for x in range(4):
                    t = nc.tensor.transpose(tps[n % 2][:, x, :],
                                            cache[c][:, 2 * (quad % 2) + x // 2, (x % 2) * HD:(x % 2 + 1) * HD],
                                            ident[:])
                t.then_inc(s_keys, 1)

            def scores(g):
                turn_keys(g, 0)
                for quad in range(4):
                    n = 4 * g + quad
                    if quad < 3:
                        turn_keys(g, quad + 1)
                    pe.wait_ge(s_keys_sb, n + 1)
                    if quad == 0:
                        pe.wait_ge(s_one_sb, done("q", g))
                        if g >= 2:
                            pe.wait_ge(s_st_sb, g - 1)
                    for x in range(4):
                        row = (4 * quad + x) * QPK
                        t = nc.tensor.matmul(st_ps[g % 2][:, row:row + QPK], keys_t[n % 2][:, x, :],
                                             qt[g][:, row:row + QPK], start=True, stop=True)
                t.then_inc(s_st, 1)

            def turn_scores(g):
                pe.wait_ge(s_st_sb, g + 1)
                single("score", g, score_t[g][:], P)

            def turn_probs(g):
                pe.wait_ge(s_exp, g + 1)
                single("prob", g, prob[g][:, 0:KEYS], R)

            def values(g):
                pe.wait_ge(s_one_sb, done("prob", g))
                if g >= 2:
                    pe.wait_ge(s_ot_sb, g - 1)
                for pair in range(NS * KVH):
                    seq, n = pair // KVH, pair % KVH
                    t = nc.tensor.matmul(ot_ps[g % 2][:, pair * QPK:(pair + 1) * QPK],
                                         cache[2 * g + seq // 4][:, seq % 4, KVW + n * HD:KVW + (n + 1) * HD],
                                         prob_t[g][:, pair * QPK:(pair + 1) * QPK], start=True, stop=True)
                t.then_inc(s_ot, 1)

            def turn_sums(g):
                pe.wait_ge(s_ot_sb, g + 1)
                single("sum", g, sum_t[g][:], P)

            pe.wait_ge(s_ident, 2)
            pe.wait_ge(s_q, 16 * GROUPS)
            for g in each:
                single("q", g, q_rows[:, g, :], R)
            scores(0)
            turn_scores(0)
            scores(1)
            turn_scores(1)
            turn_probs(0)
            values(0)
            scores(2)
            turn_scores(2)
            turn_probs(1)
            turn_sums(0)
            values(1)
            turn_probs(2)
            values(2)
            turn_sums(1)
            turn_sums(2)

        @block.scalar
        def _(act):
            def copy_single(kind, g, dst):
                act.wait_ge(s_one, done(kind, g))
                act.wait_ge(s_one_sb, done(kind, g) - 1)
                nc.scalar.activation(dst, bank(kind, g)[0:dst.shape[0], 0:dst.shape[1]], ACT.Copy)\
                  .then_inc(s_one_sb, 1)

            def keys(g):
                for quad in range(4):
                    n = 4 * g + quad
                    act.wait_ge(s_keys, n + 1)
                    nc.scalar.activation(keys_t[n % 2][:], tps[n % 2][:], ACT.Copy).then_inc(s_keys_sb, 1)
                act.wait_ge(s_st, g + 1)
                nc.scalar.activation(score_t[g][:], st_ps[g % 2][:, 0:R], ACT.Copy).then_inc(s_st_sb, 1)
                copy_single("score", g, score[g][:, 0:KEYS])

            def exponentials(g):
                act.wait_ge(s_bias, 2 * g + 2)
                nc.scalar.activation(prob[g][:], score[g][:], ACT.Exp, bias=stat[:, 0, g:g + 1], scale=SCALE,
                                     accum_out=stat[:, 1, g:g + 1]).then_inc(s_exp, 1)
                copy_single("prob", g, prob_t[g][:])

            def copy_sums(g):
                act.wait_ge(s_ot, g + 1)
                nc.scalar.activation(sum_t[g][:], ot_ps[g % 2][:, 0:R], ACT.Copy).then_inc(s_ot_sb, 1)

            for g in each:
                copy_single("q", g, qt[g][:])
            keys(0)
            keys(1)
            exponentials(0)
            copy_sums(0)
            keys(2)
            exponentials(1)
            copy_sums(1)
            exponentials(2)
            copy_sums(2)
            act.wait_ge(s_step, 3)
            nc.scalar.activation(stat[:, 2, :], stat[:, 3, :], ACT.Exp).then_inc(s_w, 1)

        @block.vector
        def _(dve):
            def new_score(g):
                if g > 0:
                    dve.wait_ge(s_new, g)
                nc.vector.tensor_tensor_reduce(out=product[:], in0=q_rows[:, g, :], in1=new[:, g, 0, :],
                                               scale=1.0, scalar=0.0, op0=ALU.mult, op1=ALU.add,
                                               accum_out=score[g][:, KEYS:KEYS + 1]).then_inc(s_new, 1)

            def maximum(g):
                dve.wait_ge(s_new, g + 1)
                dve.wait_ge(s_one_sb, done("score", g))
                if g > 0:
                    dve.wait_ge(s_bias, 2 * g)
                nc.vector.tensor_reduce(small[:, 0:1], score[g][:], AX_X, ALU.max, negate=True).then_inc(s_bias, 1)
                dve.wait_ge(s_bias, 2 * g + 1)
                nc.vector.tensor_scalar(stat[:, 0, g:g + 1], small[:, 0:1], SCALE, None, ALU.mult).then_inc(s_bias, 1)

            def add_new_value(g):
                dve.wait_ge(s_exp, g + 1)
                dve.wait_ge(s_one, done("sum", g))
                dve.wait_ge(s_one_sb, done("sum", g) - 1)
                nc.vector.scalar_tensor_tensor(out=sums[:, g, :], in0=new[:, g, 1, :],
                                               scalar=prob[g][:, KEYS:KEYS + 1],
                                               in1=bank("sum", g)[0:R, 0:HD],
                                               op0=ALU.mult, op1=ALU.add).then_inc(s_one_sb, 1)

            dve.wait_ge(s_q, 16 * GROUPS)
            dve.wait_ge(s_new_rows, 16 * GROUPS)
            for g in each:
                new_score(g)
            maximum(0)
            maximum(1)
            maximum(2)
            add_new_value(0)
            least, total, inverse = small[:, 1:2], small[:, 2:3], small[:, 3:4]
            dve.wait_ge(s_bias, 2 * GROUPS)
            nc.vector.tensor_reduce(least, stat[:, 0, :], AX_X, ALU.min).then_inc(s_step, 1)
            dve.wait_ge(s_step, 1)
            nc.vector.tensor_scalar(stat[:, 3, :], stat[:, 0, :], least, None, ALU.subtract).then_inc(s_step, 1)
            dve.wait_ge(s_step, 2)
            nc.vector.tensor_scalar(stat[:, 3, :], stat[:, 3, :], -1.0, None, ALU.mult).then_inc(s_step, 1)
            add_new_value(1)
            add_new_value(2)
            dve.wait_ge(s_w, 1)
            nc.vector.tensor_tensor(stat[:, 3, :], stat[:, 2, :], stat[:, 1, :], ALU.mult).then_inc(s_step, 1)
            dve.wait_ge(s_step, 4)
            nc.vector.tensor_reduce(total, stat[:, 3, :], AX_X, ALU.add).then_inc(s_step, 1)
            dve.wait_ge(s_step, 5)
            nc.vector.reciprocal(inverse, total).then_inc(s_step, 1)
            dve.wait_ge(s_step, 6)
            nc.vector.tensor_scalar(stat[:, 3, :], stat[:, 2, :], inverse, None, ALU.mult).then_inc(s_step, 1)
            dve.wait_ge(s_one_sb, len(SINGLES))
            dve.wait_ge(s_step, 7)
            nc.vector.tensor_scalar(merged[:], sums[:, 0, :], stat[:, 3, 0:1], None, ALU.mult).then_inc(s_step, 1)
            for g in (1, 2):
                dve.wait_ge(s_step, 7 + g)
                nc.vector.scalar_tensor_tensor(out=merged[:], in0=sums[:, g, :], scalar=stat[:, 3, g:g + 1],
                                               in1=merged[:], op0=ALU.mult, op1=ALU.add).then_inc(s_step, 1)


def attention_output_phase(nc, hn_rows, h_rows, partials, o_sample, w_z, w_out, pre_gain, norm_post,
                           y_prompt, y_sample):
    UN = 2
    BODIES = (NT - 3) // UN
    TAIL = range(UN * BODIES + 1, NT + 1)

    with ExitStack() as ctx:
        def sb(name, shape, dt=F32):
            return ctx.enter_context(nc.sbuf_tensor(f"d_{name}", shape, dt))

        def ps(name, shape):
            return ctx.enter_context(nc.psum_tensor(f"d_{name}", shape, F32))

        def sem(name):
            return nc.alloc_semaphore(f"d_{name}")

        w_hi = sb("w_hi", [P, 2, KT, D], F32R)
        w_lo = sb("w_lo", [P, 2, KT, D], F32R)
        tok = [sb(f"tok{b}", [P, D]) for b in range(2)]
        ht_hi = sb("ht_hi", [P, KT, P], F32R)
        ht_lo = sb("ht_lo", [P, KT, P], F32R)
        gt_hi = sb("gt_hi", [P, KT, P], F32R)
        gt_lo = sb("gt_lo", [P, KT, P], F32R)
        part = [sb(f"part{b}", [P, GROUPS, OMW]) for b in range(2)]
        silu_z = sb("silu_z", [P, D])
        normed = sb("normed", [P, D])
        h_buf = [sb(f"h{b}", [P, D]) for b in range(2)]
        w_raw = [*(sb(f"w_raw{b}", [P, D]) for b in range(2)), normed, h_buf[1]]
        RAW = len(w_raw)
        post_gain = sb("post_gain", [P, D])
        gains = sb("gains", [P, KT])
        coef = sb("coef", [P, 3, GROUPS, HEADS])
        small = sb("small", [P, 3, HEADS])
        eps = sb("eps", [P, 1])
        stat = sb("stat", [P, 3])
        scratch = sb("scratch", [P, 3])
        ident = sb("ident", [P, P])

        z_ps = ps("z", [P, D])
        out_ps = ps("out", [P, D])
        square = ps("square", [P, D])
        tps = [ps(f"tps{b}", [P, BANK]) for b in range(2)]

        s_const = sem("gains_landed")
        s_ident = sem("ident_ready")
        s_eps = sem("eps_ready")
        s_wraw = [sem(f"w_landed{b}") for b in range(RAW)]
        s_whi = sem("w_hi_ready")
        s_wlo = sem("w_lo_ready")
        s_tok = [sem(f"tok_landed{b}") for b in range(2)]
        s_h = [sem(f"h_landed{b}") for b in range(2)]
        s_p = [sem(f"partials_landed{b}") for b in range(2)]
        s_tr = sem("transposed")
        s_tr_hi = sem("transposed_hi")
        s_tr_free = sem("transpose_evacuated")
        s_z = sem("z_ready")
        s_silu = sem("silu_ready")
        s_diff = sem("merge_steps")
        s_exp = sem("weights_ready")
        s_mul = sem("weighted")
        s_mul2 = sem("weighted_last")
        s_gated = sem("gated_ready")
        s_out = sem("product_ready")
        s_square = sem("squares")
        s_root = sem("roots")
        s_rstd = sem("rstd_steps")
        s_normed = sem("normed_ready")
        s_y = sem("y_ready")
        s_ystore = [sem(f"y_stored{b}") for b in range(2)]

        block = ctx.enter_context(nc.Block())

        def tile(i, u, k=0):
            return 2 * i + 1 + u + k, (1 + u + k) % 2, i + (1 + u + k) // 2

        def height(t):
            return NS if isinstance(t, int) and t == NT else P

        def above(value, bound):
            return not isinstance(value, int) or value >= bound

        def token_job(t):
            return 0 if isinstance(t, int) and t == 0 else 4 * t - 2

        def gated_job(t):
            return 4 * t + 2 if isinstance(t, int) and t == NT else 4 * t + 4

        def run_steps(engine, step):
            step(0, -1)
            with engine.Fori(0, BODIES) as i:
                for u in range(UN):
                    step(i, u)
            for t in TAIL:
                step(0, t - 1)

        @block.sync
        def _(sp):
            def load_tokens(t, b):
                n = height(t)
                sp.dma_start(tok[b][0:n, :], hn_rows[bass.ds(t * P, n), :]).then_inc(s_tok[b], 16)

            def load_parts(t, b):
                if height(t) == NS:
                    sp.dma_start(part[b][0:NS, 0, 0:D], o_sample).then_inc(s_p[b], 16)
                    return
                for g in range(GROUPS):
                    sp.dma_start(part[b][:, g, :], partials[g][bass.ds(t * P, P), :]).then_inc(s_p[b], 16)

            def step(i, u):
                t, b, m = tile(i, u)
                if not isinstance(t, int) or t + 3 <= NT:
                    if above(t, 0):
                        sp.wait_ge(s_const, 16)
                        sp.wait_ge(s_tr, token_job(t + 1) + 2)
                    load_tokens(*tile(i, u, 3)[:2])
                n = height(t)
                if isinstance(t, int) and t == 0:
                    sp.wait_ge(s_wlo, 2 * KT)
                if above(t, 2):
                    sp.wait_ge(s_const, 16)
                    sp.wait_ge(s_ystore[b], 16 * m)
                sp.dma_start(h_buf[b][0:n, :], h_rows[bass.ds(t * P, n), :]).then_inc(s_h[b], 16)
                if not isinstance(t, int) or t + 2 <= NT:
                    sp.wait_ge(s_const, 16)
                    sp.wait_ge(s_tr, gated_job(t) + 2)
                    load_parts(t + 2, b)
                if above(t, 1):
                    store(*tile(i, u, -1)[:2])

            def store(t, b):
                n = height(t)
                sp.wait_ge(s_const, 16)
                sp.wait_ge(s_y, t + 1)
                dst = y_sample if n == NS else y_prompt[bass.ds(t * P, P), :]
                sp.dma_start(dst, h_buf[b][0:n, :]).then_inc(s_ystore[b], 16)

            load_tokens(0, 0)
            sp.dma_start(gains[:], pre_gain.rearrange("(k p) -> p k", p=P),
                         allow_slow_non_contiguous=True).then_inc(s_const, 16)
            for k in range(2 * KT):
                if k >= RAW:
                    sp.wait_ge(s_wlo, k - RAW + 1)
                src = (w_z, w_out)[k // KT].rearrange("(k p) n -> p k n", p=P)[:, k % KT, :]
                sp.dma_start(w_raw[k % RAW][:], src).then_inc(s_wraw[k % RAW], 16)
                if k == 2:
                    load_tokens(1, 1)
                    load_parts(0, 0)
                if k == KT:
                    load_parts(1, 1)
                    sp.wait_ge(s_tr, 2)
                    load_tokens(2, 0)
                    sp.dma_start(post_gain[:], norm_post.partition_broadcast(P)).then_inc(s_const, 16)
            run_steps(sp, step)
            store(NT, NT % 2)
            for b in range(2):
                sp.wait_ge(s_ystore[b], 16 * (NT // 2 + (b == 0)))

        @block.tensor
        def _(pe):
            def turn(number, bank, src, first, n):
                if above(number, 2):
                    pe.wait_ge(s_tr_free, number - 1)
                for x in range(4):
                    last = nc.tensor.transpose(tps[bank][:, x * n:(x + 1) * n],
                                               src[0:n, first + x * P:first + (x + 1) * P], ident[0:n, 0:n])
                last.then_inc(s_tr, 1)

            def turn_tokens(t, b, m):
                pe.wait_ge(s_tok[b], 16 * m + 16)
                for half in range(2):
                    turn(token_job(t) + half, half, tok[b], half * BANK, height(t))

            def turn_gated(t, b):
                pe.wait_ge(s_gated, t + 1)
                for half in range(2):
                    turn(gated_job(t) + half, half, part[b][:, 0, :], half * BANK, height(t))

            def product(dst, which, hi_t, lo_t, ks, n, weights=False):
                for k in ks:
                    if weights:
                        pe.wait_ge(s_wlo, which * KT + k + 1)
                    for c in range(D // BANK):
                        cols = slice(c * BANK, (c + 1) * BANK)
                        hi, lo = hi_t[:, k, 0:n], lo_t[:, k, 0:n]
                        nc.tensor.matmul(dst[0:n, cols], hi, w_hi[:, which, k, cols], start=(k == 0), stop=False)
                        nc.tensor.matmul(dst[0:n, cols], hi, w_lo[:, which, k, cols], start=False, stop=False)
                        last = nc.tensor.matmul(dst[0:n, cols], lo, w_hi[:, which, k, cols], start=False,
                                                stop=(k == KT - 1))
                return last

            def z_product(t):
                pe.wait_ge(s_tr_free, token_job(t) + 2)
                if above(t, 1):
                    pe.wait_ge(s_silu, t)
                product(z_ps, 0, ht_hi, ht_lo, range(KT), height(t),
                        weights=isinstance(t, int) and t == 0).then_inc(s_z, 1)

            def step(i, u):
                t, b, m = tile(i, u)
                turn_gated(t, b)
                if not isinstance(t, int) or t < NT:
                    z_product(t + 1)
                pe.wait_ge(s_tr_free, gated_job(t) + 2)
                if above(t, 1):
                    pe.wait_ge(s_normed, t)
                first = isinstance(t, int) and t == 0
                product(out_ps, 1, gt_hi, gt_lo, range(0, KT // 2), height(t), weights=first)
                if not isinstance(t, int) or t + 2 <= NT:
                    turn_tokens(*tile(i, u, 2))
                product(out_ps, 1, gt_hi, gt_lo, range(KT // 2, KT), height(t), weights=first).then_inc(s_out, 1)

            pe.wait_ge(s_ident, 2)
            turn_tokens(0, 0, 0)
            z_product(0)
            turn_tokens(1, 1, 0)
            run_steps(pe, step)

        def halves(hi_t, lo_t, n):
            return [(hi_t[:, 4 * x:4 * x + 4, 0:n], lo_t[:, 4 * x:4 * x + 4, 0:n]) for x in range(2)]

        def bank_view(x, n):
            return tps[x][:, 0:4 * n].rearrange("p (k n) -> p k n", k=4)

        @block.scalar
        def _(act):
            def high(number, hi_t, lo_t, n):
                for x, (hi, _lo) in enumerate(halves(hi_t, lo_t, n)):
                    act.wait_ge(s_tr, number + x + 1)
                    nc.scalar.activation(hi, bank_view(x, n), ACT.Copy).then_inc(s_tr_hi, 1)

            def split_w(k):
                act.wait_ge(s_wraw[k % RAW], 16 * (k // RAW + 1))
                nc.scalar.activation(w_hi[:, k // KT, k % KT, :], w_raw[k % RAW][:], ACT.Copy,
                                     scale=gains[:, k:k + 1] if k < KT else 1.0).then_inc(s_whi, 1)

            def root(t):
                n = height(t)
                act.wait_ge(s_out, t + 1)
                if above(t, 1):
                    act.wait_ge(s_rstd, 6 * t)
                nc.scalar.activation(square[0:n, :], out_ps[0:n, :], ACT.Square,
                                     accum_out=stat[0:n, 0:1]).then_inc(s_square, 1)
                act.wait_ge(s_square, t + 1)
                nc.scalar.activation(stat[0:n, 1:2], stat[0:n, 0:1], ACT.Sqrt, scale=1.0 / D,
                                     bias=eps[0:n, :]).then_inc(s_root, 1)

            def weights(t):
                act.wait_ge(s_diff, 6 * t + 2)
                nc.scalar.activation(coef[:, 1, :, :], coef[:, 0, :, :], ACT.Exp).then_inc(s_exp, 1)

            def gate(t):
                n = height(t)
                act.wait_ge(s_z, t + 1)
                if above(t, 1):
                    act.wait_ge(s_gated, t)
                nc.scalar.activation(silu_z[0:n, :], z_ps[0:n, :], ACT.Silu).then_inc(s_silu, 1)

            def step(i, u):
                t, b, m = tile(i, u)
                high(gated_job(t), gt_hi, gt_lo, height(t))
                if above(t, 1):
                    root(t - 1)
                if not isinstance(t, int) or t + 1 < NT:
                    weights(t + 1)
                if not isinstance(t, int) or t < NT:
                    gate(t + 1)
                if not isinstance(t, int) or t + 2 <= NT:
                    high(token_job(t + 2), ht_hi, ht_lo, height(t + 2))

            high(0, ht_hi, ht_lo, P)
            act.wait_ge(s_const, 16)
            for k in range(KT):
                split_w(k)
            weights(0)
            gate(0)
            high(token_job(1), ht_hi, ht_lo, P)
            for k in range(KT, 2 * KT):
                split_w(k)
            act.wait_ge(s_eps, 1)
            run_steps(act, step)
            root(NT)

        def weigh(engine, b, g):
            x = part[b][:, g, 0:D].rearrange("p (h d) -> p h d", d=HD)
            return engine.tensor_tensor(x, x, coef[:, 2, g, :].unsqueeze(2).to_broadcast([P, HEADS, HD]), ALU.mult)

        @block.vector
        def _(dve):
            def low(number, hi_t, lo_t, n):
                for x, (hi, lo) in enumerate(halves(hi_t, lo_t, n)):
                    dve.wait_ge(s_tr_hi, number + x + 1)
                    nc.vector.tensor_tensor(lo, bank_view(x, n), hi.bitcast(F32), ALU.subtract).then_inc(s_tr_free, 1)

            def split_w(k):
                dve.wait_ge(s_whi, k + 1)
                hi, lo = w_hi[:, k // KT, k % KT, :].bitcast(F32), w_lo[:, k // KT, k % KT, :]
                if k < KT:
                    nc.vector.scalar_tensor_tensor(out=lo, in0=w_raw[k % RAW][:], scalar=gains[:, k:k + 1], in1=hi,
                                                   op0=ALU.mult, op1=ALU.subtract).then_inc(s_wlo, 1)
                else:
                    nc.vector.tensor_tensor(lo, w_raw[k % RAW][:], hi, ALU.subtract).then_inc(s_wlo, 1)

            def normalise(t):
                n = height(t)
                dve.wait_ge(s_root, t + 1)
                reciprocal_root(dve, s_rstd, 6 * t, stat[0:n, 0:1], stat[0:n, 1:2], scratch[0:n, :], stat[0:n, 2:3])
                if above(t, 1):
                    dve.wait_ge(s_y, t)
                dve.wait_ge(s_rstd, 6 * t + 6)
                nc.vector.scalar_tensor_tensor(out=normed[0:n, :], in0=out_ps[0:n, :], scalar=stat[0:n, 2:3],
                                               in1=post_gain[0:n, :], op0=ALU.mult, op1=ALU.mult)\
                  .then_inc(s_normed, 1)

            def coefficients(t, b, m):
                bias, denominators = (part[b][:, :, first:first + HEADS] for first in (D, D + HEADS))
                dve.wait_ge(s_p[b], 16 * GROUPS * m + 16 * GROUPS)
                if above(t, 1):
                    dve.wait_ge(s_mul, 2 * t)
                    dve.wait_ge(s_mul2, 3 * t)
                nc.vector.tensor_reduce(small[:, 0, :], bias.rearrange("p g h -> p h g"), AX_X, ALU.min)\
                  .then_inc(s_diff, 1)
                dve.wait_ge(s_diff, 6 * t + 1)
                shape = [P, GROUPS, HEADS]
                nc.vector.tensor_tensor(coef[:, 0, :, :], small[:, 0:1, :].to_broadcast(shape), bias,
                                        ALU.subtract).then_inc(s_diff, 1)
                dve.wait_ge(s_exp, t + 1)
                nc.vector.tensor_tensor(coef[:, 0, :, :], coef[:, 1, :, :], denominators, ALU.mult).then_inc(s_diff, 1)
                dve.wait_ge(s_diff, 6 * t + 3)
                nc.vector.tensor_reduce(small[:, 1, :], coef[:, 0, :, :].rearrange("p g h -> p h g"), AX_X,
                                        ALU.add).then_inc(s_diff, 1)
                dve.wait_ge(s_diff, 6 * t + 4)
                nc.vector.reciprocal(small[:, 2, :], small[:, 1, :]).then_inc(s_diff, 1)
                dve.wait_ge(s_diff, 6 * t + 5)
                nc.vector.tensor_tensor(coef[:, 2, :, :], coef[:, 1, :, :], small[:, 2:3, :].to_broadcast(shape),
                                        ALU.mult).then_inc(s_diff, 1)

            def merge(t, b, m):
                n = height(t)
                groups = [part[b][0:n, g, 0:D] for g in range(GROUPS)]
                if n == P:
                    coefficients(t, b, m)
                    dve.wait_ge(s_diff, 6 * t + 6)
                    weigh(nc.vector, b, 2).then_inc(s_mul2, 1)
                    dve.wait_ge(s_mul, 2 * t + 2)
                    nc.vector.tensor_tensor(groups[0], groups[0], groups[1], ALU.add).then_inc(s_mul2, 1)
                    dve.wait_ge(s_mul2, 3 * t + 2)
                    nc.vector.tensor_tensor(groups[0], groups[0], groups[2], ALU.add).then_inc(s_mul2, 1)
                    dve.wait_ge(s_mul2, 3 * t + 3)
                else:
                    dve.wait_ge(s_p[b], 16 * GROUPS * m + 16)
                dve.wait_ge(s_silu, t + 1)
                nc.vector.tensor_tensor(groups[0], groups[0], silu_z[0:n, :], ALU.mult).then_inc(s_gated, 1)

            def step(i, u):
                t, b, m = tile(i, u)
                low(gated_job(t), gt_hi, gt_lo, height(t))
                if above(t, 1):
                    normalise(t - 1)
                if not isinstance(t, int) or t < NT:
                    merge(*tile(i, u, 1))
                if not isinstance(t, int) or t + 2 <= NT:
                    low(token_job(t + 2), ht_hi, ht_lo, height(t + 2))

            nc.vector.memset(eps[:], EPS).then_inc(s_eps, 1)
            low(0, ht_hi, ht_lo, P)
            dve.wait_ge(s_const, 16)
            for k in range(KT):
                split_w(k)
            merge(0, 0, 0)
            low(token_job(1), ht_hi, ht_lo, P)
            for k in range(KT, 2 * KT):
                split_w(k)
            dve.wait_ge(s_const, 32)
            dve.wait_ge(s_wlo, 2 * KT)
            run_steps(dve, step)
            normalise(NT)

        @block.gpsimd
        def _(pool):
            def add(t, b, m):
                n = height(t)
                pool.wait_ge(s_h[b], 16 * m + 16)
                pool.wait_ge(s_normed, t + 1)
                nc.gpsimd.tensor_tensor(h_buf[b][0:n, :], h_buf[b][0:n, :], normed[0:n, :], ALU.add).then_inc(s_y, 1)

            def weigh_two(t, b):
                pool.wait_ge(s_diff, 6 * t + 6)
                for g in range(2):
                    weigh(nc.gpsimd, b, g).then_inc(s_mul, 1)

            def step(i, u):
                t, b, m = tile(i, u)
                if above(t, 1):
                    add(*tile(i, u, -1))
                if not isinstance(t, int) or t + 1 < NT:
                    weigh_two(*tile(i, u, 1)[:2])

            nc.gpsimd.memset(ident[:], 0.0).then_inc(s_ident, 1)
            pool.wait_ge(s_ident, 1)
            nc.gpsimd.affine_select(out=ident[:], in_=ident[:], compare_op=ALU.not_equal, fill=1.0, base=0,
                                    pattern=[[-1, P]], channel_multiplier=1).then_inc(s_ident, 1)
            weigh_two(0, 0)
            run_steps(pool, step)
            add(NT, 0, NT // 2)


def decoder_program(nc, ins, outs, scratch):
    with nc.cleanup_on_exit():
        conv_projection_phase(nc, ins["x_prompt"], ins["x_sample"], ins["state_conv"], ins["a_norm_pre"],
                              ins["a_w_in"], ins["a_conv"], scratch["y_t"], outs["state_conv_prompt"],
                              outs["state_conv_sample"], [ins[f"cache_kv_g{g}"] for g in range(GROUPS)],
                              [outs[f"cache_kv_g{g}_sample"] for g in range(GROUPS)])
    with nc.cleanup_on_exit():
        conv_output_phase(nc, ins["x_prompt"], ins["x_sample"], scratch["y_t"], ins["a_w_out"], ins["a_norm_post"],
                          scratch["h_rows"], scratch["hn_rows"])
    for g in range(GROUPS):
        with nc.cleanup_on_exit():
            group_phase(nc, g, scratch["hn_rows"], ins["w_kv"], ins["b_w_in"], ins["kv_norm"], ins["b_norm_pre"],
                        ins["rope_rows"], scratch[f"partial{g}"], outs[f"cache_kv_g{g}_prompt"],
                        scratch[f"q_sample{g}"], scratch[f"new_rows{g}"],
                        outs[f"cache_kv_g{g}_sample"][:, WINDOWS[g] - 1, :])
    with nc.cleanup_on_exit():
        sample_attention_phase(nc, [scratch[f"q_sample{g}"] for g in range(GROUPS)],
                               [scratch[f"new_rows{g}"] for g in range(GROUPS)],
                               [ins[f"cache_kv_g{g}"] for g in range(GROUPS)], scratch["o_sample"])
    with nc.cleanup_on_exit():
        attention_output_phase(nc, scratch["hn_rows"], scratch["h_rows"],
                               [scratch[f"partial{g}"] for g in range(GROUPS)], scratch["o_sample"],
                               ins["b_w_in"][:, GROUPS * D:(GROUPS + 1) * D], ins["b_w_out"], ins["b_norm_pre"],
                               ins["b_norm_post"], outs["y_prompt"], outs["y_sample"])


def rope_table():
    exponent = -np.arange(HD // 2, dtype=np.float32) * np.float32(2.0) / np.float32(HD)
    frequency = (ROPE_THETA ** exponent.astype(np.float64)).astype(np.float32)
    angle = np.arange(SEQ + 1, dtype=np.float32)[:, None] * frequency[None, :]
    angle = angle.astype(np.float64)
    return np.concatenate([np.cos(angle), -np.sin(angle), np.sin(angle)], axis=1).astype(np.float32)


INPUT_SHAPES = {
    "x_prompt": (SEQ, D), "x_sample": (NS, D), "state_conv": (2 * NS, D),
    **{f"cache_kv_g{g}": (NS, WINDOWS[g], 2 * KVW) for g in range(GROUPS)},
    "a_norm_pre": (D,), "a_w_in": (D, 4 * D), "a_conv": (3, D), "a_w_out": (D, D), "a_norm_post": (D,),
    "kv_norm": (D,), "w_kv": (D, 2 * GROUPS * KVW), "b_norm_pre": (D,), "b_w_in": (D, (GROUPS + 1) * D),
    "b_w_out": (D, D), "b_norm_post": (D,),
}
OUTPUT_SHAPES = {
    "y_prompt": ((SEQ, D), (1, SEQ, D)),
    "y_sample": ((NS, D), (NS, 1, D)),
    "state_conv_prompt": ((2, D), (1, 1, 2, D)),
    **{f"cache_kv_g{g}_prompt": ((WINDOWS[g], 2 * KVW), (1, WINDOWS[g], 2, KVH, HD)) for g in range(GROUPS)},
    "state_conv_sample": ((NS, 2, D), (1, NS, 2, D)),
    **{f"cache_kv_g{g}_sample": ((NS, WINDOWS[g], 2 * KVW), (NS, WINDOWS[g], 2, KVH, HD)) for g in range(GROUPS)},
}
SCRATCH_SHAPES = {
    "y_t": (D, TOK), "h_rows": (TOK, D), "hn_rows": (TOK, D), "o_sample": (NS, D),
    **{f"partial{g}": (SEQ, OMW) for g in range(GROUPS)},
    **{f"q_sample{g}": (NS, D) for g in range(GROUPS)},
    **{f"new_rows{g}": (NS * HEADS, 2 * HD) for g in range(GROUPS)},
}


def kernel(**inputs):
    import concourse.bacc as bacc
    from concourse.bass_utils import run_bass_kernel_spmd

    nc = bacc.Bacc("TRN2", target_bir_lowering=False, num_devices=1)
    arrays = {name: np.ascontiguousarray(inputs[name]).reshape(shape) for name, shape in INPUT_SHAPES.items()}
    arrays["rope_rows"] = rope_table()
    ins = {name: nc.dram_tensor(name, list(a.shape), F32, kind="ExternalInput").ap() for name, a in arrays.items()}
    outs = {name: nc.dram_tensor(f"out_{name}", list(shape), F32, kind="ExternalOutput").ap()
            for name, (shape, _) in OUTPUT_SHAPES.items()}
    scratch = {name: nc.dram_tensor(f"scratch_{name}", list(shape), F32, kind="Internal").ap()
               for name, shape in SCRATCH_SHAPES.items()}
    decoder_program(nc, ins, outs, scratch)
    results = run_bass_kernel_spmd(nc, [arrays], core_ids=[0]).results[0]
    return tuple(np.asarray(results[f"out_{name}"]).reshape(shape) for name, (_, shape) in OUTPUT_SHAPES.items())
```

```python
from collections import namedtuple
from contextlib import ExitStack

import numpy as np

import concourse.bass as bass
from concourse import mybir

F32 = mybir.dt.float32
F32R = mybir.dt.float32r
BF16 = mybir.dt.bfloat16
ALU = mybir.AluOpType
ACT = mybir.ActivationFunctionType
AX_X = mybir.AxisListType.X

P = 128
D = 1024
KT = D // P
SEQ = 2048
NS = 8
TOK = SEQ + NS
NT = SEQ // P
BANK = 512
EPS = 1e-6


def row_tile(t):
    return P if t < NT else NS


def reciprocal_root(dve, done, before, square_sum, root, scratch, out):
    mean, r, e = scratch[:, 0:1], scratch[:, 1:2], scratch[:, 2:3]
    nc = dve.bass
    nc.vector.tensor_scalar(mean, square_sum, 1.0 / D, EPS, ALU.mult, ALU.add).then_inc(done, 1)
    nc.vector.reciprocal(r, root).then_inc(done, 1)
    dve.wait_ge(done, before + 2)
    nc.vector.tensor_tensor(e, r, r, ALU.mult).then_inc(done, 1)
    dve.wait_ge(done, before + 3)
    nc.vector.tensor_tensor(e, e, mean, ALU.mult).then_inc(done, 1)
    dve.wait_ge(done, before + 4)
    nc.vector.tensor_scalar(e, e, -0.5, 1.5, ALU.mult, ALU.add).then_inc(done, 1)
    dve.wait_ge(done, before + 5)
    nc.vector.tensor_tensor(out, r, e, ALU.mult).then_inc(done, 1)


def conv_projection_phase(nc, x_prompt, x_sample, state_conv, norm_pre, w_in, w_conv,
                          y_t, state_out_prompt, state_out_sample, caches, caches_out):
    CHUNK = 412
    NCH = -(-TOK // CHUNK)
    size = [min(CHUNK, TOK - c * CHUNK) for c in range(NCH)]
    LAST = size[-1] - NS
    NF = D // P
    GATES = (1, 2, 0, 3)
    XB = 3
    JOBS = 2 * NCH

    with ExitStack() as ctx:
        def sb(name, shape, dt=F32):
            return ctx.enter_context(nc.sbuf_tensor(name, shape, dt))

        def sem(name):
            return nc.alloc_semaphore(name)

        ht_hi = sb("a_ht_hi", [P, KT, TOK], F32R)
        ht_lo = sb("a_ht_lo", [P, KT, TOK], F32R)
        w_raw = [sb(f"a_w_raw{b}", [P, KT, P]) for b in range(2)]
        w_hi = [sb(f"a_w_hi{k}", [P, KT, P], F32R) for k in range(4)]
        w_lo = [sb(f"a_w_lo{k}", [P, KT, P], F32R) for k in range(4)]
        u_buf = [sb(f"a_u{b}", [P, 2 + CHUNK]) for b in range(2)]
        conv = sb("a_conved", [P, TOK])
        c_sb = [sb(f"a_c{b}", [P, CHUNK]) for b in range(2)]
        silu_z = [sb(f"a_silu_z{b}", [P, CHUNK]) for b in range(2)]
        y_buf = [sb(f"a_y{b}", [P, CHUNK]) for b in range(2)]
        x_buf = [sb(f"a_x{b}", [P, D]) for b in range(XB)]
        gain = sb("a_gain", [P, D])
        ident = sb("a_ident", [P, P])
        stat = sb("a_stat", [P, 3, NT + 1])
        eps = sb("a_eps", [P, 1])
        scratch = sb("a_scratch", [P, 3])
        rows = x_buf[XB - 1]
        col_all = sb("a_col_all", [P, NF, 19])
        col = sb("a_col", [P, 19])
        last_u = sb("a_last_u", [P, NF, 2 + NS])
        state_rows = x_buf[0]

        pair = [ctx.enter_context(nc.psum_tensor(f"a_pair{b}", [P, 2, BANK], F32)) for b in range(2)]
        tps = [ctx.enter_context(nc.psum_tensor(f"a_tps{b}", [P, BANK], F32)) for b in range(2)]
        square = ctx.enter_context(nc.psum_tensor("a_square", [P, D], F32))

        s_const = sem("a_const")
        s_rows = sem("a_rows")
        s_ident = sem("a_ident_ready")
        s_eps = sem("a_eps_ready")
        s_x = [sem(f"a_x_landed{b}") for b in range(XB)]
        s_sumsq = sem("a_sumsq")
        s_root = sem("a_root")
        s_rstd = sem("a_rstd")
        s_xn = sem("a_xn")
        s_tr = sem("a_transposed")
        s_tr_hi = sem("a_transposed_hi")
        s_tr_free = sem("a_transpose_evacuated")
        s_col = sem("a_col_ready")
        s_wraw = [sem(f"a_w_landed{b}") for b in range(2)]
        s_whi = sem("a_w_hi_ready")
        s_wlo = sem("a_w_lo_ready")
        s_pair = sem("a_pair_ready")
        s_c = sem("a_c_copied")
        s_z = sem("a_silu_ready")
        s_free = sem("a_pair_evacuated")
        s_halo = sem("a_halo")
        s_tap0 = sem("a_tap0")
        s_tap1 = sem("a_tap1")
        s_tap2 = sem("a_tap2")
        s_stap = sem("a_sample_taps")
        s_lastu = sem("a_last_u_kept")
        s_y = sem("a_y_ready")
        s_ystore = [sem(f"a_y_stored{b}") for b in range(2)]
        s_out = sem("a_state_stored")
        s_moved = sem("a_cache_moved")

        w_view = w_in.rearrange("(k p) (g n) -> p k g n", p=P, g=4)

        block = ctx.enter_context(nc.Block())

        def x_tile(t):
            return x_prompt[t * P:(t + 1) * P, :] if t < NT else x_sample

        STATE_JOB = 1 + 2 * (NT + 1)

        @block.sync
        def _(sp):
            def load_w(i, half):
                if not isinstance(i, int) or i + half > 0:
                    sp.wait_ge(s_wlo, 4 * i + 2 * half)
                for k in (2 * half + 1, 2 * half):
                    src = w_view[:, :, GATES[k], bass.ds(i * P, P)]
                    sp.dma_start(w_raw[k % 2][:], src).then_inc(s_wraw[k % 2], 16)

            def load_x(t):
                if t >= XB:
                    sp.wait_ge(s_tr, 1 + 2 * (t - XB) + 2)
                elif t == XB - 1:
                    sp.wait_ge(s_tr, 1)
                sp.dma_start(x_buf[t % XB][0:row_tile(t), :], x_tile(t)).then_inc(s_x[t % XB], 16)

            def store_y(i, c):
                b = (NCH + c) % 2
                sp.wait_ge(s_const, 16)
                sp.wait_ge(s_y, NCH * i + c + 1)
                sp.dma_start(y_t[bass.ds(i * P, P), c * CHUNK:c * CHUNK + size[c]],
                             y_buf[b][:, 0:size[c]]).then_inc(s_ystore[b], 16)

            for b in range(2):
                sp.sem_inc(s_ystore[b], 16)
            load_x(0)
            sp.dma_start(gain[:], norm_pre.partition_broadcast(P)).then_inc(s_const, 16)
            sp.dma_start(rows[0:16, :], state_conv).then_inc(s_rows, 16)
            sp.dma_start(rows[16:19, :], w_conv).then_inc(s_rows, 16)
            load_w(0, 0)
            for t in range(1, NT + 1):
                load_x(t)
                if t == 5:
                    load_w(0, 1)
            with sp.Fori(0, NF - 1) as i:
                for half in range(2):
                    load_w(i + 1, half)
                for c in range(NCH):
                    store_y(i, c)
            for c in range(NCH):
                store_y(NF - 1, c)
            sp.dma_start(state_out_sample[:, 0, :],
                         state_conv.rearrange("(s j) d -> s j d", j=2)[:, 1, :]).then_inc(s_out, 16)
            sp.wait_ge(s_tr_free, STATE_JOB + 2)
            sp.dma_start(state_out_prompt, state_rows[0:2, :]).then_inc(s_out, 16)
            sp.dma_start(state_out_sample[:, 1, :], state_rows[2:2 + NS, :]).then_inc(s_out, 16)
            sp.wait_ge(s_out, 48)
            sp.wait_ge(s_moved, 16 * NS * (JOBS + 2))
            for b in range(2):
                sp.wait_ge(s_ystore[b], 16 + 16 * NF * len([c for c in range(NCH) if (NCH + c) % 2 == b]))

        @block.gpsimd
        def _(pool):
            nc.gpsimd.memset(ident[:], 0.0).then_inc(s_ident, 1)
            pool.wait_ge(s_ident, 1)
            nc.gpsimd.affine_select(out=ident[:], in_=ident[:], compare_op=ALU.not_equal, fill=1.0, base=0,
                                    pattern=[[-1, P]], channel_multiplier=1).then_inc(s_ident, 1)

            def split_w_lo(i, k):
                pool.wait_ge(s_whi, 4 * i + k + 1)
                nc.gpsimd.tensor_tensor(w_lo[k][:], w_raw[k % 2][:], w_hi[k][:].bitcast(F32),
                                        ALU.subtract).then_inc(s_wlo, 1)

            for k in range(4):
                split_w_lo(0, k)
            with pool.Fori(1, NF) as i:
                for k in range(4):
                    split_w_lo(i, k)

        @block.tensor
        def _(pe):
            def transpose_tile(t):
                n = row_tile(t)
                pe.wait_ge(s_xn, t + 1)
                for half in range(2):
                    job = 1 + 2 * t + half
                    if job >= 2:
                        pe.wait_ge(s_tr_free, job - 1)
                    for k in range(4):
                        last = nc.tensor.transpose(tps[job % 2][:, k * n:(k + 1) * n],
                                                   x_buf[t % XB][0:n, (4 * half + k) * P:(4 * half + k + 1) * P],
                                                   ident[0:n, 0:n])
                    last.then_inc(s_tr, 1)

            def product_pair(i, half, c, tiles=()):
                job = JOBS * i + NCH * half + c
                slot = (NCH * half + c) % 2
                if not isinstance(job, int) or job >= 2:
                    pe.wait_ge(s_free, job - 1)
                pe.wait_ge(s_wlo, 4 * i + 2 * half + 2)
                cols = slice(c * CHUNK, c * CHUNK + size[c])
                for g in range(2):
                    out = pair[slot][:, g, 0:size[c]]
                    for k in range(KT):
                        if (g * KT + k) % 4 == 1 and (g * KT + k) // 4 < len(tiles):
                            transpose_tile(tiles[(g * KT + k) // 4])
                        hi, lo = w_hi[2 * half + g][:, k, :], w_lo[2 * half + g][:, k, :]
                        nc.tensor.matmul(out, hi, ht_hi[:, k, cols], start=(k == 0), stop=False)
                        nc.tensor.matmul(out, hi, ht_lo[:, k, cols], start=False, stop=False)
                        last = nc.tensor.matmul(out, lo, ht_hi[:, k, cols], start=False, stop=(k == KT - 1))
                last.then_inc(s_pair, 1)

            pe.wait_ge(s_ident, 2)
            pe.wait_ge(s_rows, 32)
            for k in range(KT):
                last = nc.tensor.transpose(tps[0][:, 19 * k:19 * k + 19], rows[0:19, k * P:(k + 1) * P],
                                           ident[0:19, 0:19])
            last.then_inc(s_tr, 1)
            need = [min(NT + 1, -(-(c * CHUNK + size[c]) // P)) for c in range(NCH)]
            for t in range(need[0]):
                transpose_tile(t)
            for c in range(NCH):
                pe.wait_ge(s_tr_free, 1 + 2 * need[c])
                product_pair(0, 0, c, range(need[c], need[min(c + 1, NCH - 1)]))
            with pe.Fori(1, NF) as i:
                for c in range(NCH):
                    product_pair(i - 1, 1, c)
                for c in range(NCH):
                    product_pair(i, 0, c)
            for c in range(NCH):
                product_pair(NF - 1, 1, c)
            pe.wait_ge(s_lastu, NF)
            for half in range(2):
                job = STATE_JOB + half
                for k in range(4):
                    last = nc.tensor.transpose(tps[job % 2][0:2 + NS, k * P:(k + 1) * P],
                                               last_u[:, 4 * half + k, :], ident[:])
                last.then_inc(s_tr, 1)

        @block.scalar
        def _(act):
            def norm_stats(t):
                n = row_tile(t)
                act.wait_ge(s_x[t % XB], 16 * (t // XB + 1))
                nc.scalar.activation(square[0:n, :], x_buf[t % XB][0:n, :], ACT.Square,
                                     accum_out=stat[0:n, 0, t:t + 1]).then_inc(s_sumsq, 1)
                act.wait_ge(s_sumsq, t + 1)
                nc.scalar.activation(stat[0:n, 1, t:t + 1], stat[0:n, 0, t:t + 1], ACT.Sqrt,
                                     scale=1.0 / D, bias=eps[0:n, :]).then_inc(s_root, 1)

            def tokens_hi(t):
                n = row_tile(t)
                for half in range(2):
                    job = 1 + 2 * t + half
                    act.wait_ge(s_tr, job + 1)
                    nc.scalar.activation(ht_hi[:, 4 * half:4 * half + 4, t * P:t * P + n],
                                         tps[job % 2][:, 0:4 * n].rearrange("p (k n) -> p k n", k=4),
                                         ACT.Copy).then_inc(s_tr_hi, 1)

            def split_w_hi(i, k):
                act.wait_ge(s_wraw[k % 2], 16 * (2 * i + k // 2 + 1))
                if not isinstance(i, int) or i > 0:
                    act.wait_ge(s_pair, JOBS * (i - 1) + (NCH if k < 2 else JOBS))
                nc.scalar.activation(w_hi[k][:], w_raw[k % 2][:], ACT.Copy).then_inc(s_whi, 1)

            def copy_c(i, c):
                act.wait_ge(s_pair, JOBS * i + c + 1)
                nc.scalar.activation(c_sb[c % 2][:, 0:size[c]], pair[c % 2][:, 0, 0:size[c]],
                                     ACT.Copy).then_inc(s_c, 1)

            def tap0(i, c):
                n = size[c] if c < NCH - 1 else LAST
                act.wait_ge(s_halo, NCH * i + c + 1)
                act.wait_ge(s_free, JOBS * i + c + 1)
                nc.scalar.activation(conv[:, c * CHUNK:c * CHUNK + n], u_buf[c % 2][:, 0:n], ACT.Copy,
                                     scale=col[:, 16:17]).then_inc(s_tap0, 1)

            def gate_z(i, c):
                b = (NCH + c) % 2
                act.wait_ge(s_pair, JOBS * i + NCH + c + 1)
                if c >= 2:
                    act.wait_ge(s_y, NCH * i + c - 1)
                nc.scalar.activation(silu_z[b][:, 0:size[c]], pair[b][:, 1, 0:size[c]],
                                     ACT.Silu).then_inc(s_z, 1)

            def move_caches(i, part):
                for cache, moved in zip(caches, caches_out):
                    count = cache.shape[1] - 1
                    large = count >= 1024
                    if part > 0 and not large:
                        continue
                    size_of = -(-count // JOBS) if large else count
                    begin = part * size_of
                    size_of = min(size_of, count - begin)
                    act.dma_start(moved[bass.ds(i, 1), begin:begin + size_of, :],
                                  cache[bass.ds(i, 1), begin + 1:begin + 1 + size_of, :]).then_inc(s_moved, 16)

            act.wait_ge(s_eps, 1)
            norm_stats(0)
            split_w_hi(0, 0)
            split_w_hi(0, 1)
            norm_stats(1)
            done = 0
            for c in range(NCH):
                need = min(NT + 1, -(-(c * CHUNK + size[c]) // P))
                for t in range(done, need):
                    tokens_hi(t)
                    if t + 2 <= NT:
                        norm_stats(t + 2)
                done = need
                if c >= 1:
                    copy_c(0, c - 1)
                    tap0(0, c - 1)
                    if c == 2:
                        split_w_hi(0, 2)
                        split_w_hi(0, 3)
            copy_c(0, NCH - 1)
            tap0(0, NCH - 1)
            with act.Fori(1, NF) as i:
                for c in range(NCH):
                    gate_z(i - 1, c)
                    move_caches(i - 1, c)
                    if c == 0:
                        split_w_hi(i, 0)
                        split_w_hi(i, 1)
                for c in range(NCH):
                    copy_c(i, c)
                    tap0(i, c)
                    move_caches(i - 1, NCH + c)
                    if c == 0:
                        split_w_hi(i, 2)
                        split_w_hi(i, 3)
            for c in range(NCH):
                gate_z(NF - 1, c)
                for part in (2 * c, 2 * c + 1):
                    move_caches(NF - 1, part)
            act.wait_ge(s_tr, STATE_JOB + 1)
            nc.scalar.activation(state_rows[0:2 + NS, 0:BANK], tps[STATE_JOB % 2][0:2 + NS, :],
                                 ACT.Copy).then_inc(s_tr_free, 1)

        @block.vector
        def _(dve):
            def normalise(t):
                n = row_tile(t)
                dve.wait_ge(s_root, t + 1)
                reciprocal_root(dve, s_rstd, 6 * t, stat[0:n, 0, t:t + 1], stat[0:n, 1, t:t + 1],
                                scratch[0:n, :], stat[0:n, 2, t:t + 1])
                if t == 0:
                    dve.wait_ge(s_const, 16)
                dve.wait_ge(s_rstd, 6 * t + 6)
                nc.vector.scalar_tensor_tensor(out=x_buf[t % XB][0:n, :], in0=x_buf[t % XB][0:n, :],
                                               scalar=stat[0:n, 2, t:t + 1], in1=gain[0:n, :],
                                               op0=ALU.mult, op1=ALU.mult).then_inc(s_xn, 1)

            def tokens_lo(t):
                n = row_tile(t)
                for half in range(2):
                    job = 1 + 2 * t + half
                    dve.wait_ge(s_tr_hi, 2 * t + half + 1)
                    cols = (slice(None), slice(4 * half, 4 * half + 4), slice(t * P, t * P + n))
                    nc.vector.tensor_tensor(ht_lo[cols],
                                            tps[job % 2][:, 0:4 * n].rearrange("p (k n) -> p k n", k=4),
                                            ht_hi[cols].bitcast(F32), ALU.subtract).then_inc(s_tr_free, 1)

            def load_columns(i):
                dve.wait_ge(s_tr_free, 1)
                nc.vector.tensor_copy(col[:], col_all[:, bass.ds(i, 1), :].rearrange("p a c -> p (a c)"))\
                  .then_inc(s_col, 1)

            def conv_inputs(i, c):
                b, n = c % 2, size[c] if c < NCH - 1 else LAST
                if c == 0:
                    nc.vector.memset(u_buf[0][:, 0:2], 0.0).then_inc(s_halo, 1)
                else:
                    nc.vector.tensor_copy(u_buf[b][:, 0:2], u_buf[1 - b][:, CHUNK:CHUNK + 2]).then_inc(s_halo, 1)
                dve.wait_ge(s_c, NCH * i + c + 1)
                nc.vector.tensor_tensor(u_buf[b][:, 2:2 + size[c]], c_sb[b][:, 0:size[c]],
                                        pair[b][:, 1, 0:size[c]], ALU.mult).then_inc(s_free, 1)
                dve.wait_ge(s_free, JOBS * i + c + 1)
                out = conv[:, c * CHUNK:c * CHUNK + n]
                if c == 0:
                    dve.wait_ge(s_col, i + 1)
                dve.wait_ge(s_halo, NCH * i + c + 1)
                dve.wait_ge(s_tap0, NCH * i + c + 1)
                nc.vector.scalar_tensor_tensor(out=out, in0=u_buf[b][:, 1:1 + n], scalar=col[:, 17:18], in1=out,
                                               op0=ALU.mult, op1=ALU.add).then_inc(s_tap1, 1)
                dve.wait_ge(s_tap1, NCH * i + c + 1)
                nc.vector.scalar_tensor_tensor(out=out, in0=u_buf[b][:, 2:2 + n], scalar=col[:, 18:19], in1=out,
                                               op0=ALU.mult, op1=ALU.add).then_inc(s_tap2, 1)
                if c < NCH - 1:
                    return
                past = col[:, 0:2 * NS].rearrange("p (s j) -> p s j", j=2)
                out = conv[:, SEQ:TOK]
                nc.vector.tensor_scalar(out, past[:, :, 0], col[:, 16:17], None, ALU.mult).then_inc(s_stap, 1)
                for tap, src in ((1, past[:, :, 1]), (2, u_buf[b][:, 2 + LAST:2 + LAST + NS])):
                    dve.wait_ge(s_stap, 3 * i + tap)
                    nc.vector.scalar_tensor_tensor(out=out, in0=src, scalar=col[:, 16 + tap:17 + tap], in1=out,
                                                   op0=ALU.mult, op1=ALU.add).then_inc(s_stap, 1)
                nc.vector.tensor_copy(last_u[:, bass.ds(i, 1), :].rearrange("p a c -> p (a c)"),
                                      u_buf[b][:, LAST:LAST + 2 + NS]).then_inc(s_lastu, 1)

            def gated(i, c):
                b = (NCH + c) % 2
                cols = slice(c * CHUNK, c * CHUNK + size[c])
                dve.wait_ge(s_z, NCH * i + c + 1)
                if c == 0:
                    dve.wait_ge(s_stap, 3 * i + 3)
                    dve.wait_ge(s_tap2, NCH * i + NCH)
                count = [k for k in range(NCH) if (NCH + k) % 2 == b]
                dve.wait_ge(s_ystore[b], 16 + 16 * (len(count) * i + count.index(c)))
                nc.vector.tensor_tensor(y_buf[b][:, 0:size[c]], pair[b][:, 0, 0:size[c]], conv[:, cols],
                                        ALU.mult).then_inc(s_free, 1)
                dve.wait_ge(s_free, JOBS * i + NCH + c + 1)
                nc.vector.tensor_tensor(y_buf[b][:, 0:size[c]], y_buf[b][:, 0:size[c]],
                                        silu_z[b][:, 0:size[c]], ALU.mult).then_inc(s_y, 1)

            nc.vector.memset(eps[:], EPS).then_inc(s_eps, 1)
            normalise(0)
            dve.wait_ge(s_tr, 1)
            nc.vector.tensor_copy(col_all[:].rearrange("p k c -> p (k c)"), tps[0][:, 0:19 * KT]).then_inc(s_tr_free, 1)
            load_columns(0)
            normalise(1)
            done = 0
            for c in range(NCH):
                need = min(NT + 1, -(-(c * CHUNK + size[c]) // P))
                for t in range(done, need):
                    tokens_lo(t)
                    if t + 2 <= NT:
                        normalise(t + 2)
                done = need
                if c >= 1:
                    conv_inputs(0, c - 1)
            conv_inputs(0, NCH - 1)
            with dve.Fori(1, NF) as i:
                for c in range(NCH):
                    gated(i - 1, c)
                load_columns(i)
                for c in range(NCH):
                    conv_inputs(i, c)
            for c in range(NCH):
                gated(NF - 1, c)
            dve.wait_ge(s_tr, STATE_JOB + 2)
            nc.vector.tensor_copy(state_rows[0:2 + NS, BANK:D], tps[(STATE_JOB + 1) % 2][0:2 + NS, :])\
              .then_inc(s_tr_free, 1)


def conv_output_phase(nc, x_prompt, x_sample, y_t, w_out, norm_post, h_rows, hn_rows):
    HALVES = D // BANK
    RAW = 4

    with ExitStack() as ctx:
        def sb(name, shape, dt=F32):
            return ctx.enter_context(nc.sbuf_tensor(name, shape, dt))

        def sem(name):
            return nc.alloc_semaphore(name)

        w_raw = [sb(f"b_w_raw{b}", [P, D]) for b in range(RAW)]
        w_hi = sb("b_w_hi", [P, KT, D], F32R)
        w_lo = sb("b_w_lo", [P, KT, D], F32R)
        y_raw = [sb(f"b_y_raw{b}", [P, KT, P]) for b in range(2)]
        y_hi = [sb(f"b_y_hi{b}", [P, KT, P], F32R) for b in range(2)]
        y_lo = [sb(f"b_y_lo{b}", [P, KT, P], F32R) for b in range(2)]
        x_buf = [sb(f"b_x{b}", [P, D]) for b in range(2)]
        normed = sb("b_normed", [P, D])
        h_buf = [sb(f"b_h{b}", [P, D]) for b in range(2)]
        hn_buf = [sb(f"b_hn{b}", [P, D]) for b in range(2)]
        gain = sb("b_gain", [P, D])
        eps = sb("b_eps", [P, 1])
        stat = [sb(f"b_stat{b}", [P, 6]) for b in range(2)]
        scratch = sb("b_scratch", [P, 3])

        out_ps = [ctx.enter_context(nc.psum_tensor(f"b_out{b}", [P, D], F32)) for b in range(2)]
        square = ctx.enter_context(nc.psum_tensor("b_square", [P, D], F32))

        s_gain = sem("b_gain_landed")
        s_eps = sem("b_eps_ready")
        s_wraw = [sem(f"b_w_landed{b}") for b in range(RAW)]
        s_whi = sem("b_w_hi_ready")
        s_wlo = sem("b_w_lo_ready")
        s_y = [sem(f"b_y_landed{b}") for b in range(2)]
        s_x = [sem(f"b_x_landed{b}") for b in range(2)]
        s_yhi = sem("b_y_hi_ready")
        s_ylo = sem("b_y_lo_ready")
        s_out = sem("b_product_ready")
        s_square = sem("b_squares")
        s_root = sem("b_roots")
        s_rstd = sem("b_rstd_steps")
        s_normed = sem("b_normed_ready")
        s_h = sem("b_h_ready")
        s_hn = sem("b_hn_ready")
        s_hstore = [sem(f"b_h_stored{b}") for b in range(2)]
        s_hnstore = [sem(f"b_hn_stored{b}") for b in range(2)]

        w_view = w_out.rearrange("(k p) n -> p k n", p=P)
        y_view = y_t.rearrange("(k p) t -> p k t", p=P)
        block = ctx.enter_context(nc.Block())
        LOOPS = NT // 2 - 1
        TAIL = range(2 * LOOPS, NT + 1)

        @block.sync
        def _(sp):
            def load_y(t, u):
                n = NS if isinstance(t, int) and t == NT else P
                if not isinstance(t, int) or t >= 2:
                    sp.wait_ge(s_gain, 16)
                    sp.wait_ge(s_ylo, t - 1)
                sp.dma_start(y_raw[u][:, :, 0:n], y_view[:, :, bass.ds(t * P, n)]).then_inc(s_y[u], 16)

            def load_x(t, u):
                n = NS if isinstance(t, int) and t == NT else P
                if not isinstance(t, int) or t >= 2:
                    sp.wait_ge(s_gain, 16)
                    sp.wait_ge(s_h, t - 1)
                src = x_sample if n == NS else x_prompt[bass.ds(t * P, P), :]
                sp.dma_start(x_buf[u][0:n, :], src).then_inc(s_x[u], 16)

            def store(t, u):
                n = NS if isinstance(t, int) and t == NT else P
                sp.wait_ge(s_gain, 16)
                sp.wait_ge(s_h, t + 1)
                sp.dma_start(h_rows[bass.ds(t * P, n), :], h_buf[u][0:n, :]).then_inc(s_hstore[u], 16)
                sp.wait_ge(s_gain, 16)
                sp.wait_ge(s_hn, t + 1)
                sp.dma_start(hn_rows[bass.ds(t * P, n), :], hn_buf[u][0:n, :]).then_inc(s_hnstore[u], 16)

            for s in (*s_hstore, *s_hnstore):
                sp.sem_inc(s, 16)
            for k in range(KT):
                if k >= RAW:
                    sp.wait_ge(s_wlo, k - RAW + 1)
                if k == 0:
                    load_y(0, 0)
                if k == 4:
                    load_x(0, 0)
                    sp.dma_start(gain[:], norm_post.partition_broadcast(P)).then_inc(s_gain, 16)
                sp.dma_start(w_raw[k % RAW][:], w_view[:, k, :]).then_inc(s_wraw[k % RAW], 16)
            load_y(1, 1)
            load_x(1, 1)
            with sp.Fori(0, LOOPS) as i:
                for u in range(2):
                    load_y(2 * i + u + 2, u)
                    load_x(2 * i + u + 2, u)
                    store(2 * i + u, u)
            load_y(NT, 0)
            load_x(NT, 0)
            for t in TAIL:
                store(t, t % 2)
            for b in range(2):
                sp.wait_ge(s_hstore[b], 16 + 16 * (NT // 2 + (b == 0)))
                sp.wait_ge(s_hnstore[b], 16 + 16 * (NT // 2 + (b == 0)))

        @block.tensor
        def _(pe):
            def product(t, u):
                n = NS if isinstance(t, int) and t == NT else P
                pe.wait_ge(s_ylo, t + 1)
                if not isinstance(t, int) or t >= 2:
                    pe.wait_ge(s_normed, t - 1)
                for k in range(KT):
                    if isinstance(t, int) and t == 0:
                        pe.wait_ge(s_wlo, k + 1)
                    for c in range(HALVES):
                        out, cols = out_ps[u][0:n, c * BANK:(c + 1) * BANK], slice(c * BANK, (c + 1) * BANK)
                        hi, lo = y_hi[u][:, k, 0:n], y_lo[u][:, k, 0:n]
                        nc.tensor.matmul(out, hi, w_hi[:, k, cols], start=(k == 0), stop=False)
                        nc.tensor.matmul(out, hi, w_lo[:, k, cols], start=False, stop=False)
                        last = nc.tensor.matmul(out, lo, w_hi[:, k, cols], start=False, stop=(k == KT - 1))
                last.then_inc(s_out, 1)

            product(0, 0)
            product(1, 1)
            with pe.Fori(1, LOOPS) as i:
                for u in range(2):
                    product(2 * i + u, u)
            for t in TAIL:
                product(t, t % 2)

        @block.scalar
        def _(act):
            def y_high(t, u, i):
                n = NS if isinstance(t, int) and t == NT else P
                act.wait_ge(s_y[u], 16 * i + 16)
                if not isinstance(t, int) or t >= 2:
                    act.wait_ge(s_out, t - 1)
                nc.scalar.activation(y_hi[u][:, :, 0:n], y_raw[u][:, :, 0:n], ACT.Copy).then_inc(s_yhi, 1)

            def norms(t, u, i, ahead=True):
                n = NS if isinstance(t, int) and t == NT else P
                act.wait_ge(s_out, t + 1)
                nc.scalar.activation(square[0:n, :], out_ps[u][0:n, :], ACT.Square,
                                     accum_out=stat[u][0:n, 0:1]).then_inc(s_square, 1)
                act.wait_ge(s_square, 2 * t + 1)
                nc.scalar.activation(stat[u][0:n, 1:2], stat[u][0:n, 0:1], ACT.Sqrt, scale=1.0 / D,
                                     bias=eps[0:n, :]).then_inc(s_root, 1)
                if ahead:
                    y_high(t + 2, u, i + 1)
                act.wait_ge(s_h, t + 1)
                nc.scalar.activation(square[0:n, :], h_buf[u][0:n, :], ACT.Square,
                                     accum_out=stat[u][0:n, 3:4]).then_inc(s_square, 1)
                act.wait_ge(s_square, 2 * t + 2)
                nc.scalar.activation(stat[u][0:n, 4:5], stat[u][0:n, 3:4], ACT.Sqrt, scale=1.0 / D,
                                     bias=eps[0:n, :]).then_inc(s_root, 1)
                act.wait_ge(s_rstd, 12 * t + 12)
                act.wait_ge(s_hnstore[u], 16 + 16 * i)
                nc.scalar.activation(hn_buf[u][0:n, :], h_buf[u][0:n, :], ACT.Copy,
                                     scale=stat[u][0:n, 5:6]).then_inc(s_hn, 1)

            y_high(0, 0, 0)
            act.wait_ge(s_eps, 1)
            for k in range(KT):
                act.wait_ge(s_wraw[k % RAW], 16 * (k // RAW + 1))
                nc.scalar.activation(w_hi[:, k, :], w_raw[k % RAW][:], ACT.Copy).then_inc(s_whi, 1)
            y_high(1, 1, 0)
            with act.Fori(0, LOOPS) as i:
                for u in range(2):
                    norms(2 * i + u, u, i)
            for t in TAIL:
                norms(t, t % 2, t // 2, ahead=t + 2 <= NT)

        @block.vector
        def _(dve):
            def y_low(t, u):
                n = NS if isinstance(t, int) and t == NT else P
                dve.wait_ge(s_yhi, t + 1)
                nc.vector.tensor_tensor(y_lo[u][:, :, 0:n], y_raw[u][:, :, 0:n], y_hi[u][:, :, 0:n].bitcast(F32),
                                        ALU.subtract).then_inc(s_ylo, 1)

            def norms(t, u, ahead=True):
                n = NS if isinstance(t, int) and t == NT else P
                dve.wait_ge(s_root, 2 * t + 1)
                reciprocal_root(dve, s_rstd, 12 * t, stat[u][0:n, 0:1], stat[u][0:n, 1:2],
                                scratch[0:n, :], stat[u][0:n, 2:3])
                if isinstance(t, int) and t == 0:
                    dve.wait_ge(s_gain, 16)
                dve.wait_ge(s_rstd, 12 * t + 6)
                nc.vector.scalar_tensor_tensor(out=normed[0:n, :], in0=out_ps[u][0:n, :],
                                               scalar=stat[u][0:n, 2:3], in1=gain[0:n, :],
                                               op0=ALU.mult, op1=ALU.mult).then_inc(s_normed, 1)
                if ahead:
                    y_low(t + 2, u)
                dve.wait_ge(s_root, 2 * t + 2)
                reciprocal_root(dve, s_rstd, 12 * t + 6, stat[u][0:n, 3:4], stat[u][0:n, 4:5],
                                scratch[0:n, :], stat[u][0:n, 5:6])

            nc.vector.memset(eps[:], EPS).then_inc(s_eps, 1)
            y_low(0, 0)
            for k in range(KT):
                dve.wait_ge(s_whi, k + 1)
                nc.vector.tensor_tensor(w_lo[:, k, :], w_raw[k % RAW][:], w_hi[:, k, :].bitcast(F32),
                                        ALU.subtract).then_inc(s_wlo, 1)
            y_low(1, 1)
            with dve.Fori(0, LOOPS) as i:
                for u in range(2):
                    norms(2 * i + u, u)
            for t in TAIL:
                norms(t, t % 2, ahead=t + 2 <= NT)

        @block.gpsimd
        def _(pool):
            def add(t, u, i):
                n = NS if isinstance(t, int) and t == NT else P
                pool.wait_ge(s_x[u], 16 * i + 16)
                pool.wait_ge(s_hstore[u], 16 + 16 * i)
                pool.wait_ge(s_hnstore[u], 16 + 16 * i)
                pool.wait_ge(s_normed, t + 1)
                nc.gpsimd.tensor_tensor(h_buf[u][0:n, :], x_buf[u][0:n, :], normed[0:n, :],
                                        ALU.add).then_inc(s_h, 1)

            with pool.Fori(0, LOOPS) as i:
                for u in range(2):
                    add(2 * i + u, u, i)
            for t in TAIL:
                add(t, t % 2, t // 2)


HD = 128
HEADS = 8
KVH = 2
QPK = HEADS // KVH
KVW = KVH * HD
GROUPS = 3
WINDOWS = (128, 512, 2048)
DILATIONS = (1, 4, 16)
ROPE_THETA = 10000.0
SCALE = HD ** -0.5
MASKED = -1e30
OMW = D + 2 * HEADS

Item = namedtuple("Item", "g i u last")


def attention_phase(nc, hn_rows, w_kv, w_q, kv_gain, q_gain, rope_rows,
                    partials, caches_out, q_sample, new_rows, newest):
    TILES = SEQ // P
    UN = 4
    BODIES = TILES // UN
    EACH = range(GROUPS)
    ITEMS = TILES + 1
    KW = KVW + KVW + D
    BANK_COLS = [slice(b * BANK, (b + 1) * BANK) for b in range(3)]

    def rows(w):
        step = DILATIONS[w.g]
        row_i, row_u = ((UN * P, P), (1, UN * P), (UN, 1))[w.g]
        return bass.ds(row_i * w.i + row_u * w.u, P, step=step)

    def ahead(w, k):
        u = w.u + k
        if not w.last or u < UN:
            return Item(w.g, w.i + u // UN, u % UN, w.last)
        if w.g == GROUPS - 1:
            return None
        return Item(w.g + 1, 0, None, False) if u == UN else Item(w.g + 1, 0, u - UN - 1, False)

    def exists(w, k):
        return not w.last or w.u + k < UN or w.g < GROUPS - 1

    def ordinal(w):
        return ITEMS * w.g + (0 if w.u is None else 1 + UN * w.i + w.u)

    def parity(w):
        return (ITEMS * w.g + (0 if w.u is None else 1 + w.u)) % 2

    def landed(w):
        return (ITEMS * w.g + (0 if w.u is None else 1 + w.u)) // 2 + (0 if w.u is None else UN // 2 * w.i) + 1

    def height(w):
        return NS if w.u is None else P

    def number(w):
        return TILES * w.g + UN * w.i + w.u

    def has_before(w):
        return w.g == 0 or (w.g == 1 and w.u > 0)

    def names(w):
        probs = ("a", "b") if has_before(w) else ("a",)
        tokens = ("h0", "h1") if exists(w, 2) else ()
        return ["q0", "k", "q1", *tokens, *("p0" + x for x in probs), *("p1" + x for x in probs), "o0", "o1"]

    per_body = [sum(len(names(Item(g, 0, u, False))) for u in range(UN)) for g in EACH]
    first_job = [6, 6 + BODIES * per_body[0] + 2, 6 + BODIES * (per_body[0] + per_body[1]) + 4]
    assert all(n % 2 == 0 for n in per_body)

    def job(w, name):
        before = sum(len(names(w._replace(u=v))) for v in range(w.u)) + names(w).index(name)
        return first_job[w.g] + before + per_body[w.g] * w.i, before % 2

    def run_steps(engine, g, step):
        with engine.Fori(0, BODIES - 1) as i:
            for u in range(UN):
                step(Item(g, i, u, False))
        for u in range(UN):
            step(Item(g, BODIES - 1, u, True))

    def sample(g):
        return Item(g, 0, None, False)

    def first(g, u):
        return Item(g, 0, u, False)

    with ExitStack() as ctx:
        def sb(name, shape, dt=F32):
            return ctx.enter_context(nc.sbuf_tensor(f"g_{name}", shape, dt))

        def ps(name, shape):
            return ctx.enter_context(nc.psum_tensor(f"g_{name}", shape, F32))

        def sem(name):
            return nc.alloc_semaphore(f"g_{name}")

        w_raw = [sb(f"w_raw{b}", [P, KW]) for b in range(2)]
        w_hi = sb("w_hi", [P, KT, KW], F32R)
        w_lo = sb("w_lo", [P, KT, KW], F32R)
        gains = sb("gains", [P, 2, KT])
        tok = [sb(f"tok{b}", [P, D]) for b in range(2)]
        ht_hi = [sb(f"ht_hi{b}", [P, KT, P], F32R) for b in range(2)]
        ht_lo = [sb(f"ht_lo{b}", [P, KT, P], F32R) for b in range(2)]
        trig = [sb(f"trig{b}", [P, 3, HD // 2]) for b in range(2)]
        rot_a = sb("rot_a", [P, 3, BANK])
        rot_b = sb("rot_b", [P, 3, BANK])
        raw = [w_raw[0][:], w_raw[1][:], *(x[:].rearrange("p b n -> p (b n)") for x in (rot_a, rot_b))]
        RAW = len(raw)
        q_rot = [sb(f"q_rot{n}", [P, BANK]) for n in range(KVH)]
        kv_rows = [sb(f"kv_rows{b}", [P, 2 * KVW]) for b in range(2)]
        qt_hi = [sb(f"qt_hi{n}", [P, BANK], F32R) for n in range(KVH)]
        qt_lo = [sb(f"qt_lo{n}", [P, BANK], F32R) for n in range(KVH)]
        kt_hi = sb("kt_hi", [P, KVH, 2 * P], F32R)
        kt_lo = sb("kt_lo", [P, KVH, 2 * P], F32R)
        v_hi = [sb(f"v_hi{b}", [P, KVW], F32R) for b in range(2)]
        v_lo = [sb(f"v_lo{b}", [P, KVW], F32R) for b in range(2)]
        probs = sb("probs", [P, QPK, 2 * P])
        pt_hi = sb("pt_hi", [P, 2 * BANK], F32R)
        pt_lo = sb("pt_lo", [P, 2 * BANK], F32R)
        sum_t = [sb(f"sum_t{n}", [P, BANK]) for n in range(KVH)]
        minus_max = sb("minus_max", [P, QPK])
        part = [sb(f"part{b}", [P, OMW]) for b in range(2)]
        mask_f = sb("mask_f", [P, 3, P])
        mask = sb("mask", [P, (3 + 2 * BODIES) * P], BF16)
        ident = sb("ident", [P, P])

        proj = ps("proj", [P, 3, BANK])
        score = ps("score", [P, QPK, 2 * P])
        tps = [ps(f"tps{b}", [P, BANK]) for b in range(2)]
        out_ps = ps("out", [P, BANK])

        s_gains = sem("gains_landed")
        s_ident = sem("ident_ready")
        s_mask = sem("mask_ready")
        s_wraw = [sem(f"w_landed{b}") for b in range(RAW)]
        s_whi = sem("w_hi_ready")
        s_wlo = sem("w_lo_ready")
        s_tok = [sem(f"tok_landed{b}") for b in range(2)]
        s_trig = [sem(f"trig_landed{b}") for b in range(2)]
        s_tr = sem("transposed")
        s_tr_hi = sem("transposed_hi")
        s_tr_free = sem("transpose_evacuated")
        s_proj = sem("projected")
        s_rope = sem("rope_products")
        s_rot = sem("rotated")
        s_v = sem("v_copied")
        s_vhi = sem("v_hi_ready")
        s_vlo = sem("v_lo_ready")
        s_score = sem("scores_ready")
        s_masked = sem("scores_masked")
        s_max = sem("max_ready")
        s_bias = sem("bias_ready")
        s_exp = sem("exps_ready")
        s_pv = sem("pv_ready")
        s_sum_t = sem("sums_t_copied")
        s_kvstore = [[sem(f"kv_stored{g}_{b}") for b in range(2)] for g in EACH]
        s_partstore = [sem(f"partial_stored{b}") for b in range(2)]
        s_sstore = sem("sample_stored")

        SAMPLE_STORES = 16 * (1 + HEADS + KVH)
        kv_view = w_kv.rearrange("(k p) (j g n) -> p k j g n", p=P, j=2, g=GROUPS)
        q_view = w_q.rearrange("(k p) n -> p k n", p=P)
        block = ctx.enter_context(nc.Block())

        def cached(w):
            return w.g == 2 or (w.g == 1 and w.u == UN - 1) or (w.g == 0 and w.last and w.u == UN - 1)

        def kv_rows_stored(engine, w):
            if w.u is None:
                return
            if w.g > 0 and isinstance(w.i, int) and w.i == 0 and w.u == 0:
                old = w.g - 1
                engine.wait_ge(s_kvstore[old][(ITEMS * old + TILES) % 2], 16 + 16 * (1 if old == 0 else BODIES))
            elif w.g == 1 and w.u == 1:
                engine.wait_ge(s_kvstore[1][parity(w)], 16 + 16 * w.i)
            elif w.g == 2 and not (isinstance(w.i, int) and w.i == 0 and w.u < 2):
                engine.wait_ge(s_kvstore[2][parity(w)], 16 + 16 * (2 * w.i + w.u // 2))

        @block.sync
        def _(sp):
            def load_tokens(w):
                n = height(w)
                src = hn_rows[SEQ:TOK, :] if w.u is None else hn_rows[rows(w), :]
                sp.dma_start(tok[parity(w)][0:n, :], src).then_inc(s_tok[parity(w)], 16)

            def load_trig(w):
                n = height(w)
                if w.u is None:
                    src = rope_rows[SEQ:SEQ + 1, :].rearrange("a (c n) -> a c n", c=3).to_broadcast([NS, 3, HD // 2])
                else:
                    src = rope_rows[rows(w), :].rearrange("t (c n) -> t c n", c=3)
                sp.dma_start(trig[parity(w)][0:n], src).then_inc(s_trig[parity(w)], 16)

            def load_weights(g, ks):
                for k in ks:
                    if k >= RAW:
                        sp.wait_ge(s_wlo, KT * g + k - RAW + 1)
                    elif g > 0 and k >= 2:
                        sp.wait_ge(s_rot, 3 * ordinal(sample(g)))
                    sp.dma_start(raw[k % RAW][:, 0:2 * KVW].rearrange("p (j n) -> p j n", j=2),
                                 kv_view[:, k, :, g, :]).then_inc(s_wraw[k % RAW], 16)
                    sp.dma_start(raw[k % RAW][:, 2 * KVW:KW],
                                 q_view[:, k, g * D:(g + 1) * D]).then_inc(s_wraw[k % RAW], 16)

            def store_sample(g):
                w = sample(g)
                kv = kv_rows[parity(w)]
                sp.wait_ge(s_rot, 3 * ordinal(w) + 3)
                sp.wait_ge(s_v, ordinal(w) + 1)
                sp.dma_start(newest[g], kv[0:NS, :]).then_inc(s_sstore, 16)
                for x in range(HEADS):
                    sp.dma_start(new_rows[g].rearrange("(b x) (j d) -> b x j d", x=HEADS, j=2)[:, x],
                                 kv[0:NS, :].rearrange("b (j n d) -> b j n d", j=2, n=KVH)[:, :, x // QPK, :])\
                      .then_inc(s_sstore, 16)
                for n in range(KVH):
                    sp.dma_start(q_sample[g][:, n * BANK:(n + 1) * BANK], q_rot[n][0:NS, :]).then_inc(s_sstore, 16)

            def step(w):
                prefetch = w.last and w.g < GROUPS - 1
                if exists(w, 2):
                    sp.wait_ge(s_gains, 32)
                    sp.wait_ge(s_rope, 3 * ordinal(w) + 3)
                    load_trig(ahead(w, 2))
                if prefetch and w.u == UN - 1:
                    load_weights(w.g + 1, (4, 5))
                if exists(w, 4):
                    sp.wait_ge(s_gains, 32)
                    sp.wait_ge(s_tr, job(w, "h1")[0] + 1)
                    load_tokens(ahead(w, 4))
                if cached(w):
                    sp.wait_ge(s_gains, 32)
                    sp.wait_ge(s_rot, 3 * ordinal(w) + 1)
                    out = caches_out[w.g]
                    dst = (out, out[bass.ds(w.i, P, step=DILATIONS[1]), :] if w.g == 1 else None,
                           out[rows(w), :] if w.g == 2 else None)[w.g]
                    sp.dma_start(dst, kv_rows[parity(w)][:]).then_inc(s_kvstore[w.g][parity(w)], 16)
                if prefetch and w.u == 1:
                    load_weights(w.g + 1, (0, 1))
                if prefetch and w.u == UN - 1:
                    load_weights(w.g + 1, (6, 7))
                sp.wait_ge(s_gains, 32)
                sp.wait_ge(s_tr_free, job(w, "o1")[0] + 1)
                sp.dma_start(partials[w.g][rows(w), :], part[w.u % 2][:]).then_inc(s_partstore[w.u % 2], 16)
                if prefetch and w.u == 2:
                    load_weights(w.g + 1, (2, 3))

            for s in (*s_kvstore[1], *s_kvstore[2], s_kvstore[0][0], s_kvstore[0][1], *s_partstore):
                sp.sem_inc(s, 16)
            load_tokens(sample(0))
            load_weights(0, (0, 1))
            load_trig(sample(0))
            load_tokens(first(0, 0))
            load_trig(first(0, 0))
            load_weights(0, range(2, KT))
            sp.wait_ge(s_tr, 2)
            load_tokens(first(0, 1))
            for g in EACH:
                w = sample(g)
                sp.wait_ge(s_rope, 3 * ordinal(w) + 3)
                load_trig(first(g, 1))
                store_sample(g)
                if g == 0:
                    sp.wait_ge(s_tr, 4)
                    load_tokens(first(g, 2))
                sp.wait_ge(s_tr, first_job[g])
                load_tokens(first(g, 3))
                run_steps(sp, g, step)
            sp.wait_ge(s_sstore, SAMPLE_STORES * GROUPS)
            for b in range(2):
                sp.wait_ge(s_partstore[b], 16 + 16 * GROUPS * TILES // 2)
                sp.wait_ge(s_kvstore[2][b], 16 + 16 * TILES // 2)
            for g in (0, 1):
                sp.wait_ge(s_kvstore[g][(ITEMS * g + TILES) % 2], 16 + 16 * (1 if g == 0 else BODIES))

        @block.tensor
        def _(pe):
            def bank_wait(number):
                if not isinstance(number, int) or number >= 2:
                    pe.wait_ge(s_tr_free, number - 1)

            def turn(number, bank, src, blocks, n=P):
                bank_wait(number)
                for x, first in enumerate(blocks):
                    t = nc.tensor.transpose(tps[bank][:, x * n:(x + 1) * n], src[0:n, first:first + P],
                                            ident[0:n, 0:n])
                t.then_inc(s_tr, 1)

            def turn_tokens(w, jobs):
                pe.wait_ge(s_tok[parity(w)], 16 * landed(w))
                for half in range(2):
                    turn(*jobs[half], tok[parity(w)], [(4 * half + k) * P for k in range(4)], height(w))

            def product(w, bank, k):
                n, b = height(w), parity(w)
                out, cols = proj[0:n, bank, :], BANK_COLS[bank]
                hi, lo = ht_hi[b][:, k, 0:n], ht_lo[b][:, k, 0:n]
                nc.tensor.matmul(out, hi, w_hi[:, k, cols], start=(k == 0), stop=False)
                nc.tensor.matmul(out, hi, w_lo[:, k, cols], start=False, stop=False)
                last = nc.tensor.matmul(out, lo, w_hi[:, k, cols], start=False, stop=(k == KT - 1))
                if k == KT - 1:
                    last.then_inc(s_proj, 1)

            def project(w, bank, k0, k1):
                if k0 == 0:
                    pe.wait_ge(s_rope, 3 * ordinal(w) - 2 + bank)
                for k in range(k0, k1):
                    product(w, bank, k)

            def project_sample(w, ks):
                for k in ks:
                    if k == 0 and w.g > 0:
                        pe.wait_ge(s_rope, 3 * ordinal(w))
                    pe.wait_ge(s_wlo, KT * w.g + k + 1)
                    for bank in range(3):
                        product(w, bank, k)

            def scores(w, n):
                a = number(w)
                pe.wait_ge(s_tr_free, job(w, ("k", "q1")[n])[0] + 1)
                if n == 1:
                    pe.wait_ge(s_exp, 8 * a + 4)
                cols = slice(0, 2 * P) if has_before(w) else slice((w.u % 2) * P, (w.u % 2 + 1) * P)
                for h in range(QPK):
                    q, out = slice(h * P, (h + 1) * P), score[:, h, cols]
                    nc.tensor.matmul(out, qt_hi[n][:, q], kt_hi[:, n, cols], start=True, stop=False)
                    nc.tensor.matmul(out, qt_hi[n][:, q], kt_lo[:, n, cols], start=False, stop=False)
                    t = nc.tensor.matmul(out, qt_lo[n][:, q], kt_hi[:, n, cols], start=False, stop=True)
                t.then_inc(s_score, 1)

            def turn_probs(w, n):
                pe.wait_ge(s_exp, 8 * number(w) + 4 * n + 4)
                src = probs[:].rearrange("p h k -> p (h k)")
                if has_before(w):
                    for x, name in enumerate("ab"):
                        turn(*job(w, f"p{n}{name}"), src, [(4 * x + y) * P for y in range(4)])
                else:
                    turn(*job(w, f"p{n}a"), src, [(2 * h + w.u % 2) * P for h in range(QPK)])

            def values(w, n):
                a = number(w)
                parities = (0, 1) if has_before(w) else (w.u % 2,)
                pe.wait_ge(s_tr_free, job(w, f"p{n}" + ("b" if has_before(w) else "a"))[0] + 1)
                pe.wait_ge(s_vlo, a + 1)
                if n == 1:
                    pe.wait_ge(s_sum_t, 2 * a + 1)
                v = slice(n * HD, (n + 1) * HD)
                shape = dict(h=QPK, y=len(parities))
                hi, lo = (x[:, 0:len(parities) * BANK].rearrange("p (h y q) -> p y h q", **shape)
                          for x in (pt_hi, pt_lo))
                for y, par in enumerate(parities):
                    start, final = y == 0, y == len(parities) - 1
                    nc.tensor.matmul(out_ps[:], v_hi[par][:, v], hi[:, y], start=start, stop=False)
                    nc.tensor.matmul(out_ps[:], v_lo[par][:, v], hi[:, y], start=False, stop=False)
                    t = nc.tensor.matmul(out_ps[:], v_hi[par][:, v], lo[:, y], start=False, stop=final)
                t.then_inc(s_pv, 1)

            def turn_sums(w, n):
                pe.wait_ge(s_sum_t, 2 * number(w) + n + 1)
                turn(*job(w, f"o{n}"), sum_t[n], [h * P for h in range(QPK)])

            def between(w, spot):
                if w is None:
                    return
                if w.u is None:
                    project_sample(w, ((), (), (0, 1), (2,), (3, 4), (5, 6, 7))[spot])
                else:
                    for part_of in (((0, 0, 2),), ((0, 2, KT),), ((1, 0, 6),), ((1, 6, KT), (2, 0, 4)), ((2, 4, 7),),
                                    ((2, 7, KT),))[spot]:
                        project(w, *part_of)

            def step(w):
                following = ahead(w, 1)
                pe.wait_ge(s_rot, 3 * ordinal(w) + 2)
                turn(*job(w, "q0"), q_rot[0], [h * P for h in range(QPK)])
                between(following, 0)
                turn(*job(w, "k"), kv_rows[parity(w)], [n * P for n in range(KVH)])
                between(following, 1)
                scores(w, 0)
                pe.wait_ge(s_rot, 3 * ordinal(w) + 3)
                turn(*job(w, "q1"), q_rot[1], [h * P for h in range(QPK)])
                between(following, 2)
                if exists(w, 2):
                    turn_tokens(ahead(w, 2), [job(w, "h0"), job(w, "h1")])
                scores(w, 1)
                turn_probs(w, 0)
                between(following, 3)
                values(w, 0)
                turn_probs(w, 1)
                between(following, 4)
                values(w, 1)
                turn_sums(w, 0)
                between(following, 5)
                turn_sums(w, 1)

            pe.wait_ge(s_ident, 2)
            turn_tokens(sample(0), [(0, 0), (1, 1)])
            project_sample(sample(0), range(0, 4))
            turn_tokens(first(0, 0), [(2, 0), (3, 1)])
            project_sample(sample(0), range(4, KT))
            for g in EACH:
                turn_tokens(first(g, 1), [(first_job[g] - 2, 0), (first_job[g] - 1, 1)])
                for bank in range(3):
                    project(first(g, 0), bank, 0, KT)
                if g == 0:
                    pe.wait_ge(s_mask, 4)
                run_steps(pe, g, step)

        def evacuations(w):
            par = slice((w.u % 2) * P, (w.u % 2 + 1) * P)
            to = {"q0": (BANK, qt_hi[0][:], qt_lo[0][:]), "q1": (BANK, qt_hi[1][:], qt_lo[1][:]),
                  "k": (KVW, kt_hi[:, :, par], kt_lo[:, :, par])}
            if exists(w, 2):
                b, n = parity(ahead(w, 2)), height(ahead(w, 2))
                for half in range(2):
                    k = slice(4 * half, 4 * half + 4)
                    to[f"h{half}"] = (4 * n, ht_hi[b][:, k, 0:n], ht_lo[b][:, k, 0:n])
            for n in range(KVH):
                for x, name in enumerate("ab"):
                    cols = slice(x * BANK, (x + 1) * BANK)
                    to[f"p{n}{name}"] = (BANK, pt_hi[:, cols], pt_lo[:, cols])
                to[f"o{n}"] = (BANK, part[w.u % 2][:, n * BANK:n * BANK + BANK // 2],
                               part[w.u % 2][:, n * BANK + BANK // 2:(n + 1) * BANK])
            return {name: (job(w, name), *to[name]) for name in names(w)}

        def bank_view(bank, width, like):
            src = tps[bank][:, 0:width]
            return src.rearrange("p (a b) -> p a b", a=like.shape[1]) if len(like.shape) == 3 else src

        def token_jobs(w, jobs):
            b, n = parity(w), height(w)
            return [((jobs + half, half), 4 * n, ht_hi[b][:, 4 * half:4 * half + 4, 0:n],
                     ht_lo[b][:, 4 * half:4 * half + 4, 0:n]) for half in range(2)]

        WEIGHT_COLS = (slice(0, 2 * KVW), slice(2 * KVW, KW))

        @block.scalar
        def _(act):
            def high(at, width, hi, lo):
                act.wait_ge(s_tr, at[0] + 1)
                nc.scalar.activation(hi, bank_view(at[1], width, hi), ACT.Copy).then_inc(s_tr_hi, 1)

            def sums_left(at, width, left, right):
                act.wait_ge(s_tr, at[0] + 1)
                nc.scalar.activation(left, tps[at[1]][:, 0:BANK // 2], ACT.Copy).then_inc(s_tr_hi, 1)

            def copy_v(w):
                n, b = height(w), parity(w)
                act.wait_ge(s_proj, 3 * ordinal(w) + 1)
                kv_rows_stored(act, w)
                nc.scalar.activation(kv_rows[b][0:n, KVW:2 * KVW], proj[0:n, 0, KVW:2 * KVW],
                                     ACT.Copy).then_inc(s_v, 1)

            def split_weights(g, k):
                if g > 0 and k == 0:
                    act.wait_ge(s_proj, 3 * ordinal(sample(g)))
                act.wait_ge(s_wraw[k % RAW], 32 * (KT // RAW * g + k // RAW + 1))
                for x, cols in enumerate(WEIGHT_COLS):
                    nc.scalar.activation(w_hi[:, k, cols], raw[k % RAW][:, cols], ACT.Copy,
                                         scale=gains[:, x, k:k + 1]).then_inc(s_whi, 1)

            def exponentials(w, n):
                act.wait_ge(s_bias, 2 * number(w) + n + 1)
                cols = slice(0, 2 * P) if has_before(w) else slice((w.u % 2) * P, (w.u % 2 + 1) * P)
                for h in range(QPK):
                    x = QPK * n + h
                    nc.scalar.activation(probs[:, h, cols], score[:, h, cols], ACT.Exp,
                                         bias=part[w.u % 2][:, D + x:D + x + 1], scale=SCALE,
                                         accum_out=part[w.u % 2][:, D + HEADS + x:D + HEADS + x + 1])\
                      .then_inc(s_exp, 1)

            def copy_sums(w, n):
                act.wait_ge(s_pv, 2 * number(w) + n + 1)
                nc.scalar.activation(sum_t[n][:], out_ps[:], ACT.Copy).then_inc(s_sum_t, 1)

            def step(w):
                ev, following = evacuations(w), ahead(w, 1)
                next_sample = following is not None and following.u is None

                def split(*which):
                    for name in which:
                        if name in ev:
                            high(*ev[name])

                def weights(*ks):
                    for k in ks if next_sample else ():
                        split_weights(following.g, k)

                split("q0", "k")
                act.wait_ge(s_v, ordinal(w) + 1)
                nc.scalar.activation(v_hi[w.u % 2][:], kv_rows[parity(w)][:, KVW:2 * KVW], ACT.Copy)\
                  .then_inc(s_vhi, 1)
                weights(0)
                if following and not next_sample:
                    copy_v(following)
                split("q1")
                exponentials(w, 0)
                weights(1, 2)
                split("h0", "h1")
                split("p0a", "p0b")
                exponentials(w, 1)
                weights(3, 4)
                copy_sums(w, 0)
                split("p1a", "p1b")
                weights(5)
                copy_sums(w, 1)
                weights(6)
                sums_left(*ev["o0"])
                weights(7)
                sums_left(*ev["o1"])
                if next_sample:
                    copy_v(following)

            for x, gain in enumerate((kv_gain, q_gain)):
                act.dma_start(gains[:, x, :], gain.rearrange("(k p) -> p k", p=P),
                              allow_slow_non_contiguous=True).then_inc(s_gains, 16)
            for x in token_jobs(sample(0), 0):
                high(*x)
            act.wait_ge(s_gains, 32)
            for k in range(KT):
                split_weights(0, k)
                for x in token_jobs(first(0, 0), 2) if k == 4 else ():
                    high(*x)
            copy_v(sample(0))
            for g in EACH:
                for x in token_jobs(first(g, 1), first_job[g] - 2):
                    high(*x)
                copy_v(first(g, 0))
                act.wait_ge(s_sstore, SAMPLE_STORES * (g + 1))
                run_steps(act, g, step)

        @block.vector
        def _(dve):
            def low(at, width, hi, lo):
                dve.wait_ge(s_tr_hi, at[0] + 1)
                nc.vector.tensor_tensor(lo, bank_view(at[1], width, hi), hi.bitcast(F32),
                                        ALU.subtract).then_inc(s_tr_free, 1)

            def sums_right(at, width, left, right):
                dve.wait_ge(s_tr_hi, at[0] + 1)
                nc.vector.tensor_copy(right, tps[at[1]][:, BANK // 2:BANK]).then_inc(s_tr_free, 1)

            def rope(w, bank):
                heads = KVH if bank == 0 else QPK
                e, b, n = ordinal(w), parity(w), height(w)
                dve.wait_ge(s_proj, 3 * e + bank + 1)
                if bank == 0:
                    dve.wait_ge(s_v, e + 1)
                dve.wait_ge(s_trig[b], 16 * landed(w))
                if w.u is None:
                    dve.wait_ge(s_wlo, KT * (w.g + 1))
                if w.u is not None or w.g > 0:
                    dve.wait_ge(s_rot, 3 * e + bank - 2)
                src = proj[0:n, bank, 0:heads * HD].rearrange("p (h c x) -> p h c x", h=heads, c=2)
                a, c = (x[0:n, bank, 0:heads * HD].rearrange("p (h c x) -> p h c x", h=heads, c=2)
                        for x in (rot_a, rot_b))
                shape = [n, heads, 2, HD // 2]
                nc.vector.tensor_tensor(a, src, trig[b][0:n, 0:1, :].unsqueeze(1).to_broadcast(shape), ALU.mult)
                nc.vector.tensor_tensor(c, src[:, :, ::-1, :],
                                        trig[b][0:n, 1:3, :].unsqueeze(1).to_broadcast(shape),
                                        ALU.mult).then_inc(s_rope, 1)

            def maxima(w, n):
                a = number(w)
                width = 2 * P if has_before(w) else P
                cols = slice(0, 2 * P) if has_before(w) else slice((w.u % 2) * P, (w.u % 2 + 1) * P)
                if w.g == 0 and w.u == 0:
                    m = mask[:, bass.ds((3 + 2 * w.i) * P, width)]
                elif has_before(w) and w.u % 2:
                    m = mask[:, P:3 * P]
                else:
                    m = mask[:, 0:width]
                dve.wait_ge(s_score, 2 * a + n + 1)
                nc.vector.tensor_tensor(score[:, :, cols], score[:, :, cols],
                                        m.unsqueeze(1).to_broadcast([P, QPK, width]), ALU.add).then_inc(s_masked, 1)
                dve.wait_ge(s_masked, 2 * a + n + 1)
                nc.vector.tensor_reduce(minus_max[:], score[:, :, cols], AX_X, ALU.max, negate=True)\
                  .then_inc(s_max, 1)
                dve.wait_ge(s_partstore[w.u % 2], 16 + 16 * (TILES // 2 * w.g + 2 * w.i + w.u // 2))
                dve.wait_ge(s_max, 2 * a + n + 1)
                nc.vector.tensor_scalar(part[w.u % 2][:, D + QPK * n:D + QPK * (n + 1)], minus_max[:], SCALE, None,
                                        ALU.mult).then_inc(s_bias, 1)

            def split_weights(g, k):
                for x, cols in enumerate(WEIGHT_COLS):
                    dve.wait_ge(s_whi, 2 * (KT * g + k) + x + 1)
                    t = nc.vector.scalar_tensor_tensor(out=w_lo[:, k, cols], in0=raw[k % RAW][:, cols],
                                                       scalar=gains[:, x, k:k + 1],
                                                       in1=w_hi[:, k, cols].bitcast(F32),
                                                       op0=ALU.mult, op1=ALU.subtract)
                t.then_inc(s_wlo, 1)

            def step(w):
                ev, following = evacuations(w), ahead(w, 1)
                next_sample = following is not None and following.u is None

                def split(*which):
                    for name in which:
                        if name in ev:
                            low(*ev[name])

                def turned(bank):
                    if following and not next_sample:
                        rope(following, bank)

                def weights(*ks):
                    for k in ks if next_sample else ():
                        split_weights(following.g, k)

                split("q0", "k")
                maxima(w, 0)
                weights(0)
                turned(0)
                split("q1")
                weights(1, 2)
                split("h0", "h1")
                maxima(w, 1)
                split("p0a", "p0b")
                weights(3, 4)
                turned(1)
                split("p1a", "p1b")
                weights(5, 6)
                sums_right(*ev["o0"])
                weights(7)
                turned(2)
                sums_right(*ev["o1"])
                if next_sample:
                    for bank in range(3):
                        rope(following, bank)

            for x in token_jobs(sample(0), 0):
                low(*x)
            for k in range(KT):
                split_weights(0, k)
                for x in token_jobs(first(0, 0), 2) if k == 4 else ():
                    low(*x)
            for bank in range(3):
                rope(sample(0), bank)
            for g in EACH:
                for x in token_jobs(first(g, 1), first_job[g] - 2):
                    low(*x)
                for bank in range(3):
                    rope(first(g, 0), bank)
                if g == 0:
                    dve.wait_ge(s_mask, 4)
                run_steps(dve, g, step)

        @block.gpsimd
        def _(pool):
            def rotated(w, bank):
                heads, n = KVH if bank == 0 else QPK, height(w)
                dst = kv_rows[parity(w)] if bank == 0 else q_rot[bank - 1]
                if bank == 0:
                    kv_rows_stored(pool, w)
                pool.wait_ge(s_rope, 3 * ordinal(w) + bank + 1)
                nc.gpsimd.tensor_tensor(dst[0:n, 0:heads * HD], rot_a[0:n, bank, 0:heads * HD],
                                        rot_b[0:n, bank, 0:heads * HD], ALU.add).then_inc(s_rot, 1)

            def step(w):
                pool.wait_ge(s_vhi, number(w) + 1)
                nc.gpsimd.tensor_tensor(v_lo[w.u % 2][:], kv_rows[parity(w)][:, KVW:2 * KVW],
                                        v_hi[w.u % 2][:].bitcast(F32), ALU.subtract).then_inc(s_vlo, 1)
                if exists(w, 1):
                    for bank in range(3):
                        rotated(ahead(w, 1), bank)

            nc.gpsimd.memset(ident[:], 0.0).then_inc(s_ident, 1)
            pool.wait_ge(s_ident, 1)
            nc.gpsimd.affine_select(out=ident[:], in_=ident[:], compare_op=ALU.not_equal, fill=1.0, base=0,
                                    pattern=[[-1, P]], channel_multiplier=1).then_inc(s_ident, 1)
            nc.gpsimd.memset(mask_f[:, 0:2, :], 0.0)
            nc.gpsimd.memset(mask_f[:, 2, :], MASKED).then_inc(s_mask, 1)
            pool.wait_ge(s_mask, 1)
            nc.gpsimd.affine_select(out=mask_f[:, 0, :], in_=mask_f[:, 0, :], compare_op=ALU.is_ge, fill=MASKED,
                                    base=0, pattern=[[-1, P]], channel_multiplier=1).then_inc(s_mask, 1)
            nc.gpsimd.affine_select(out=mask_f[:, 1, :], in_=mask_f[:, 1, :], compare_op=ALU.is_ge, fill=MASKED,
                                    base=0, pattern=[[1, P]], channel_multiplier=-1).then_inc(s_mask, 1)
            for zero in (kt_hi[:, :, P:2 * P], kt_lo[:, :, P:2 * P], v_hi[1][:], v_lo[1][:]):
                nc.gpsimd.memset(zero.bitcast(F32), 0.0)
            pool.wait_ge(s_ident, 2)
            pool.wait_ge(s_mask, 3)
            for x, kind in enumerate([0, 1, 0] + [0, 2] + [0, 1] * (BODIES - 1)):
                t = nc.gpsimd.tensor_copy(mask[:, x * P:(x + 1) * P], mask_f[:, kind, :])
            t.then_inc(s_mask, 1)
            for bank in range(3):
                rotated(sample(0), bank)
            for g in EACH:
                pool.wait_ge(s_sstore, SAMPLE_STORES * (g + 1))
                for bank in range(3):
                    rotated(first(g, 0), bank)
                run_steps(pool, g, step)


def sample_attention_phase(nc, q_sample, new_rows, caches, o_sample, w_z, w_out, pre_gain, w_hi, w_lo):
    R = NS * HEADS
    KEYS = P

    with ExitStack() as ctx:
        def sb(name, shape, dt=F32):
            return ctx.enter_context(nc.sbuf_tensor(f"s_{name}", shape, dt))

        def ps(name, shape):
            return ctx.enter_context(nc.psum_tensor(f"s_{name}", shape, F32))

        def sem(name):
            return nc.alloc_semaphore(f"s_{name}")

        each = range(GROUPS)
        cache = [sb(f"cache{c}", [P, NS // 2, 2 * KVW]) for c in range(2 * GROUPS)]
        q_rows = sb("q_rows", [R, GROUPS, HD])
        new = sb("new", [R, GROUPS, 2, HD])
        qt = [sb(f"qt{g}", [P, R]) for g in each]
        keys_t = [sb(f"keys_t{b}", [P, 4, P]) for b in range(2)]
        score_t = [sb(f"score_t{g}", [P, R]) for g in each]
        score = [sb(f"score{g}", [R, KEYS + 1]) for g in each]
        prob = [sb(f"prob{g}", [R, KEYS + 1]) for g in each]
        prob_t = [sb(f"prob_t{g}", [P, R]) for g in each]
        sum_t = [sb(f"sum_t{g}", [P, R]) for g in each]
        product = sb("product", [R, HD])
        sums = sb("sums", [R, GROUPS, HD])
        stat = sb("stat", [R, 4, GROUPS])
        small = sb("small", [R, 4])
        merged = sb("merged", [R, HD])
        ident = sb("ident", [P, P])
        gains = sb("gains", [P, KT])
        RAW = 3
        w_raw = [sb(f"w_raw{b}", [P, D]) for b in range(RAW)]

        tps = [ps(f"tps{b}", [P, 4, P]) for b in range(2)]
        one = [ps(f"one{b}", [P, BANK]) for b in range(2)]
        st_ps = [ps(f"scores_t{b}", [P, BANK]) for b in range(2)]
        ot_ps = [ps(f"sums_t{b}", [P, BANK]) for b in range(2)]

        s_ident = sem("ident_ready")
        s_q = sem("queries_landed")
        s_new_rows = sem("new_rows_landed")
        s_cache = [sem(f"cache_landed{c}") for c in range(2 * GROUPS)]
        s_keys = sem("keys_turned")
        s_keys_sb = sem("keys_copied")
        s_one = sem("single_turned")
        s_one_sb = sem("single_copied")
        s_st = sem("scores_t_ready")
        s_st_sb = sem("scores_t_copied")
        s_new = sem("new_score")
        s_bias = sem("bias_steps")
        s_exp = sem("exps_ready")
        s_ot = sem("sums_t_ready")
        s_ot_sb = sem("sums_t_copied")
        s_w = sem("weights_ready")
        s_step = sem("merge_steps")
        s_out = sem("stored")
        s_gains = sem("gains_landed")
        s_wraw = [sem(f"w_landed{b}") for b in range(RAW)]
        s_whi = sem("w_hi_ready")
        s_wlo = sem("w_lo_ready")

        block = ctx.enter_context(nc.Block())

        SINGLES = [("q", 0), ("q", 1), ("q", 2), ("score", 0), ("score", 1), ("prob", 0),
                   ("score", 2), ("prob", 1), ("sum", 0), ("prob", 2), ("sum", 1), ("sum", 2)]

        def bank(kind, g):
            return one[SINGLES.index((kind, g)) % 2]

        def done(kind, g):
            return SINGLES.index((kind, g)) + 1

        @block.sync
        def _(sp):
            for g in each:
                cached = caches[g].rearrange("b (k d) c -> k d b c", d=DILATIONS[g])[:, 0, :, :]
                for half in range(2):
                    sp.dma_start(cache[2 * g + half][:], cached[:, half * 4:half * 4 + 4, :])\
                      .then_inc(s_cache[2 * g + half], 16)
                    if g == half == 0:
                        for x in each:
                            sp.dma_start(q_rows[:, x, :], q_sample[x].rearrange("b (x d) -> (b x) d", d=HD))\
                              .then_inc(s_q, 16)
                if g == 0:
                    for x in each:
                        sp.dma_start(new[:, x, :, :], new_rows[x].rearrange("r (j d) -> r j d", j=2))\
                          .then_inc(s_new_rows, 16)
            for k in range(2 * KT):
                if k >= RAW:
                    sp.wait_ge(s_wlo, k - RAW + 1)
                src = (w_z, w_out)[k // KT].rearrange("(k p) n -> p k n", p=P)[:, k % KT, :]
                sp.dma_start(w_raw[k % RAW][:], src).then_inc(s_wraw[k % RAW], 16)
            sp.wait_ge(s_step, 10)
            sp.dma_start(o_sample.rearrange("b (x d) -> (b x) d", d=HD), merged[:]).then_inc(s_out, 16)
            sp.wait_ge(s_out, 16)

        @block.gpsimd
        def _(pool):
            nc.gpsimd.memset(ident[:], 0.0).then_inc(s_ident, 1)
            pool.wait_ge(s_ident, 1)
            nc.gpsimd.affine_select(out=ident[:], in_=ident[:], compare_op=ALU.not_equal, fill=1.0, base=0,
                                    pattern=[[-1, P]], channel_multiplier=1).then_inc(s_ident, 1)

        @block.tensor
        def _(pe):
            def single(kind, g, src, rows):
                n = SINGLES.index((kind, g))
                if n >= 2:
                    pe.wait_ge(s_one_sb, n - 1)
                nc.tensor.transpose(one[n % 2][0:src.shape[1], 0:rows], src, ident[0:rows, 0:rows]).then_inc(s_one, 1)

            def turn_keys(g, quad):
                n, c = 4 * g + quad, 2 * g + quad // 2
                pe.wait_ge(s_cache[c], 16)
                if n >= 2:
                    pe.wait_ge(s_keys_sb, n - 1)
                for x in range(4):
                    t = nc.tensor.transpose(tps[n % 2][:, x, :],
                                            cache[c][:, 2 * (quad % 2) + x // 2, (x % 2) * HD:(x % 2 + 1) * HD],
                                            ident[:])
                t.then_inc(s_keys, 1)

            def scores(g):
                turn_keys(g, 0)
                for quad in range(4):
                    n = 4 * g + quad
                    if quad < 3:
                        turn_keys(g, quad + 1)
                    pe.wait_ge(s_keys_sb, n + 1)
                    if quad == 0:
                        pe.wait_ge(s_one_sb, done("q", g))
                        if g >= 2:
                            pe.wait_ge(s_st_sb, g - 1)
                    for x in range(4):
                        row = (4 * quad + x) * QPK
                        t = nc.tensor.matmul(st_ps[g % 2][:, row:row + QPK], keys_t[n % 2][:, x, :],
                                             qt[g][:, row:row + QPK], start=True, stop=True)
                t.then_inc(s_st, 1)

            def turn_scores(g):
                pe.wait_ge(s_st_sb, g + 1)
                single("score", g, score_t[g][:], P)

            def turn_probs(g):
                pe.wait_ge(s_exp, g + 1)
                single("prob", g, prob[g][:, 0:KEYS], R)

            def values(g):
                pe.wait_ge(s_one_sb, done("prob", g))
                if g >= 2:
                    pe.wait_ge(s_ot_sb, g - 1)
                for pair in range(NS * KVH):
                    seq, n = pair // KVH, pair % KVH
                    t = nc.tensor.matmul(ot_ps[g % 2][:, pair * QPK:(pair + 1) * QPK],
                                         cache[2 * g + seq // 4][:, seq % 4, KVW + n * HD:KVW + (n + 1) * HD],
                                         prob_t[g][:, pair * QPK:(pair + 1) * QPK], start=True, stop=True)
                t.then_inc(s_ot, 1)

            def turn_sums(g):
                pe.wait_ge(s_ot_sb, g + 1)
                single("sum", g, sum_t[g][:], P)

            pe.wait_ge(s_ident, 2)
            pe.wait_ge(s_q, 16 * GROUPS)
            for g in each:
                single("q", g, q_rows[:, g, :], R)
            scores(0)
            turn_scores(0)
            scores(1)
            turn_scores(1)
            turn_probs(0)
            values(0)
            scores(2)
            turn_scores(2)
            turn_probs(1)
            turn_sums(0)
            values(1)
            turn_probs(2)
            values(2)
            turn_sums(1)
            turn_sums(2)

        @block.scalar
        def _(act):
            def copy_single(kind, g, dst):
                act.wait_ge(s_one, done(kind, g))
                act.wait_ge(s_one_sb, done(kind, g) - 1)
                nc.scalar.activation(dst, bank(kind, g)[0:dst.shape[0], 0:dst.shape[1]], ACT.Copy)\
                  .then_inc(s_one_sb, 1)

            def split_weights(ks):
                for k in ks:
                    act.wait_ge(s_wraw[k % RAW], 16 * (k // RAW + 1))
                    nc.scalar.activation(w_hi[:, k // KT, k % KT, :], w_raw[k % RAW][:], ACT.Copy,
                                         scale=gains[:, k:k + 1] if k < KT else 1.0).then_inc(s_whi, 1)

            def keys(g, weights=()):
                for quad in range(4):
                    n = 4 * g + quad
                    act.wait_ge(s_keys, n + 1)
                    nc.scalar.activation(keys_t[n % 2][:], tps[n % 2][:], ACT.Copy).then_inc(s_keys_sb, 1)
                    split_weights(weights[quad:quad + 1])
                act.wait_ge(s_st, g + 1)
                nc.scalar.activation(score_t[g][:], st_ps[g % 2][:, 0:R], ACT.Copy).then_inc(s_st_sb, 1)
                copy_single("score", g, score[g][:, 0:KEYS])

            def exponentials(g):
                act.wait_ge(s_bias, 2 * g + 2)
                nc.scalar.activation(prob[g][:], score[g][:], ACT.Exp, bias=stat[:, 0, g:g + 1], scale=SCALE,
                                     accum_out=stat[:, 1, g:g + 1]).then_inc(s_exp, 1)
                copy_single("prob", g, prob_t[g][:])

            def copy_sums(g):
                act.wait_ge(s_ot, g + 1)
                nc.scalar.activation(sum_t[g][:], ot_ps[g % 2][:, 0:R], ACT.Copy).then_inc(s_ot_sb, 1)

            act.dma_start(gains[:], pre_gain.rearrange("(k p) -> p k", p=P),
                          allow_slow_non_contiguous=True).then_inc(s_gains, 16)
            for g in each:
                copy_single("q", g, qt[g][:])
            keys(0)
            act.wait_ge(s_gains, 16)
            keys(1, range(0, 4))
            exponentials(0)
            split_weights(range(4, 6))
            copy_sums(0)
            keys(2, range(6, 10))
            exponentials(1)
            split_weights(range(10, 13))
            copy_sums(1)
            exponentials(2)
            split_weights(range(13, 16))
            copy_sums(2)
            act.wait_ge(s_step, 3)
            nc.scalar.activation(stat[:, 2, :], stat[:, 3, :], ACT.Exp).then_inc(s_w, 1)

        @block.vector
        def _(dve):
            def new_score(g):
                if g > 0:
                    dve.wait_ge(s_new, g)
                nc.vector.tensor_tensor_reduce(out=product[:], in0=q_rows[:, g, :], in1=new[:, g, 0, :],
                                               scale=1.0, scalar=0.0, op0=ALU.mult, op1=ALU.add,
                                               accum_out=score[g][:, KEYS:KEYS + 1]).then_inc(s_new, 1)

            def maximum(g):
                dve.wait_ge(s_new, g + 1)
                dve.wait_ge(s_one_sb, done("score", g))
                if g > 0:
                    dve.wait_ge(s_bias, 2 * g)
                nc.vector.tensor_reduce(small[:, 0:1], score[g][:], AX_X, ALU.max, negate=True).then_inc(s_bias, 1)
                dve.wait_ge(s_bias, 2 * g + 1)
                nc.vector.tensor_scalar(stat[:, 0, g:g + 1], small[:, 0:1], SCALE, None, ALU.mult).then_inc(s_bias, 1)

            def add_new_value(g):
                dve.wait_ge(s_exp, g + 1)
                dve.wait_ge(s_one, done("sum", g))
                dve.wait_ge(s_one_sb, done("sum", g) - 1)
                nc.vector.scalar_tensor_tensor(out=sums[:, g, :], in0=new[:, g, 1, :],
                                               scalar=prob[g][:, KEYS:KEYS + 1],
                                               in1=bank("sum", g)[0:R, 0:HD],
                                               op0=ALU.mult, op1=ALU.add).then_inc(s_one_sb, 1)

            def split_weights(ks):
                for k in ks:
                    dve.wait_ge(s_whi, k + 1)
                    hi, lo = w_hi[:, k // KT, k % KT, :].bitcast(F32), w_lo[:, k // KT, k % KT, :]
                    if k < KT:
                        nc.vector.scalar_tensor_tensor(out=lo, in0=w_raw[k % RAW][:], scalar=gains[:, k:k + 1],
                                                       in1=hi, op0=ALU.mult, op1=ALU.subtract).then_inc(s_wlo, 1)
                    else:
                        nc.vector.tensor_tensor(lo, w_raw[k % RAW][:], hi, ALU.subtract).then_inc(s_wlo, 1)

            dve.wait_ge(s_q, 16 * GROUPS)
            dve.wait_ge(s_new_rows, 16 * GROUPS)
            for g in each:
                new_score(g)
            maximum(0)
            dve.wait_ge(s_gains, 16)
            split_weights(range(0, 4))
            maximum(1)
            split_weights(range(4, 10))
            maximum(2)
            add_new_value(0)
            split_weights(range(10, 16))
            least, total, inverse = small[:, 1:2], small[:, 2:3], small[:, 3:4]
            dve.wait_ge(s_bias, 2 * GROUPS)
            nc.vector.tensor_reduce(least, stat[:, 0, :], AX_X, ALU.min).then_inc(s_step, 1)
            dve.wait_ge(s_step, 1)
            nc.vector.tensor_scalar(stat[:, 3, :], stat[:, 0, :], least, None, ALU.subtract).then_inc(s_step, 1)
            dve.wait_ge(s_step, 2)
            nc.vector.tensor_scalar(stat[:, 3, :], stat[:, 3, :], -1.0, None, ALU.mult).then_inc(s_step, 1)
            add_new_value(1)
            add_new_value(2)
            dve.wait_ge(s_w, 1)
            nc.vector.tensor_tensor(stat[:, 3, :], stat[:, 2, :], stat[:, 1, :], ALU.mult).then_inc(s_step, 1)
            dve.wait_ge(s_step, 4)
            nc.vector.tensor_reduce(total, stat[:, 3, :], AX_X, ALU.add).then_inc(s_step, 1)
            dve.wait_ge(s_step, 5)
            nc.vector.reciprocal(inverse, total).then_inc(s_step, 1)
            dve.wait_ge(s_step, 6)
            nc.vector.tensor_scalar(stat[:, 3, :], stat[:, 2, :], inverse, None, ALU.mult).then_inc(s_step, 1)
            dve.wait_ge(s_one_sb, len(SINGLES))
            dve.wait_ge(s_step, 7)
            nc.vector.tensor_scalar(merged[:], sums[:, 0, :], stat[:, 3, 0:1], None, ALU.mult).then_inc(s_step, 1)
            for g in (1, 2):
                dve.wait_ge(s_step, 7 + g)
                nc.vector.scalar_tensor_tensor(out=merged[:], in0=sums[:, g, :], scalar=stat[:, 3, g:g + 1],
                                               in1=merged[:], op0=ALU.mult, op1=ALU.add).then_inc(s_step, 1)


def attention_output_phase(nc, hn_rows, h_rows, partials, o_sample, w_hi, w_lo, norm_post, y_prompt, y_sample):
    UN = 2
    BODIES = (NT - 3) // UN
    TAIL = range(UN * BODIES + 1, NT + 1)

    with ExitStack() as ctx:
        def sb(name, shape, dt=F32):
            return ctx.enter_context(nc.sbuf_tensor(f"d_{name}", shape, dt))

        def ps(name, shape):
            return ctx.enter_context(nc.psum_tensor(f"d_{name}", shape, F32))

        def sem(name):
            return nc.alloc_semaphore(f"d_{name}")

        tok = [sb(f"tok{b}", [P, D]) for b in range(2)]
        ht_hi = sb("ht_hi", [P, KT, P], F32R)
        ht_lo = sb("ht_lo", [P, KT, P], F32R)
        gt_hi = sb("gt_hi", [P, KT, P], F32R)
        gt_lo = sb("gt_lo", [P, KT, P], F32R)
        part = [sb(f"part{b}", [P, GROUPS, OMW]) for b in range(2)]
        silu_z = sb("silu_z", [P, D])
        normed = sb("normed", [P, D])
        h_buf = [sb(f"h{b}", [P, D]) for b in range(2)]
        post_gain = sb("post_gain", [P, D])
        coef = sb("coef", [P, 3, GROUPS, HEADS])
        small = sb("small", [P, 3, HEADS])
        eps = sb("eps", [P, 1])
        stat = sb("stat", [P, 3])
        scratch = sb("scratch", [P, 3])
        ident = sb("ident", [P, P])

        z_ps = ps("z", [P, D])
        out_ps = ps("out", [P, D])
        square = ps("square", [P, D])
        tps = [ps(f"tps{b}", [P, BANK]) for b in range(2)]

        s_const = sem("gain_landed")
        s_ident = sem("ident_ready")
        s_eps = sem("eps_ready")
        s_tok = [sem(f"tok_landed{b}") for b in range(2)]
        s_h = [sem(f"h_landed{b}") for b in range(2)]
        s_p = [sem(f"partials_landed{b}") for b in range(2)]
        s_tr = sem("transposed")
        s_tr_hi = sem("transposed_hi")
        s_tr_free = sem("transpose_evacuated")
        s_z = sem("z_ready")
        s_silu = sem("silu_ready")
        s_diff = sem("merge_steps")
        s_exp = sem("weights_ready")
        s_mul = sem("weighted")
        s_mul2 = sem("weighted_last")
        s_gated = sem("gated_ready")
        s_out = sem("product_ready")
        s_square = sem("squares")
        s_root = sem("roots")
        s_rstd = sem("rstd_steps")
        s_normed = sem("normed_ready")
        s_y = sem("y_ready")
        s_ystore = [sem(f"y_stored{b}") for b in range(2)]

        block = ctx.enter_context(nc.Block())

        def tile(i, u, k=0):
            return 2 * i + 1 + u + k, (1 + u + k) % 2, i + (1 + u + k) // 2

        def height(t):
            return NS if isinstance(t, int) and t == NT else P

        def above(value, bound):
            return not isinstance(value, int) or value >= bound

        def token_job(t):
            return 0 if isinstance(t, int) and t == 0 else 4 * t - 2

        def gated_job(t):
            return 4 * t + 2 if isinstance(t, int) and t == NT else 4 * t + 4

        def run_steps(engine, step):
            step(0, -1)
            with engine.Fori(0, BODIES) as i:
                for u in range(UN):
                    step(i, u)
            for t in TAIL:
                step(0, t - 1)

        @block.sync
        def _(sp):
            def load_tokens(t, b):
                n = height(t)
                sp.dma_start(tok[b][0:n, :], hn_rows[bass.ds(t * P, n), :]).then_inc(s_tok[b], 16)

            def load_parts(t, b):
                if height(t) == NS:
                    sp.dma_start(part[b][0:NS, 0, 0:D], o_sample).then_inc(s_p[b], 16)
                    return
                for g in range(GROUPS):
                    sp.dma_start(part[b][:, g, :], partials[g][bass.ds(t * P, P), :]).then_inc(s_p[b], 16)

            def step(i, u):
                t, b, m = tile(i, u)
                if not isinstance(t, int) or t + 3 <= NT:
                    if above(t, 0):
                        sp.wait_ge(s_const, 16)
                        sp.wait_ge(s_tr, token_job(t + 1) + 2)
                    load_tokens(*tile(i, u, 3)[:2])
                n = height(t)
                if above(t, 2):
                    sp.wait_ge(s_const, 16)
                    sp.wait_ge(s_ystore[b], 16 + 16 * m)
                sp.dma_start(h_buf[b][0:n, :], h_rows[bass.ds(t * P, n), :]).then_inc(s_h[b], 16)
                if not isinstance(t, int) or t + 2 <= NT:
                    sp.wait_ge(s_const, 16)
                    sp.wait_ge(s_tr, gated_job(t) + 2)
                    load_parts(t + 2, b)
                if above(t, 1):
                    store(*tile(i, u, -1)[:2])

            def store(t, b):
                n = height(t)
                sp.wait_ge(s_const, 16)
                sp.wait_ge(s_y, t + 1)
                dst = y_sample if n == NS else y_prompt[bass.ds(t * P, P), :]
                sp.dma_start(dst, h_buf[b][0:n, :]).then_inc(s_ystore[b], 16)

            for b in range(2):
                sp.sem_inc(s_ystore[b], 16)
            load_tokens(0, 0)
            load_parts(0, 0)
            sp.dma_start(post_gain[:], norm_post.partition_broadcast(P)).then_inc(s_const, 16)
            load_tokens(1, 1)
            load_parts(1, 1)
            sp.wait_ge(s_tr, 2)
            load_tokens(2, 0)
            run_steps(sp, step)
            store(NT, NT % 2)
            for b in range(2):
                sp.wait_ge(s_ystore[b], 16 + 16 * (NT // 2 + (b == 0)))

        @block.tensor
        def _(pe):
            def turn(number, bank, src, first, n):
                if above(number, 2):
                    pe.wait_ge(s_tr_free, number - 1)
                for x in range(4):
                    last = nc.tensor.transpose(tps[bank][:, x * n:(x + 1) * n],
                                               src[0:n, first + x * P:first + (x + 1) * P], ident[0:n, 0:n])
                last.then_inc(s_tr, 1)

            def turn_tokens(t, b, m):
                pe.wait_ge(s_tok[b], 16 * m + 16)
                for half in range(2):
                    turn(token_job(t) + half, half, tok[b], half * BANK, height(t))

            def turn_gated(t, b):
                pe.wait_ge(s_gated, t + 1)
                for half in range(2):
                    turn(gated_job(t) + half, half, part[b][:, 0, :], half * BANK, height(t))

            def product(dst, which, hi_t, lo_t, ks, n):
                for k in ks:
                    for c in range(D // BANK):
                        cols = slice(c * BANK, (c + 1) * BANK)
                        hi, lo = hi_t[:, k, 0:n], lo_t[:, k, 0:n]
                        nc.tensor.matmul(dst[0:n, cols], hi, w_hi[:, which, k, cols], start=(k == 0), stop=False)
                        nc.tensor.matmul(dst[0:n, cols], hi, w_lo[:, which, k, cols], start=False, stop=False)
                        last = nc.tensor.matmul(dst[0:n, cols], lo, w_hi[:, which, k, cols], start=False,
                                                stop=(k == KT - 1))
                return last

            def z_product(t):
                pe.wait_ge(s_tr_free, token_job(t) + 2)
                if above(t, 1):
                    pe.wait_ge(s_silu, t)
                product(z_ps, 0, ht_hi, ht_lo, range(KT), height(t)).then_inc(s_z, 1)

            def step(i, u):
                t, b, m = tile(i, u)
                turn_gated(t, b)
                if not isinstance(t, int) or t < NT:
                    z_product(t + 1)
                pe.wait_ge(s_tr_free, gated_job(t) + 2)
                if above(t, 1):
                    pe.wait_ge(s_normed, t)
                product(out_ps, 1, gt_hi, gt_lo, range(0, KT // 2), height(t))
                if not isinstance(t, int) or t + 2 <= NT:
                    turn_tokens(*tile(i, u, 2))
                product(out_ps, 1, gt_hi, gt_lo, range(KT // 2, KT), height(t)).then_inc(s_out, 1)

            pe.wait_ge(s_ident, 2)
            turn_tokens(0, 0, 0)
            z_product(0)
            turn_tokens(1, 1, 0)
            run_steps(pe, step)

        def halves(hi_t, lo_t, n):
            return [(hi_t[:, 4 * x:4 * x + 4, 0:n], lo_t[:, 4 * x:4 * x + 4, 0:n]) for x in range(2)]

        def bank_view(x, n):
            return tps[x][:, 0:4 * n].rearrange("p (k n) -> p k n", k=4)

        @block.scalar
        def _(act):
            def high(number, hi_t, lo_t, n):
                for x, (hi, _lo) in enumerate(halves(hi_t, lo_t, n)):
                    act.wait_ge(s_tr, number + x + 1)
                    nc.scalar.activation(hi, bank_view(x, n), ACT.Copy).then_inc(s_tr_hi, 1)

            def root(t):
                n = height(t)
                act.wait_ge(s_out, t + 1)
                if above(t, 1):
                    act.wait_ge(s_rstd, 6 * t)
                nc.scalar.activation(square[0:n, :], out_ps[0:n, :], ACT.Square,
                                     accum_out=stat[0:n, 0:1]).then_inc(s_square, 1)
                act.wait_ge(s_square, t + 1)
                nc.scalar.activation(stat[0:n, 1:2], stat[0:n, 0:1], ACT.Sqrt, scale=1.0 / D,
                                     bias=eps[0:n, :]).then_inc(s_root, 1)

            def weights(t):
                act.wait_ge(s_diff, 6 * t + 2)
                nc.scalar.activation(coef[:, 1, :, :], coef[:, 0, :, :], ACT.Exp).then_inc(s_exp, 1)

            def gate(t):
                n = height(t)
                act.wait_ge(s_z, t + 1)
                if above(t, 1):
                    act.wait_ge(s_gated, t)
                nc.scalar.activation(silu_z[0:n, :], z_ps[0:n, :], ACT.Silu).then_inc(s_silu, 1)

            def step(i, u):
                t, b, m = tile(i, u)
                high(gated_job(t), gt_hi, gt_lo, height(t))
                if above(t, 1):
                    root(t - 1)
                if not isinstance(t, int) or t + 1 < NT:
                    weights(t + 1)
                if not isinstance(t, int) or t < NT:
                    gate(t + 1)
                if not isinstance(t, int) or t + 2 <= NT:
                    high(token_job(t + 2), ht_hi, ht_lo, height(t + 2))

            high(0, ht_hi, ht_lo, P)
            weights(0)
            gate(0)
            high(token_job(1), ht_hi, ht_lo, P)
            act.wait_ge(s_eps, 1)
            run_steps(act, step)
            root(NT)

        def weigh(engine, b, g):
            x = part[b][:, g, 0:D].rearrange("p (h d) -> p h d", d=HD)
            return engine.tensor_tensor(x, x, coef[:, 2, g, :].unsqueeze(2).to_broadcast([P, HEADS, HD]), ALU.mult)

        @block.vector
        def _(dve):
            def low(number, hi_t, lo_t, n):
                for x, (hi, lo) in enumerate(halves(hi_t, lo_t, n)):
                    dve.wait_ge(s_tr_hi, number + x + 1)
                    nc.vector.tensor_tensor(lo, bank_view(x, n), hi.bitcast(F32), ALU.subtract).then_inc(s_tr_free, 1)

            def normalise(t):
                n = height(t)
                dve.wait_ge(s_root, t + 1)
                reciprocal_root(dve, s_rstd, 6 * t, stat[0:n, 0:1], stat[0:n, 1:2], scratch[0:n, :], stat[0:n, 2:3])
                if above(t, 1):
                    dve.wait_ge(s_y, t)
                dve.wait_ge(s_rstd, 6 * t + 6)
                nc.vector.scalar_tensor_tensor(out=normed[0:n, :], in0=out_ps[0:n, :], scalar=stat[0:n, 2:3],
                                               in1=post_gain[0:n, :], op0=ALU.mult, op1=ALU.mult)\
                  .then_inc(s_normed, 1)

            def coefficients(t, b, m):
                bias, denominators = (part[b][:, :, first:first + HEADS] for first in (D, D + HEADS))
                dve.wait_ge(s_p[b], 16 * GROUPS * m + 16 * GROUPS)
                if above(t, 1):
                    dve.wait_ge(s_mul, 2 * t)
                    dve.wait_ge(s_mul2, 3 * t)
                nc.vector.tensor_reduce(small[:, 0, :], bias.rearrange("p g h -> p h g"), AX_X, ALU.min)\
                  .then_inc(s_diff, 1)
                dve.wait_ge(s_diff, 6 * t + 1)
                shape = [P, GROUPS, HEADS]
                nc.vector.tensor_tensor(coef[:, 0, :, :], small[:, 0:1, :].to_broadcast(shape), bias,
                                        ALU.subtract).then_inc(s_diff, 1)
                dve.wait_ge(s_exp, t + 1)
                nc.vector.tensor_tensor(coef[:, 0, :, :], coef[:, 1, :, :], denominators, ALU.mult).then_inc(s_diff, 1)
                dve.wait_ge(s_diff, 6 * t + 3)
                nc.vector.tensor_reduce(small[:, 1, :], coef[:, 0, :, :].rearrange("p g h -> p h g"), AX_X,
                                        ALU.add).then_inc(s_diff, 1)
                dve.wait_ge(s_diff, 6 * t + 4)
                nc.vector.reciprocal(small[:, 2, :], small[:, 1, :]).then_inc(s_diff, 1)
                dve.wait_ge(s_diff, 6 * t + 5)
                nc.vector.tensor_tensor(coef[:, 2, :, :], coef[:, 1, :, :], small[:, 2:3, :].to_broadcast(shape),
                                        ALU.mult).then_inc(s_diff, 1)

            def merge(t, b, m):
                n = height(t)
                groups = [part[b][0:n, g, 0:D] for g in range(GROUPS)]
                if n == P:
                    coefficients(t, b, m)
                    dve.wait_ge(s_diff, 6 * t + 6)
                    weigh(nc.vector, b, 2).then_inc(s_mul2, 1)
                    dve.wait_ge(s_mul, 2 * t + 2)
                    nc.vector.tensor_tensor(groups[0], groups[0], groups[1], ALU.add).then_inc(s_mul2, 1)
                    dve.wait_ge(s_mul2, 3 * t + 2)
                    nc.vector.tensor_tensor(groups[0], groups[0], groups[2], ALU.add).then_inc(s_mul2, 1)
                    dve.wait_ge(s_mul2, 3 * t + 3)
                else:
                    dve.wait_ge(s_p[b], 16 * GROUPS * m + 16)
                dve.wait_ge(s_silu, t + 1)
                nc.vector.tensor_tensor(groups[0], groups[0], silu_z[0:n, :], ALU.mult).then_inc(s_gated, 1)

            def step(i, u):
                t, b, m = tile(i, u)
                low(gated_job(t), gt_hi, gt_lo, height(t))
                if above(t, 1):
                    normalise(t - 1)
                if not isinstance(t, int) or t < NT:
                    merge(*tile(i, u, 1))
                if not isinstance(t, int) or t + 2 <= NT:
                    low(token_job(t + 2), ht_hi, ht_lo, height(t + 2))

            nc.vector.memset(eps[:], EPS).then_inc(s_eps, 1)
            low(0, ht_hi, ht_lo, P)
            merge(0, 0, 0)
            low(token_job(1), ht_hi, ht_lo, P)
            dve.wait_ge(s_const, 16)
            run_steps(dve, step)
            normalise(NT)

        @block.gpsimd
        def _(pool):
            def add(t, b, m):
                n = height(t)
                pool.wait_ge(s_h[b], 16 * m + 16)
                pool.wait_ge(s_normed, t + 1)
                nc.gpsimd.tensor_tensor(h_buf[b][0:n, :], h_buf[b][0:n, :], normed[0:n, :], ALU.add).then_inc(s_y, 1)

            def weigh_two(t, b):
                pool.wait_ge(s_diff, 6 * t + 6)
                for g in range(2):
                    weigh(nc.gpsimd, b, g).then_inc(s_mul, 1)

            def step(i, u):
                t, b, m = tile(i, u)
                if above(t, 1):
                    add(*tile(i, u, -1))
                if not isinstance(t, int) or t + 1 < NT:
                    weigh_two(*tile(i, u, 1)[:2])

            nc.gpsimd.memset(ident[:], 0.0).then_inc(s_ident, 1)
            pool.wait_ge(s_ident, 1)
            nc.gpsimd.affine_select(out=ident[:], in_=ident[:], compare_op=ALU.not_equal, fill=1.0, base=0,
                                    pattern=[[-1, P]], channel_multiplier=1).then_inc(s_ident, 1)
            weigh_two(0, 0)
            run_steps(pool, step)
            add(NT, 0, NT // 2)


def decoder_program(nc, ins, outs, scratch):
    with nc.cleanup_on_exit():
        conv_projection_phase(nc, ins["x_prompt"], ins["x_sample"], ins["state_conv"], ins["a_norm_pre"],
                              ins["a_w_in"], ins["a_conv"], scratch["y_t"], outs["state_conv_prompt"],
                              outs["state_conv_sample"], [ins[f"cache_kv_g{g}"] for g in range(GROUPS)],
                              [outs[f"cache_kv_g{g}_sample"] for g in range(GROUPS)])
    with nc.cleanup_on_exit():
        conv_output_phase(nc, ins["x_prompt"], ins["x_sample"], scratch["y_t"], ins["a_w_out"], ins["a_norm_post"],
                          scratch["h_rows"], scratch["hn_rows"])
    with nc.cleanup_on_exit():
        attention_phase(nc, scratch["hn_rows"], ins["w_kv"], ins["b_w_in"], ins["kv_norm"], ins["b_norm_pre"],
                        ins["rope_rows"], [scratch[f"partial{g}"] for g in range(GROUPS)],
                        [outs[f"cache_kv_g{g}_prompt"] for g in range(GROUPS)],
                        [scratch[f"q_sample{g}"] for g in range(GROUPS)],
                        [scratch[f"new_rows{g}"] for g in range(GROUPS)],
                        [outs[f"cache_kv_g{g}_sample"][:, WINDOWS[g] - 1, :] for g in range(GROUPS)])
    with (nc.sbuf_tensor("w_output_hi", [P, 2, KT, D], F32R) as w_hi,
          nc.sbuf_tensor("w_output_lo", [P, 2, KT, D], F32R) as w_lo):
        with nc.cleanup_on_exit():
            sample_attention_phase(nc, [scratch[f"q_sample{g}"] for g in range(GROUPS)],
                                   [scratch[f"new_rows{g}"] for g in range(GROUPS)],
                                   [ins[f"cache_kv_g{g}"] for g in range(GROUPS)], scratch["o_sample"],
                                   ins["b_w_in"][:, GROUPS * D:(GROUPS + 1) * D], ins["b_w_out"],
                                   ins["b_norm_pre"], w_hi, w_lo)
        with nc.cleanup_on_exit():
            attention_output_phase(nc, scratch["hn_rows"], scratch["h_rows"],
                                   [scratch[f"partial{g}"] for g in range(GROUPS)], scratch["o_sample"],
                                   w_hi, w_lo, ins["b_norm_post"], outs["y_prompt"], outs["y_sample"])


def rope_table():
    exponent = -np.arange(HD // 2, dtype=np.float32) * np.float32(2.0) / np.float32(HD)
    frequency = (ROPE_THETA ** exponent.astype(np.float64)).astype(np.float32)
    angle = np.arange(SEQ + 1, dtype=np.float32)[:, None] * frequency[None, :]
    angle = angle.astype(np.float64)
    return np.concatenate([np.cos(angle), -np.sin(angle), np.sin(angle)], axis=1).astype(np.float32)


INPUT_SHAPES = {
    "x_prompt": (SEQ, D), "x_sample": (NS, D), "state_conv": (2 * NS, D),
    **{f"cache_kv_g{g}": (NS, WINDOWS[g], 2 * KVW) for g in range(GROUPS)},
    "a_norm_pre": (D,), "a_w_in": (D, 4 * D), "a_conv": (3, D), "a_w_out": (D, D), "a_norm_post": (D,),
    "kv_norm": (D,), "w_kv": (D, 2 * GROUPS * KVW), "b_norm_pre": (D,), "b_w_in": (D, (GROUPS + 1) * D),
    "b_w_out": (D, D), "b_norm_post": (D,),
}
OUTPUT_SHAPES = {
    "y_prompt": ((SEQ, D), (1, SEQ, D)),
    "y_sample": ((NS, D), (NS, 1, D)),
    "state_conv_prompt": ((2, D), (1, 1, 2, D)),
    **{f"cache_kv_g{g}_prompt": ((WINDOWS[g], 2 * KVW), (1, WINDOWS[g], 2, KVH, HD)) for g in range(GROUPS)},
    "state_conv_sample": ((NS, 2, D), (1, NS, 2, D)),
    **{f"cache_kv_g{g}_sample": ((NS, WINDOWS[g], 2 * KVW), (NS, WINDOWS[g], 2, KVH, HD)) for g in range(GROUPS)},
}
SCRATCH_SHAPES = {
    "y_t": (D, TOK), "h_rows": (TOK, D), "hn_rows": (TOK, D), "o_sample": (NS, D),
    **{f"partial{g}": (SEQ, OMW) for g in range(GROUPS)},
    **{f"q_sample{g}": (NS, D) for g in range(GROUPS)},
    **{f"new_rows{g}": (NS * HEADS, 2 * HD) for g in range(GROUPS)},
}


def kernel(**inputs):
    import concourse.bacc as bacc
    from concourse.bass_utils import run_bass_kernel_spmd

    nc = bacc.Bacc("TRN2", target_bir_lowering=False, num_devices=1)
    arrays = {name: np.ascontiguousarray(inputs[name]).reshape(shape) for name, shape in INPUT_SHAPES.items()}
    arrays["rope_rows"] = rope_table()
    ins = {name: nc.dram_tensor(name, list(a.shape), F32, kind="ExternalInput").ap() for name, a in arrays.items()}
    outs = {name: nc.dram_tensor(f"out_{name}", list(shape), F32, kind="ExternalOutput").ap()
            for name, (shape, _) in OUTPUT_SHAPES.items()}
    scratch = {name: nc.dram_tensor(f"scratch_{name}", list(shape), F32, kind="Internal").ap()
               for name, shape in SCRATCH_SHAPES.items()}
    decoder_program(nc, ins, outs, scratch)
    results = run_bass_kernel_spmd(nc, [arrays], core_ids=[0]).results[0]
    return tuple(np.asarray(results[f"out_{name}"]).reshape(shape) for name, (_, shape) in OUTPUT_SHAPES.items())
```
